# Optimizing a Trainium2 kernel written in Bass

```python
import math
import jax
import jax.numpy as jnp
from jax import lax
import numpy as np

D_MODEL = 1024
BATCH = 1
SEQ = 1024
DEPTH = 1

MEM_LEN = 256
RMS_EPS = 1e-5

SSM_HEADS = 8
SSM_HEAD_DIM = 64
SSM_WIDTH = SSM_HEADS * SSM_HEAD_DIM
SSM_STATE = 128
SSM_GROUPS = 2
CONV_WIDTH = 4
CHUNK = 128
CONV_CH = SSM_WIDTH + 2 * SSM_GROUPS * SSM_STATE

ATTN_HEADS = 8
KV_HEADS = 2
Q_PER_KV = ATTN_HEADS // KV_HEADS
HEAD_DIM = 64
ATTN_WIDTH = ATTN_HEADS * HEAD_DIM
KV_WIDTH = KV_HEADS * HEAD_DIM
WINDOW = 128
BLOCK = WINDOW
QKV_COLS = ATTN_WIDTH + 2 * KV_WIDTH

MIX_WIDTH = SSM_WIDTH + ATTN_WIDTH
IN_COLS = SSM_WIDTH + CONV_CH + SSM_HEADS + QKV_COLS

REL_BUCKETS = 32
REL_MAX_DIST = 128

CROSS_HEADS = 4
CROSS_HEAD_DIM = 128
CROSS_WIDTH = CROSS_HEADS * CROSS_HEAD_DIM

N_EXPERTS = 32
TOP_K = 4
D_FF = D_MODEL
SWIGLU_ALPHA = 1.702
SWIGLU_LIMIT = 7.0
MOE_BLOCK = 128

kernel_name = "hybrid_ssd_swa_sink_t5_memxattn_moe"

def rmsnorm(x, g):
    xf = x.astype(jnp.float32)
    y = xf * lax.rsqrt(jnp.mean(xf * xf, axis=-1, keepdims=True) + RMS_EPS)
    return (y * g.astype(jnp.float32)).astype(x.dtype)

def causal_depthwise_conv(u, w, b):
    c = u.shape[-1]
    out = lax.conv_general_dilated(
        u, w[:, None, :].astype(u.dtype), window_strides=(1,),
        padding=[(CONV_WIDTH - 1, 0)], dimension_numbers=("NWC", "WIO", "NWC"),
        feature_group_count=c)
    return out + b.astype(u.dtype)

def segsum(a):
    t = a.shape[-1]
    cs = jnp.cumsum(a, axis=-1)
    diff = cs[..., :, None] - cs[..., None, :]
    mask = jnp.tril(jnp.ones((t, t), dtype=bool))
    return jnp.where(mask, diff, -jnp.inf)

def ssd_chunked(xh, dt, a_head, bm, cm):
    b, l, nh, p = xh.shape
    g, n = bm.shape[-2], bm.shape[-1]
    r = nh // g
    c = l // CHUNK
    xdt = (xh * dt[..., None]).reshape(b, c, CHUNK, g, r, p)
    a = (dt * a_head).reshape(b, c, CHUNK, g, r).transpose(0, 3, 4, 1, 2)
    bc = bm.reshape(b, c, CHUNK, g, n)
    cc = cm.reshape(b, c, CHUNK, g, n)
    a_cs = jnp.cumsum(a, axis=-1)
    decay = jnp.exp(segsum(a))
    cb = jnp.einsum("bclgn,bcsgn->bgcls", cc, bc)
    y_diag = jnp.einsum("bgrcls,bcsgrp->bclgrp", cb[:, :, None] * decay, xdt)
    to_end = jnp.exp(a_cs[..., -1:] - a_cs)
    states = jnp.einsum("bcsgn,bgrcs,bcsgrp->cbgrpn", bc, to_end, xdt)
    chunk_decay = jnp.exp(a_cs[..., -1]).transpose(3, 0, 1, 2)

    def step(h_state, inp):
        st, dec = inp
        return h_state * dec[..., None, None] + st, h_state

    h0 = jnp.zeros((b, g, r, p, n), jnp.float32)
    _, h_in = lax.scan(step, h0, (states, chunk_decay))
    y_off = jnp.einsum("bclgn,cbgrpn,bgrcl->bclgrp", cc, h_in, jnp.exp(a_cs))
    return (y_diag + y_off).reshape(b, l, nh, p)

def ssd_mixer(z, xbc, dt_raw, conv_w, conv_b, dt_bias, a_log, d_skip, g_ssm_out):
    b, l, _ = xbc.shape
    xbc = jax.nn.silu(causal_depthwise_conv(xbc, conv_w, conv_b))
    xs, bm, cm = jnp.split(xbc, [SSM_WIDTH, SSM_WIDTH + SSM_GROUPS * SSM_STATE], axis=-1)
    f32 = jnp.float32
    dt = jax.nn.softplus(dt_raw.astype(f32) + dt_bias.astype(f32))
    a_head = -jnp.exp(a_log.astype(f32))
    xh = xs.astype(f32).reshape(b, l, SSM_HEADS, SSM_HEAD_DIM)
    y = ssd_chunked(xh, dt, a_head,
                    bm.astype(f32).reshape(b, l, SSM_GROUPS, SSM_STATE),
                    cm.astype(f32).reshape(b, l, SSM_GROUPS, SSM_STATE))
    y = y + d_skip.astype(f32)[:, None] * xh
    y = y.reshape(b, l, SSM_WIDTH) * jax.nn.silu(z.astype(f32))
    yg = y.reshape(b, l, SSM_GROUPS, SSM_WIDTH // SSM_GROUPS)
    yg = yg * lax.rsqrt(jnp.mean(yg * yg, axis=-1, keepdims=True) + RMS_EPS)
    return (yg.reshape(b, l, SSM_WIDTH) * g_ssm_out.astype(f32)).astype(z.dtype)

def t5_bucket(dist):
    d = jnp.maximum(dist, 0)
    max_exact = REL_BUCKETS // 2
    ratio = jnp.maximum(d, max_exact).astype(jnp.float32) / max_exact
    large = max_exact + (jnp.log(ratio) / math.log(REL_MAX_DIST / max_exact)
                         * (REL_BUCKETS - max_exact)).astype(jnp.int32)
    large = jnp.minimum(large, REL_BUCKETS - 1)
    return jnp.where(d < max_exact, d, large)

def swa_mixer(qkv, sinks, rel_bias):
    b, l, _ = qkv.shape
    nb = l // BLOCK
    q, k, v = jnp.split(qkv, [ATTN_WIDTH, ATTN_WIDTH + KV_WIDTH], axis=-1)
    q = q.reshape(b, nb, BLOCK, KV_HEADS, Q_PER_KV, HEAD_DIM)
    k = k.reshape(b, nb, BLOCK, KV_HEADS, HEAD_DIM)
    v = v.reshape(b, nb, BLOCK, KV_HEADS, HEAD_DIM)

    def with_prev(t):
        prev = jnp.pad(t, ((0, 0), (1, 0), (0, 0), (0, 0), (0, 0)))[:, :-1]
        return jnp.concatenate([prev, t], axis=2)

    k2, v2 = with_prev(k), with_prev(v)
    s = jnp.einsum("bnqkgd,bnskd->bnkgqs", q, k2).astype(jnp.float32) * (HEAD_DIM ** -0.5)
    q_pos = jnp.arange(BLOCK)[:, None]
    k_pos = jnp.arange(2 * BLOCK)[None, :] - BLOCK
    dist = q_pos - k_pos
    bias = rel_bias.astype(jnp.float32)[t5_bucket(dist)]
    bias = bias.reshape(BLOCK, 2 * BLOCK, KV_HEADS, Q_PER_KV).transpose(2, 3, 0, 1)
    in_window = (dist >= 0) & (dist < WINDOW)
    k_abs = jnp.arange(nb)[:, None] * BLOCK + k_pos
    mask = in_window[None] & (k_abs >= 0)[:, None, :]
    s = jnp.where(mask[None, :, None, None], s + bias, -jnp.inf)
    sink = jnp.broadcast_to(
        sinks.astype(jnp.float32).reshape(KV_HEADS, Q_PER_KV)[None, None, :, :, None, None],
        s.shape[:-1] + (1,))
    p = jax.nn.softmax(jnp.concatenate([s, sink], axis=-1), axis=-1)[..., :-1]
    o = jnp.einsum("bnkgqs,bnskd->bnqkgd", p.astype(v.dtype), v2)
    return o.reshape(b, l, ATTN_WIDTH)

def hybrid_mixer(u, w_in, b_qkv, conv_w, conv_b, dt_bias, a_log, d_skip, g_ssm_out,
                 attn_sinks, rel_bias, w_out, b_out):
    proj = u @ w_in
    z, xbc, dt_raw, qkv = jnp.split(
        proj, [SSM_WIDTH, SSM_WIDTH + CONV_CH, SSM_WIDTH + CONV_CH + SSM_HEADS], axis=-1)
    y_ssm = ssd_mixer(z, xbc, dt_raw, conv_w, conv_b, dt_bias, a_log, d_skip, g_ssm_out)
    y_attn = swa_mixer(qkv + b_qkv.astype(qkv.dtype), attn_sinks, rel_bias).astype(y_ssm.dtype)
    return jnp.concatenate([y_ssm, y_attn], axis=-1) @ w_out + b_out

def cross_attention(u, m, w_q, w_kv, w_o):
    b, l, _ = u.shape
    n_mem = m.shape[1]
    q = (u @ w_q).reshape(b, l, CROSS_HEADS, CROSS_HEAD_DIM)
    k, v = jnp.split(m @ w_kv, 2, axis=-1)
    k = k.reshape(b, n_mem, CROSS_HEADS, CROSS_HEAD_DIM)
    v = v.reshape(b, n_mem, CROSS_HEADS, CROSS_HEAD_DIM)
    s = jnp.einsum("blhd,bmhd->bhlm", q, k).astype(jnp.float32) * (CROSS_HEAD_DIM ** -0.5)
    p = jax.nn.softmax(s, axis=-1).astype(v.dtype)
    o = jnp.einsum("bhlm,bmhd->blhd", p, v).reshape(b, l, CROSS_WIDTH)
    return o @ w_o

def clamped_swiglu(h):
    x_glu, x_lin = h[..., ::2], h[..., 1::2]
    x_glu = jnp.minimum(x_glu, SWIGLU_LIMIT)
    x_lin = jnp.clip(x_lin, -SWIGLU_LIMIT, SWIGLU_LIMIT)
    return x_glu * jax.nn.sigmoid(SWIGLU_ALPHA * x_glu) * (x_lin + 1.0)

def moe(u, w_router, b_router, w1, b1, w2, b2):
    b, l, d = u.shape
    n_tok = b * l
    n_assign = n_tok * TOP_K
    xt = u.reshape(n_tok, d)
    logits = xt @ w_router + b_router
    top_vals, top_idx = lax.top_k(logits, TOP_K)
    gates = jax.nn.softmax(top_vals.astype(jnp.float32), axis=-1).astype(xt.dtype)
    e_flat = top_idx.reshape(-1).astype(jnp.int32)
    tok_flat = jnp.arange(n_assign, dtype=jnp.int32) // TOP_K
    g_flat = gates.reshape(-1)
    counts = jnp.bincount(e_flat, length=N_EXPERTS).astype(jnp.int32)
    padded = (counts + MOE_BLOCK - 1) // MOE_BLOCK * MOE_BLOCK
    padded_end = jnp.cumsum(padded)
    padded_start = padded_end - padded
    count_start = jnp.cumsum(counts) - counts
    order = jnp.argsort(e_flat, stable=True)
    se = e_flat[order]
    rank = jnp.arange(n_assign, dtype=jnp.int32) - count_start[se]
    dest = padded_start[se] + rank
    n_blocks = (n_assign + MOE_BLOCK - 1) // MOE_BLOCK + N_EXPERTS
    n_rows = n_blocks * MOE_BLOCK
    row_tok = jnp.zeros((n_rows,), jnp.int32).at[dest].set(tok_flat[order])
    row_gate = jnp.zeros((n_rows,), xt.dtype).at[dest].set(g_flat[order])
    block_start = jnp.arange(n_blocks, dtype=jnp.int32) * MOE_BLOCK
    block_exp = jnp.minimum(jnp.searchsorted(padded_end, block_start, side="right"),
                            N_EXPERTS - 1).astype(jnp.int32)

    def expert_block(args):
        toks, e = args
        hdn = xt[toks] @ w1[e] + b1[e]
        return clamped_swiglu(hdn) @ w2[e] + b2[e]

    y_rows = lax.map(expert_block, (row_tok.reshape(n_blocks, MOE_BLOCK), block_exp))
    y_rows = y_rows.reshape(n_rows, d) * row_gate[:, None]
    out = jnp.zeros((n_tok, d), xt.dtype).at[row_tok].add(y_rows)
    return out.reshape(b, l, d)

def setup_inputs(seed: int = 0) -> dict:
    key = jax.random.key(seed)
    ks = iter(jax.random.split(key, 40))
    L = DEPTH
    f32 = jnp.float32

    def nrm(shape, scale):
        return jax.random.normal(next(ks), shape, f32) * scale

    def gain(shape):
        return 1.0 + nrm(shape, 0.05)

    dt0 = jnp.exp(jax.random.uniform(next(ks), (L, SSM_HEADS), f32)
                  * (math.log(0.1) - math.log(0.001)) + math.log(0.001))
    dt_bias = dt0 + jnp.log(-jnp.expm1(-dt0))
    a_log = jnp.log(jax.random.uniform(next(ks), (L, SSM_HEADS), f32, minval=1.0, maxval=16.0))
    return {
        "x": nrm((BATCH, SEQ, D_MODEL), 1.0),
        "mem": nrm((BATCH, MEM_LEN, D_MODEL), 1.0),
        "g_mix": gain((L, D_MODEL)),
        "w_in": nrm((L, D_MODEL, IN_COLS), D_MODEL ** -0.5),
        "b_qkv": nrm((L, QKV_COLS), 0.02),
        "conv_w": nrm((L, CONV_WIDTH, CONV_CH), CONV_WIDTH ** -0.5),
        "conv_b": nrm((L, CONV_CH), 0.02),
        "dt_bias": dt_bias,
        "a_log": a_log,
        "d_skip": gain((L, SSM_HEADS)),
        "g_ssm_out": gain((L, SSM_WIDTH)),
        "attn_sinks": nrm((L, ATTN_HEADS), 0.5),
        "rel_bias": nrm((REL_BUCKETS, ATTN_HEADS), 0.5),
        "w_out": nrm((L, MIX_WIDTH, D_MODEL), MIX_WIDTH ** -0.5),
        "b_out": nrm((L, D_MODEL), 0.02),
        "g_cross": gain((L, D_MODEL)),
        "g_mem": gain((L, D_MODEL)),
        "w_q_cross": nrm((L, D_MODEL, CROSS_WIDTH), D_MODEL ** -0.5),
        "w_kv_cross": nrm((L, D_MODEL, 2 * CROSS_WIDTH), D_MODEL ** -0.5),
        "w_o_cross": nrm((L, CROSS_WIDTH, D_MODEL), CROSS_WIDTH ** -0.5),
        "g_ffn": gain((L, D_MODEL)),
        "w_router": nrm((L, D_MODEL, N_EXPERTS), D_MODEL ** -0.5),
        "b_router": nrm((L, N_EXPERTS), 0.01),
        "w1": nrm((L, N_EXPERTS, D_MODEL, 2 * D_FF), D_MODEL ** -0.5),
        "b1": nrm((L, N_EXPERTS, 2 * D_FF), 0.01),
        "w2": nrm((L, N_EXPERTS, D_FF, D_MODEL), D_FF ** -0.5),
        "b2": nrm((L, N_EXPERTS, D_MODEL), 0.01),
        "g_final": gain((D_MODEL,)),
    }

def reference(x, mem, g_mix, w_in, b_qkv, conv_w, conv_b, dt_bias, a_log, d_skip, g_ssm_out,
              attn_sinks, rel_bias, w_out, b_out, g_cross, g_mem, w_q_cross, w_kv_cross,
              w_o_cross, g_ffn, w_router, b_router, w1, b1, w2, b2, g_final):
    h = x
    for i in range(DEPTH):
        h = h + hybrid_mixer(rmsnorm(h, g_mix[i]), w_in[i], b_qkv[i], conv_w[i], conv_b[i],
                             dt_bias[i], a_log[i], d_skip[i], g_ssm_out[i], attn_sinks[i],
                             rel_bias, w_out[i], b_out[i]).astype(h.dtype)
        h = h + cross_attention(rmsnorm(h, g_cross[i]), rmsnorm(mem, g_mem[i]),
                                w_q_cross[i], w_kv_cross[i], w_o_cross[i]).astype(h.dtype)
        h = h + moe(rmsnorm(h, g_ffn[i]), w_router[i], b_router[i], w1[i], b1[i],
                    w2[i], b2[i]).astype(h.dtype)
    return rmsnorm(h, g_final)


_drawn_inputs = setup_inputs


def setup_inputs(seed=0):
    import zlib

    import numpy as np

    out = dict(_drawn_inputs(seed))
    spreads = {}
    factors = {'attn_sinks': 7.283, 'g_cross': 3.336, 'b1': 8.0, 'b2': 8.0}
    for name, (base, spread) in spreads.items():
        noise = np.random.default_rng([zlib.crc32(name.encode()), seed]).standard_normal(out[name].shape)
        drawn = base * np.exp(spread * noise) if base else spread * noise
        out[name] = jnp.asarray(drawn.astype(out[name].dtype))
    for name, factor in factors.items():
        out[name] = (out[name] * factor).astype(out[name].dtype)
    return out
```

```python
from contextlib import ExitStack
import math

import numpy as np
import concourse.bass as bass
from concourse import mybir

F32 = mybir.dt.float32
BF16 = mybir.dt.bfloat16
I32 = mybir.dt.int32
U32 = mybir.dt.uint32
ALU = mybir.AluOpType
ACT = mybir.ActivationFunctionType
AX_X = mybir.AxisListType.X

P = 128
D = 1024
SEQ = 1024
NT = SEQ // P
KD = D // P
MEM = 256
EPS = 1e-5
NEG = -1e30

SH, SP_, SW = 8, 64, 512
CH = 1024
CW = 4
NC_ = CH // P
HD = 64
COL_XBC, COL_DT, COL_Q, COL_K, COL_V = 512, 1536, 1544, 2056, 2184
IN_COLS = 2312
BUCKETS, MAX_DIST = 32, 128

XH, XD = 4, 128
NE, TOPK = 32, 4
FF2 = 2048
ALPHA, LIMIT = 1.702, 7.0
PASS = 256
REGION = 1024
MAX_PASSES = NE + SEQ * TOPK // PASS
FCH = 4
FW = FF2 // FCH
GK = FW // 2 // P


class Signals:

    def __init__(self, nc, ctx, stage):
        self.nc, self.stage, self.made = nc, stage, {}
        ctx.callback(self.give_back)

    def give_back(self):
        self.nc.clear_and_free_semaphores(list(self.made.values()))
        self.nc.all_engine_barrier()

    def __getitem__(self, name):
        if name not in self.made:
            self.made[name] = self.nc.alloc_semaphore(f"{self.stage}_{name}")
        return self.made[name]


def over_heads(ap, n, width):
    return ap.unsqueeze(2).to_broadcast([P, n, width])


def repeated(ap, n, width):
    return ap.unsqueeze(1).to_broadcast([P, n, width])


def row_bcast(ap, n):
    return ap.partition_broadcast(P)


def rstd_of(pool, consts, out, mean_square, n, step, done, at):
    pool.tensor_tensor(out, mean_square, consts[:, 0, 0:n], ALU.add).then_inc(step, 1)
    pool.wait_ge(step, at)
    pool.tensor_tensor(out, out, consts[:, 1, 0:n], ALU.pow).then_inc(done, 1)


def mixer_stage(nc, a, h, scratch):
    with ExitStack() as ctx:
        sb = lambda n, s, d=F32: ctx.enter_context(nc.sbuf_tensor(n, s, d))
        s = Signals(nc, ctx, "mx")

        w_in = sb("w_in_sb", [P, KD, IN_COLS])
        w_out = sb("w_out_sb", [P, KD, D])
        ident = sb("ident", [P, P])
        upper = sb("upper", [P, P])
        ones = sb("ones", [P, P])
        ident_b = sb("ident_b", [P, P], BF16)
        negmask_b = sb("negmask_b", [P, 4, P], BF16)
        bucket_hot = sb("bucket_hot", [BUCKETS, P])
        rel_bias = sb("rel_bias_sb", [BUCKETS, 8])
        bias_rows = sb("bias_rows", [8, 3 * P])
        bias = sb("win_bias", [P, 8, 2 * P])
        g_mix = sb("g_mix_sb", [P, KD])
        conv_w = sb("conv_w_sb", [P, CW, NC_])
        conv_b = sb("conv_b_sb", [P, NC_])
        g_ssm = sb("g_ssm_sb", [P, 4])
        b_qkv = sb("b_qkv_sb", [P, 768])
        b_out = sb("b_out_sb", [P, D])
        small = sb("head_rows", [P, 4, 8])
        dt_bias, a_head, d_skip, sinks = (small[:, i, :] for i in range(4))

        row = sb("row", [P, D])
        uT = sb("uT", [P, KD, P])
        zg = sb("zg", [P, SW])
        ext = sb("conv_in", [P, NC_, P + CW - 1])
        cv = sb("conv_out", [P, NC_, P])
        xs = sb("xs_tok", [P, SW])
        bt = sb("b_tok", [P, 2 * P])
        xdt = sb("xdt", [P, SW])
        xw = sb("x_to_end", [P, SW])
        decay = sb("decay", [P, SH, P])
        state = sb("state", [P, SW])
        y = sb("y", [P, SW])
        y2 = sb("y2", [P, SW])
        d8 = sb("dt_steps", [P, 14, 8])
        (draw, nabs, ex, w1p, rest, rw, lnw, dt, av, acs, nacs, ea, te, cd) = (d8[:, i, :] for i in range(14))
        stat = sb("stat", [P, 8])
        norm_c = sb("norm_c", [P, 2, 2])
        spare = sb("spare", [P, 2])
        q_tok = sb("q_tok", [P, 4, 2, HD])
        k_tok = sb("k_tok", [P, P])
        qT = sb("qT", [P, 4, P])
        kT = sb("kT", [P, 2, P])
        v = sb("v_tok", [P, 2, P])
        sc = sb("scores", [P, 4, 2 * P])
        pT = sb("probs_t", [P, 2, 4, P])
        sm = sb("softmax", [P, 6, 8])
        prevmask = sb("prevmask", [P, 1])
        catT = pT[:, :, :, :].rearrange("p a c n -> p (a c) n")

        ps = [ctx.enter_context(nc.psum_tensor(f"mx_b{i}", [P, 512], F32)) for i in range(8)]
        block = ctx.enter_context(nc.Block())

        w_in_d = a["w_in"].rearrange("a (k p) n -> p (a k) n", p=P)
        w_out_d = a["w_out"][0]

        @block.sync
        def _(sp):
            sp.dma_start(h[:, 0, :], a["x"][0, 0:P, :]).then_inc(s["x0"], 16)
            sp.dma_start(ident[:, :], a["c_ident"]).then_inc(s["consts"], 16)
            sp.dma_start(upper[:, :], a["c_upper"]).then_inc(s["consts"], 16)
            sp.dma_start(bucket_hot[:, :], a["c_bucket"]).then_inc(s["consts"], 16)
            sp.dma_start(rel_bias[:, :], a["rel_bias"]).then_inc(s["consts"], 16)
            sp.dma_start(w_in[:, :, COL_XBC:IN_COLS], w_in_d[:, :, COL_XBC:IN_COLS]).then_inc(s["w_in"], 16)
            sp.dma_start(w_in[:, :, 0:COL_XBC], w_in_d[:, :, 0:COL_XBC]).then_inc(s["w_in"], 16)
            sp.dma_start(h[:, 1:NT, :], a["x"][0, P:SEQ, :].rearrange("(t p) d -> p t d", p=P)).then_inc(s["x"], 16)
            sp.dma_start(w_out[:, 0:4, :], w_out_d[0:SW, :].rearrange("(k p) n -> p k n", p=P)).then_inc(s["w_out"], 16)
            for g in range(2):
                rows = w_out_d[SW + 256 * g:SW + 256 * (g + 1), :]
                sp.dma_start(w_out[64 * g:64 * g + 64, 4:8, :],
                             rows.rearrange("(j d) n -> d j n", d=HD)).then_inc(s["w_out"], 16)

        @block.gpsimd
        def _(pool):
            pool.memset(kT[:, :, :], 0.0).then_inc(s["cleared"], 1)
            pool.memset(v[:, :, :], 0.0).then_inc(s["cleared"], 1)
            pool.memset(ext[:, :, :], 0.0).then_inc(s["cleared"], 1)
            pool.memset(state[:, :], 0.0).then_inc(s["cleared"], 1)
            pool.memset(ones[:, :], 1.0).then_inc(s["cleared"], 1)
            pool.memset(prevmask[:, :], NEG).then_inc(s["cleared"], 1)
            pool.memset(bias_rows[:, :], NEG).then_inc(s["cleared"], 1)
            pool.memset(norm_c[:, 0, :], EPS).then_inc(s["cleared"], 1)
            pool.memset(norm_c[:, 1, :], -0.5).then_inc(s["cleared"], 1)
            pool.wait_ge(s["cleared"], 9)
            def met():
                pool.tensor_tensor(spare[:, 1:2], norm_c[:, 0, 0:1], norm_c[:, 0, 0:1], ALU.add)

            with pool.Fori(0, NT) as t:
                pool.wait_ge(s["ss"], t + 1)
                rstd_of(pool, norm_c, stat[:, 1:2], stat[:, 0:1], 1, s["rstd_ms"], s["rstd"], t + 1)
                pool.wait_ge(s["xn"], t + 1)
                pool.wait_ge(s["x"], 16)
                pool.wait_ge(s["rows_in"], 96)
                ht = h[:, bass.ds(t, 1), :].rearrange("p a d -> p (a d)")
                pool.tensor_tensor(ht, ht, b_out[:, :], ALU.add).then_inc(s["resid"], 1)
                pool.wait_ge(s["av"], t + 1)
                pool.tensor_tensor(decay[:, :, :], over_heads(av, 8, P), repeated(upper[:, :], 8, P),
                                   ALU.mult).then_inc(s["au"], 1)
                pool.wait_ge(s["xdt"], t + 1)
                pool.wait_ge(s["te"], t + 1)
                pool.tensor_tensor(xw[:, :].rearrange("p (h d) -> p h d", h=SH),
                                   xdt[:, :].rearrange("p (h d) -> p h d", h=SH),
                                   over_heads(te, 8, SP_), ALU.mult).then_inc(s["xw"], 1)
                pool.wait_ge(s["oT1"], t + 1)
                met()
                pool.tensor_copy(kT[:, 0, :], kT[:, 1, :]).then_inc(s["shift"], 1)
                pool.tensor_copy(v[:, 0, :], v[:, 1, :]).then_inc(s["shift"], 1)
                pool.memset(prevmask[:, :], 0.0).then_inc(s["shift"], 1)
                pool.wait_ge(s["ssg"], 2 * t + 2)
                rstd_of(pool, norm_c, stat[:, 4:6], stat[:, 2:4], 2, s["rstd_g_ms"], s["rstd_g"], t + 1)

        @block.scalar
        def _(act):
            def small_row(dst, src):
                act.dma_start(dst, src).then_inc(s["rows_in"], 16)
            with nc.allow_non_contiguous_dma("gains on partitions"):
                act.dma_start(g_mix[:, :], a["g_mix"].rearrange("a (k p) -> p (a k)", p=P)).then_inc(s["cols_in"], 16)
                act.dma_start(conv_b[:, :], a["conv_b"].rearrange("a (k p) -> p (a k)", p=P)).then_inc(s["cols_in"], 16)
                act.dma_start(g_ssm[:, :], a["g_ssm_out"].rearrange("a (k p) -> p (a k)", p=P)).then_inc(s["cols_in"], 16)
                for j in range(CW):
                    act.dma_start(conv_w[:, j, :], a["conv_w"][0, j, :].rearrange("(k p) -> p k", p=P)).then_inc(s["cols_in"], 16)
            small_row(b_qkv[:, :], a["b_qkv"][0, :].partition_broadcast(P))
            small_row(b_out[:, :], a["b_out"][0, :].partition_broadcast(P))
            for i, n in enumerate(["dt_bias", "a_log", "d_skip", "attn_sinks"]):
                small_row(small[:, i, :], a[n][0, :].partition_broadcast(P))
            act.wait_ge(s["bias_rows"], 1)
            act.dma_start(scratch["bias_rows"], bias_rows[:, :].unsqueeze(1).to_broadcast([8, P, 3 * P])).then_inc(s["bias_out"], 16)
            act.wait_ge(s["bias_out"], 16)
            src = scratch["bias_rows"]
            act.dma_start(bias[:, :, :], bass.AP(src.tensor, P - 1, [[3 * P - 1, P], [3 * P * P, 8], [1, 2 * P]])).then_inc(s["bias"], 16)
            act.wait_ge(s["rows_in"], 96)
            act.activation(a_head, a_head, ACT.Exp).then_inc(s["a_exp"], 1)
            act.wait_ge(s["x0"], 16)
            act.wait_ge(s["cols_in"], 16 * 7)
            act.wait_ge(s["consts"], 64)
            act.wait_ge(s["x"], 16)
            def met():
                act.activation(spare[:, 0:1], ident[:, 0:1], ACT.Copy)

            with act.Fori(0, NT) as t:
                ht = h[:, bass.ds(t, 1), :].rearrange("p a d -> p (a d)")
                act.wait_ge(s["xbcT"], t)
                met()
                act.activation(row[:, :], ht, ACT.Square, scale=1 / 32, accum_out=stat[:, 0:1]).then_inc(s["ss"], 1)
                act.wait_ge(s["rstd"], t + 1)
                met()
                act.activation(row[:, :], ht, ACT.Copy, scale=stat[:, 1:2]).then_inc(s["xn"], 1)
                act.wait_ge(s["p_xbc"], t + 1)
                act.activation(row[:, 0:512], ps[2][:, :], ACT.Copy).then_inc(s["xbc0"], 1)
                act.wait_ge(s["p_z"], t + 1)
                act.activation(zg[:, :], ps[6][:, :], ACT.Silu).then_inc(s["zg"], 1)
                act.wait_ge(s["xbcT"], t + 1)
                act.wait_ge(s["conv"], t)
                act.activation(ext[:, 0:4, CW - 1:], ps[0][:, :].rearrange("p (c n) -> p c n", c=4), ACT.Copy).then_inc(s["ext0"], 1)
                act.wait_ge(s["qkT_ps"], t + 1)
                act.activation(qT[:, :, :], ps[7][:, :].rearrange("p (c n) -> p c n", c=4), ACT.Copy).then_inc(s["qT"], 1)
                act.wait_ge(s["nabs"], t + 1)
                act.activation(ex, nabs, ACT.Exp, scale=-1.0).then_inc(s["ex"], 1)
                act.wait_ge(s["w1p"], t + 1)
                act.activation(lnw, w1p, ACT.Ln).then_inc(s["lnw"], 1)
                for g in range(2):
                    if g == 1:
                        act.wait_ge(s["acsB"], t + 1)
                        act.wait_ge(s["te_in"], t + 1)
                        act.activation(ea, acs, ACT.Exp).then_inc(s["ea"], 1)
                        act.activation(te, te, ACT.Exp).then_inc(s["te"], 1)
                        act.activation(cd, cd, ACT.Exp).then_inc(s["cd"], 1)
                        for hh in range(8):
                            act.activation(decay[:, hh, :], ps[2 + hh // 4][:, P * (hh % 4):P * (hh % 4) + P], ACT.Exp,
                                           bias=nacs[:, hh:hh + 1]).then_inc(s["decay"], 1)
                    act.wait_ge(s["negm"], 2 * t + g + 1)
                    for j in range(4):
                        act.activation(sc[:, j, :], sc[:, j, :], ACT.Exp, bias=sm[:, 1, 4 * g + j:4 * g + j + 1],
                                       accum_out=sm[:, 2, 4 * g + j:4 * g + j + 1]).then_inc(s["pexp"], 1)
                    act.activation(sm[:, 3, 4 * g:4 * g + 4], sm[:, 5, 4 * g:4 * g + 4], ACT.Exp).then_inc(s["sinkexp"], 1)
                    act.wait_ge(s["pT_ps"], 2 * t + g + 1)
                    act.activation(pT[:, 0, :, :], ps[6][:, :].rearrange("p (c n) -> p c n", c=4), ACT.Copy).then_inc(s["pT0"], 1)
                act.wait_ge(s["conv"], t + 1)
                for c in range(NC_):
                    act.activation(cv[:, c, :], cv[:, c, :], ACT.Silu, bias=conv_b[:, c:c + 1]).then_inc(s["cv"], 1)
                act.wait_ge(s["xsbT"], t + 1)
                act.activation(xs[:, :], ps[0][:, :], ACT.Copy).then_inc(s["xs"], 1)
                act.activation(bt[:, :], ps[1][:, 0:256], ACT.Copy).then_inc(s["bt"], 1)
                act.wait_ge(s["oT1"], t + 1)
                act.activation(catT[:, 4:8, :], ps[5][:, :].rearrange("p (c n) -> p c n", c=4), ACT.Copy).then_inc(s["cat1"], 1)
                act.wait_ge(s["yg"], t + 1)
                for g in range(2):
                    act.activation(y2[:, 256 * g:256 * g + 256], y[:, 256 * g:256 * g + 256], ACT.Square, scale=1 / 16,
                                   accum_out=stat[:, 2 + g:3 + g]).then_inc(s["ssg"], 1)

        @block.tensor
        def _(pe):
            pe.wait_ge(s["consts"], 64)
            pe.matmul(ps[0][0:8, 0:P], rel_bias[:, :], bucket_hot[:, :], start=True, stop=True).then_inc(s["bias_ps"], 1)
            pe.wait_ge(s["bias_rows"], 1)
            pe.wait_ge(s["cleared"], 9)
            pe.wait_ge(s["masks"], 2)
            with pe.Fori(0, NT) as t:
                pe.wait_ge(s["xn"], t + 1)
                pe.wait_ge(s["state"], t)
                for k in range(KD):
                    m = pe.transpose(ps[k // 4][:, P * (k % 4):P * (k % 4) + P], row[:, P * k:P * k + P], ident[:, :])
                m.then_inc(s["xnT"], 1)
                pe.wait_ge(s["uT"], 2 * t + 2)
                pe.wait_ge(s["w_in"], 32)
                for n in range(2):
                    for k in range(KD):
                        m = pe.matmul(ps[2 + n][:, :], uT[:, k, :], w_in[:, k, COL_XBC + 512 * n:COL_XBC + 512 * n + 512],
                                      start=k == 0, stop=k == KD - 1)
                m.then_inc(s["p_xbc"], 1)
                for k in range(KD):
                    pe.matmul(ps[4][:, 0:8], uT[:, k, :], w_in[:, k, COL_DT:COL_Q], start=k == 0, stop=k == KD - 1)
                for k in range(KD):
                    m = pe.matmul(ps[4][:, 8:264], uT[:, k, :], w_in[:, k, COL_K:IN_COLS], start=k == 0, stop=k == KD - 1)
                m.then_inc(s["p_kv"], 1)
                pe.wait_ge(s["cat1"], t)
                for k in range(KD):
                    m = pe.matmul(ps[5][:, :], uT[:, k, :], w_in[:, k, COL_Q:COL_K], start=k == 0, stop=k == KD - 1)
                m.then_inc(s["p_q"], 1)
                pe.wait_ge(s["h1"], 2 * t)
                for k in range(KD):
                    m = pe.matmul(ps[6][:, :], uT[:, k, :], w_in[:, k, 0:COL_XBC], start=k == 0, stop=k == KD - 1)
                m.then_inc(s["p_z"], 1)
                pe.wait_ge(s["xbc0"], t + 1)
                pe.wait_ge(s["xbc1"], t + 1)
                for k in range(NC_):
                    m = pe.transpose(ps[k // 4][:, P * (k % 4):P * (k % 4) + P], row[:, P * k:P * k + P], ident[:, :])
                m.then_inc(s["xbcT"], 1)
                pe.wait_ge(s["q_tok"], t + 1)
                for j in range(4):
                    pe.transpose(ps[7][:, P * j:P * j + P], q_tok[:, j, :, :].rearrange("p g d -> p (g d)"), ident[:, :])
                m = pe.transpose(ps[2][:, 0:P], k_tok[:, :], ident[:, :])
                m.then_inc(s["qkT_ps"], 1)
                pe.wait_ge(s["qT"], t + 1)
                pe.wait_ge(s["kT"], t + 1)
                pe.wait_ge(s["zg"], t + 1)
                for g in range(2):
                    if g == 1:
                        pe.wait_ge(s["pT1"], 2 * t + 1)
                    for j in range(4):
                        m = pe.matmul(ps[6 + j // 2][:, 256 * (j % 2):256 * (j % 2) + 256], qT[64 * g:64 * g + 64, j, :],
                                      kT[64 * g:64 * g + 64, :, :].rearrange("p a n -> p (a n)"), start=True, stop=True)
                    m.then_inc(s["scores"], 1)
                    if g == 0:
                        pe.wait_ge(s["av"], t + 1)
                        pe.matmul(ps[4][:, 0:8], upper[:, :], av, start=True, stop=True).then_inc(s["acs_ps"], 1)
                        pe.wait_ge(s["au"], t + 1)
                        for n in range(2):
                            pe.matmul(ps[2 + n][:, :], ones[:, :], decay[:, 4 * n:4 * n + 4, :].rearrange("p h n -> p (h n)"),
                                      start=True, stop=False)
                            m = pe.matmul(ps[2 + n][:, :], ident_b[:, :], negmask_b[:, :, :].rearrange("p h n -> p (h n)"),
                                          start=False, stop=True)
                        m.then_inc(s["acsB"], 1)
                    pe.wait_ge(s["probs"], 2 * t + g + 1)
                    for half in range(2):
                        for j in range(4):
                            m = pe.transpose(ps[6 + half][:, P * j:P * j + P], sc[:, j, P * half:P * half + P], ident[:, :])
                    m.then_inc(s["pT_ps"], 1)
                    pe.wait_ge(s["pT0"], 2 * t + g + 1)
                    pe.wait_ge(s["pT1"], 2 * t + g + 1)
                    for half in range(2):
                        m = pe.matmul(ps[5][64 * g:64 * g + 64, :], v[:, half, 64 * g:64 * g + 64],
                                      pT[:, half, :, :].rearrange("p c n -> p (c n)"), start=half == 0, stop=half == 1)
                    m.then_inc(s["oT0" if g == 0 else "oT1"], 1)
                pe.wait_ge(s["cv"], 8 * t + 8)
                pe.wait_ge(s["acs"], t + 1)
                for g in range(2):
                    m = pe.matmul(ps[4][:, P + P * g:2 * P + P * g], cv[:, 4 + g, :], cv[:, 6 + g, :], start=True, stop=True)
                m.then_inc(s["cb"], 1)
                pe.wait_ge(s["ext1"], t + 1)
                for k in range(4):
                    pe.transpose(ps[0][:, P * k:P * k + P], cv[:, k, :], ident[:, :])
                for k in range(2):
                    m = pe.transpose(ps[1][:, P * k:P * k + P], cv[:, 4 + k, :], ident[:, :])
                m.then_inc(s["xsbT"], 1)
                pe.wait_ge(s["decay"], 8 * t + 8)
                for g in range(2):
                    m = pe.matmul(ps[3][:, 256 * g:256 * g + 256], cv[:, 6 + g, :], state[:, 256 * g:256 * g + 256],
                                  start=True, stop=True)
                m.then_inc(s["yoff"], 1)
                pe.wait_ge(s["mt"], 2 * t + 2)
                pe.wait_ge(s["xdt"], t + 1)
                pe.wait_ge(s["cd"], t + 1)
                for hh in range(SH):
                    m = pe.matmul(ps[2][:, SP_ * hh:SP_ * hh + SP_], decay[:, hh, :], xdt[:, SP_ * hh:SP_ * hh + SP_],
                                  start=True, stop=True)
                m.then_inc(s["ydiag"], 1)
                pe.wait_ge(s["bt"], t + 1)
                pe.wait_ge(s["xw"], t + 1)
                for g in range(2):
                    m = pe.matmul(ps[0][:, 256 * g:256 * g + 256], bt[:, P * g:P * g + P], xw[:, 256 * g:256 * g + 256],
                                  start=True, stop=True)
                m.then_inc(s["st_ps"], 1)
                pe.wait_ge(s["yn"], t + 1)
                for k in range(4):
                    m = pe.transpose(ps[1][:, P * k:P * k + P], y2[:, P * k:P * k + P], ident[:, :])
                m.then_inc(s["yT_ps"], 1)
                pe.wait_ge(s["cat0"], t + 1)
                pe.wait_ge(s["cat1"], t + 1)
                pe.wait_ge(s["w_out"], 48)
                for n in range(2):
                    for k in range(KD):
                        m = pe.matmul(ps[6 + n][:, :], catT[:, k, :], w_out[:, k, 512 * n:512 * n + 512],
                                      start=k == 0, stop=k == KD - 1)
                m.then_inc(s["mixed"], 1)

        @block.vector
        def _(dve):
            dve.wait_ge(s["consts"], 64)
            dve.tensor_copy(ident_b[:, :], ident[:, :]).then_inc(s["masks"], 1)
            dve.tensor_scalar(negmask_b[:, :, :], repeated(upper[:, :], 4, P), -1.0, -NEG, ALU.add, ALU.mult).then_inc(s["masks"], 1)
            dve.wait_ge(s["cleared"], 9)
            dve.wait_ge(s["bias_ps"], 1)
            dve.tensor_copy(bias_rows[:, P:2 * P], ps[0][0:8, 0:P]).then_inc(s["bias_rows"], 1)
            dve.wait_ge(s["a_exp"], 1)
            dve.tensor_scalar(a_head, a_head, -1.0, None, ALU.mult).then_inc(s["a_head"], 1)
            dve.wait_ge(s["bias"], 16)
            with dve.Fori(0, NT) as t:
                dve.wait_ge(s["xnT"], t + 1)
                for n in range(2):
                    dve.tensor_tensor(uT[:, 4 * n:4 * n + 4, :], ps[n][:, :].rearrange("p (c n) -> p c n", c=4),
                                      over_heads(g_mix[:, 4 * n:4 * n + 4], 4, P), ALU.mult).then_inc(s["uT"], 1)
                dve.wait_ge(s["p_xbc"], t + 1)
                dve.tensor_copy(row[:, 512:1024], ps[3][:, :]).then_inc(s["xbc1"], 1)
                dve.wait_ge(s["p_kv"], t + 1)
                dve.tensor_tensor(draw, ps[4][:, 0:8], dt_bias, ALU.add).then_inc(s["draw"], 1)
                dve.wait_ge(s["shift"], 3 * t)
                dve.tensor_tensor(k_tok[:, :], ps[4][:, 8:136], b_qkv[:, 512:640], ALU.add).then_inc(s["k_tok"], 1)
                dve.tensor_tensor(v[:, 1, :], ps[4][:, 136:264], b_qkv[:, 640:768], ALU.add).then_inc(s["v_tok"], 1)
                dve.wait_ge(s["draw"], t + 1)
                dve.scalar_tensor_tensor(nabs, draw, -1.0, draw, ALU.mult, ALU.max).then_inc(s["nabs"], 1)
                dve.wait_ge(s["p_q"], t + 1)
                dve.tensor_tensor(q_tok[:, :, :, :].rearrange("p j g d -> p g j d"),
                                  ps[5][:, :].rearrange("p (g j d) -> p g j d", g=2, j=4),
                                  b_qkv[:, 0:512].rearrange("p (g j d) -> p g j d", g=2, j=4), ALU.add).then_inc(s["q_tok"], 1)
                dve.wait_ge(s["ex"], t + 1)
                dve.tensor_scalar(w1p, ex, 1.0, None, ALU.add).then_inc(s["w1p"], 1)
                dve.wait_ge(s["w1p"], t + 1)
                dve.scalar_tensor_tensor(rest, w1p, -1.0, ex, ALU.add, ALU.subtract).then_inc(s["rest"], 1)
                dve.reciprocal(rw, w1p).then_inc(s["rw"], 1)
                dve.wait_ge(s["rw"], t + 1)
                dve.tensor_tensor(rest, rest, rw, ALU.mult).then_inc(s["rest2"], 1)
                dve.wait_ge(s["rest2"], t + 1)
                dve.wait_ge(s["lnw"], t + 1)
                dve.tensor_tensor(lnw, lnw, rest, ALU.subtract).then_inc(s["ln1p"], 1)
                dve.wait_ge(s["ln1p"], t + 1)
                dve.scalar_tensor_tensor(dt, draw, 0.0, lnw, ALU.max, ALU.add).then_inc(s["dt"], 1)
                dve.wait_ge(s["dt"], t + 1)
                dve.tensor_tensor(av, dt, a_head, ALU.mult).then_inc(s["av"], 1)
                dve.wait_ge(s["xbcT"], t + 1)
                dve.tensor_copy(ext[:, 4:8, CW - 1:], ps[1][:, :].rearrange("p (c n) -> p c n", c=4)).then_inc(s["ext1"], 1)
                dve.wait_ge(s["qkT_ps"], t + 1)
                dve.tensor_copy(kT[:, 1, :], ps[2][:, 0:P]).then_inc(s["kT"], 1)
                dve.wait_ge(s["acs_ps"], t + 1)
                dve.tensor_copy(acs, ps[4][:, 0:8]).then_inc(s["acs"], 1)
                dve.wait_ge(s["acs"], t + 1)
                dve.tensor_scalar(nacs, acs, -1.0, None, ALU.mult).then_inc(s["nacs"], 1)
                for g in range(2):
                    dve.wait_ge(s["scores"], 2 * t + g + 1)
                    for n in range(2):
                        dve.scalar_tensor_tensor(sc[:, 2 * n:2 * n + 2, :], ps[6 + n][:, :].rearrange("p (c n) -> p c n", c=2),
                                                 HD ** -0.5, bias[:, 4 * g + 2 * n:4 * g + 2 * n + 2, :],
                                                 ALU.mult, ALU.add).then_inc(s["sc"], 1)
                    dve.wait_ge(s["sc"], 4 * t + 2 * g + 2)
                    dve.tensor_scalar(sc[:, :, 0:P], sc[:, :, 0:P], prevmask[:, 0:1], None, ALU.add).then_inc(s["scm"], 1)
                    dve.wait_ge(s["scm"], 2 * t + g + 1)
                    hs = slice(4 * g, 4 * g + 4)
                    dve.tensor_reduce(sm[:, 0, hs], sc[:, :, :], AX_X, ALU.max).then_inc(s["smax"], 1)
                    dve.wait_ge(s["smax"], 2 * t + g + 1)
                    dve.tensor_tensor(sm[:, 0, hs], sm[:, 0, hs], sinks[:, hs], ALU.max).then_inc(s["smax2"], 1)
                    dve.wait_ge(s["smax2"], 2 * t + g + 1)
                    dve.tensor_tensor(sm[:, 5, hs], sinks[:, hs], sm[:, 0, hs], ALU.subtract).then_inc(s["sinkd"], 1)
                    dve.wait_ge(s["sinkd"], 2 * t + g + 1)
                    dve.tensor_scalar(sm[:, 1, hs], sm[:, 0, hs], -1.0, None, ALU.mult).then_inc(s["negm"], 1)
                    if g == 0:
                        dve.wait_ge(s["acsB"], t + 1)
                        dve.wait_ge(s["nacs"], t + 1)
                        dve.tensor_copy(cd[:, 0:4], ps[2][:, P - 1::P]).then_inc(s["last"], 1)
                        dve.tensor_copy(cd[:, 4:8], ps[3][:, P - 1::P]).then_inc(s["last"], 1)
                        dve.wait_ge(s["last"], 2 * t + 2)
                        dve.tensor_tensor(te, cd, nacs, ALU.add).then_inc(s["te_in"], 1)
                        dve.wait_ge(s["ext0"], t + 1)
                        dve.wait_ge(s["ext1"], t + 1)
                        for j in range(CW):
                            if j:
                                dve.wait_ge(s["tap"], (CW * NC_) * t + NC_ * j)
                            for c in range(NC_):
                                if j == 0:
                                    m = dve.tensor_scalar(cv[:, c, :], ext[:, c, 0:P], conv_w[:, 0, c:c + 1], None, ALU.mult)
                                else:
                                    m = dve.scalar_tensor_tensor(cv[:, c, :], ext[:, c, j:j + P], conv_w[:, j, c:c + 1],
                                                                 cv[:, c, :], ALU.mult, ALU.add)
                                m.then_inc(s["tap"], 1)
                        dve.wait_ge(s["tap"], (CW * NC_) * t + CW * NC_)
                        dve.tensor_copy(ext[:, :, 0:CW - 1], ext[:, :, P:P + CW - 1]).then_inc(s["conv"], 1)
                    dve.wait_ge(s["pexp"], 8 * t + 4 * g + 4)
                    dve.wait_ge(s["sinkexp"], 2 * t + g + 1)
                    dve.tensor_tensor(sm[:, 4, hs], sm[:, 2, hs], sm[:, 3, hs], ALU.add).then_inc(s["den"], 1)
                    dve.wait_ge(s["den"], 2 * t + g + 1)
                    dve.reciprocal(sm[:, 4, hs], sm[:, 4, hs]).then_inc(s["rden"], 1)
                    dve.wait_ge(s["rden"], 2 * t + g + 1)
                    dve.tensor_tensor(sc[:, :, :], sc[:, :, :], over_heads(sm[:, 4, hs], 4, 2 * P), ALU.mult).then_inc(s["probs"], 1)
                    dve.wait_ge(s["pT_ps"], 2 * t + g + 1)
                    dve.tensor_copy(pT[:, 1, :, :], ps[7][:, :].rearrange("p (c n) -> p c n", c=4)).then_inc(s["pT1"], 1)
                dve.wait_ge(s["cb"], t + 1)
                for g in range(2):
                    dve.tensor_tensor(decay[:, 4 * g:4 * g + 4, :], decay[:, 4 * g:4 * g + 4, :],
                                      repeated(ps[4][:, P + P * g:2 * P + P * g], 4, P), ALU.mult).then_inc(s["mt"], 1)
                dve.wait_ge(s["xs"], t + 1)
                hd = lambda ap: ap.rearrange("p (h d) -> p h d", h=SH)
                dve.tensor_tensor(hd(xdt[:, :]), hd(xs[:, :]), over_heads(dt, 8, SP_), ALU.mult).then_inc(s["xdt"], 1)
                dve.tensor_tensor(hd(xs[:, :]), hd(xs[:, :]), over_heads(d_skip, 8, SP_), ALU.mult).then_inc(s["skip"], 1)
                dve.wait_ge(s["yoff"], t + 1)
                dve.wait_ge(s["ea"], t + 1)
                dve.tensor_tensor(hd(y[:, :]), hd(ps[3][:, :]), over_heads(ea, 8, SP_), ALU.mult).then_inc(s["y0"], 1)
                dve.wait_ge(s["y0"], t + 1)
                dve.wait_ge(s["skip"], t + 1)
                dve.tensor_tensor(y[:, :], y[:, :], xs[:, :], ALU.add).then_inc(s["y1"], 1)
                dve.wait_ge(s["y1"], t + 1)
                dve.wait_ge(s["ydiag"], t + 1)
                dve.tensor_tensor(y[:, :], y[:, :], ps[2][:, :], ALU.add).then_inc(s["y2"], 1)
                dve.wait_ge(s["y2"], t + 1)
                dve.tensor_tensor(y[:, :], y[:, :], zg[:, :], ALU.mult).then_inc(s["yg"], 1)
                dve.wait_ge(s["cd"], t + 1)
                dve.tensor_tensor(hd(state[:, :]), hd(state[:, :]), over_heads(cd, 8, SP_), ALU.mult).then_inc(s["st_dec"], 1)
                dve.wait_ge(s["st_dec"], t + 1)
                dve.wait_ge(s["st_ps"], t + 1)
                dve.tensor_tensor(state[:, :], state[:, :], ps[0][:, :], ALU.add).then_inc(s["state"], 1)
                dve.wait_ge(s["rstd_g"], t + 1)
                dve.tensor_tensor(y2[:, :].rearrange("p (g n) -> p g n", g=2), y[:, :].rearrange("p (g n) -> p g n", g=2),
                                  over_heads(stat[:, 4:6], 2, 256), ALU.mult).then_inc(s["yn"], 1)
                dve.wait_ge(s["yT_ps"], t + 1)
                dve.tensor_tensor(catT[:, 0:4, :], ps[1][:, :].rearrange("p (c n) -> p c n", c=4),
                                  over_heads(g_ssm[:, :], 4, P), ALU.mult).then_inc(s["cat0"], 1)
                dve.wait_ge(s["mixed"], t + 1)
                dve.wait_ge(s["resid"], t + 1)
                for n in range(2):
                    hn = h[:, bass.ds(t, 1), 512 * n:512 * n + 512].rearrange("p a d -> p (a d)")
                    dve.tensor_tensor(hn, ps[6 + n][:, :], hn, ALU.add).then_inc(s["h1"], 1)


def cross_stage(nc, a, h, gates, plan_row, scratch):
    with ExitStack() as ctx:
        sb = lambda n, s, d=F32: ctx.enter_context(nc.sbuf_tensor(n, s, d))
        s = Signals(nc, ctx, "cx")
        w_kv = sb("w_kv_sb", [P, KD, 2 * XH * XD])
        w_q = sb("w_q_sb", [P, KD, XH * XD])
        w_o = sb("w_o_sb", [P, XH, D])
        w_r = sb("w_router_sb", [P, KD, NE])
        ident = sb("ident2", [P, P])
        upper = sb("upper2", [P, P])
        before_b = sb("before_b", [P, P], BF16)
        ones_b = sb("ones_b", [P, P], BF16)
        gains = sb("gains", [P, 3, KD])
        b_r = sb("b_router_sb", [P, NE])
        iota_e = sb("iota_e", [P, NE])
        entry = sb("slot_entries", [P, NT, TOPK, 2], I32)
        slots = sb("slots", [P, NT, TOPK], I32)
        zero_slots = sb("zero_slots", [P, NE * REGION // P, 2], I32)

        mem = sb("mem_rows", [P, 2, D])
        memT = sb("memT", [P, KD, MEM])
        kxT = sb("kxT", [P, XH, MEM])
        vx = sb("vx", [P, 2, XH * XD])
        stat = sb("stat2", [P, 12])
        norm_c = sb("norm_c2", [P, 2, 2])
        spare = sb("spare2", [P, 2])
        xn = sb("xn", [P, D])
        uT = sb("uT2", [P, KD, P])
        q_tok = sb("qx_tok", [P, XH * XD])
        qT = sb("qxT", [P, XH, P])
        pr = sb("px", [P, XH, MEM])
        pT = sb("pxT", [P, 2, XH, P])
        oT = sb("oxT", [P, XH, P])
        sm = sb("softmax2", [P, 4, XH])
        rows = sb("moe_rows", [P, D])
        lg = sb("logits", [P, NE])
        mx = sb("top8", [P, 8])
        ix = sb("top8_index", [P, 8], U32)
        ixf = sb("top_index", [P, TOPK])
        ge = sb("gate_exp", [P, TOPK])
        hot = sb("chosen", [P, TOPK, NE])
        picked = sb("picked", [P, TOPK, NE])
        mask = sb("mask", [P, NE])
        mask_b = sb("mask_b", [P, NE], BF16)
        carry = sb("carry", [P, NE])
        rank = sb("rank", [P, NE])
        rank4 = sb("rank4", [P, TOPK])
        slot_f = sb("slot_f", [P, TOPK])
        pl = sb("plan_work", [P, 8, NE])
        (c_up, n_pass, n_cum, before, tmp, e_hot) = (pl[:, i, :] for i in range(6))
        pi = sb("plan_int", [P, NE], I32)
        ones_e = sb("ones_e", [P, NE])
        iota_i = sb("iota_i", [P, 1])
        pv = sb("plan_values", [P, 12])
        plan = sb("plan", [P, 4], I32)

        bias_all = sb("bias_all", [NE, FF2 + D])
        bias_parts = sb("bias_parts", [NE, 3, FF2 + D], BF16)

        ps = [ctx.enter_context(nc.psum_tensor(f"cx_b{i}", [P, 512], F32)) for i in range(8)]
        block = ctx.enter_context(nc.Block())
        c4 = lambda ap: ap.rearrange("p (c n) -> p c n", c=4)
        tile_of = lambda t: h[:, bass.ds(t, 1), :].rearrange("p a d -> p (a d)")

        @block.sync
        def _(sp):
            sp.dma_start(ident[:, :], a["c_ident"]).then_inc(s["consts"], 16)
            sp.dma_start(upper[:, :], a["c_upper"]).then_inc(s["consts"], 16)
            sp.dma_start(mem[:, :, :], a["mem"][0].rearrange("(m p) d -> p m d", p=P)).then_inc(s["mem"], 16)
            sp.dma_start(w_kv[:, :, :], a["w_kv_cross"][0].rearrange("(k p) n -> p k n", p=P)).then_inc(s["w_kv"], 16)
            sp.dma_start(w_q[:, :, :], a["w_q_cross"][0].rearrange("(k p) n -> p k n", p=P)).then_inc(s["w_q"], 16)
            sp.dma_start(w_o[:, :, :], a["w_o_cross"][0].rearrange("(k p) n -> p k n", p=P)).then_inc(s["w_o"], 16)
            with nc.allow_non_contiguous_dma("gains on partitions"):
                for i, n in enumerate(["g_mem", "g_cross", "g_ffn"]):
                    sp.dma_start(gains[:, i, :], a[n].rearrange("a (k p) -> p (a k)", p=P)).then_inc(s["gains"], 16)
                sp.dma_start(w_r[:, :, :], a["w_router"][0].rearrange("(k p) n -> p k n", p=P)).then_inc(s["w_r"], 16)
            sp.dma_start(b_r[:, :], a["b_router"][0, :].partition_broadcast(P)).then_inc(s["w_r"], 16)
            sp.dma_start(bias_all[:, 0:FF2], a["b1"][0]).then_inc(s["bias_all"], 16)
            sp.dma_start(bias_all[:, FF2:], a["b2"][0]).then_inc(s["bias_all"], 16)
            sp.wait_ge(s["bias_parts"], 5)
            sp.dma_start(scratch["bias_parts"].rearrange("e j n -> e (j n)"), bias_parts[:, :, :].rearrange("e j n -> e (j n)")).then_inc(s["parts_out"], 16)
            with sp.Fori(0, NT) as t:
                sp.wait_ge(s["rows"], t + 1)
                sp.dma_start(scratch["rows"][bass.ds(t * P, P), :], rows[:, :]).then_inc(s["rows_out"], 16)
            sp.wait_ge(s["rows_out"], 16 * NT)
            sp.wait_ge(s["parts_out"], 16)
            sp.wait_ge(s["plan"], 4)
            sp.dma_start(scratch["plan"], plan[0:MAX_PASSES + 1, :]).then_inc(s["plan_out"], 16)
            sp.wait_ge(s["plan_out"], 16)
            sp.dma_start(plan_row[0:1, :], scratch["plan"].rearrange("(a p) c -> a (p c)", a=1)).then_inc(s["plan_in"], 16)
            sp.wait_ge(s["plan_in"], 16)

        @block.gpsimd
        def _(pool):
            pool.memset(zero_slots[:, :, 0:1], 0).then_inc(s["setup"], 1)
            pool.memset(zero_slots[:, :, 1:2], SEQ * TOPK).then_inc(s["setup"], 1)
            pool.memset(ones_b[:, :], 1.0).then_inc(s["setup"], 1)
            pool.memset(ones_e[:, :], 1.0).then_inc(s["setup"], 1)
            pool.memset(carry[:, :], 0.0).then_inc(s["setup"], 1)
            pool.iota(iota_e[:, :], [[1, NE]], base=0, channel_multiplier=0, allow_small_or_imprecise_dtypes=True).then_inc(s["setup"], 1)
            pool.iota(iota_i[:, :], [[0, 1]], base=0, channel_multiplier=1, allow_small_or_imprecise_dtypes=True).then_inc(s["setup"], 1)
            pool.iota(entry[:, :, :, 0], [[P, NT], [0, TOPK]], base=0, channel_multiplier=1).then_inc(s["setup"], 1)
            pool.iota(entry[:, :, :, 1], [[TOPK * P, NT], [1, TOPK]], base=0, channel_multiplier=TOPK).then_inc(s["setup"], 1)
            pool.memset(norm_c[:, 0, :], EPS).then_inc(s["setup"], 1)
            pool.memset(norm_c[:, 1, :], -0.5).then_inc(s["setup"], 1)
            pool.wait_ge(s["setup"], 11)
            pool.dma_start(scratch["slot_table"].rearrange("(p f) a -> p (f a)", p=P), zero_slots[:, :, :].rearrange("p f a -> p (f a)")).then_inc(s["table_clear"], 16)
            pool.wait_ge(s["mem_ss"], 2)
            rstd_of(pool, norm_c, stat[:, 2:4], stat[:, 0:2], 2, s["mem_rstd_ms"], s["mem_rstd"], 1)
            pool.wait_ge(s["table_clear"], 16)
            for t in range(NT):
                pool.wait_ge(s["ss"], t + 1)
                rstd_of(pool, norm_c, stat[:, 5:6], stat[:, 4:5], 1, s["rstd_ms"], s["rstd"], t + 1)
                pool.wait_ge(s["ss2"], t + 1)
                rstd_of(pool, norm_c, stat[:, 7:8], stat[:, 6:7], 1, s["rstd2_ms"], s["rstd2"], t + 1)
                pool.wait_ge(s["slots"], t + 1)
                for j in range(TOPK):
                    pool.indirect_dma_start(scratch["slot_table"], bass.IndirectOffsetOnAxis(ap=slots[:, t, j:j + 1], axis=0),
                                            entry[:, t, j, :], None).then_inc(s["table"], 16)
            pool.wait_ge(s["table"], 16 * NT * TOPK)

        @block.scalar
        def _(act):
            act.wait_ge(s["mem"], 16)
            for m in range(2):
                act.activation((xn, rows)[m][:, :], mem[:, m, :], ACT.Square, scale=1 / 32, accum_out=stat[:, m:m + 1]).then_inc(s["mem_ss"], 1)
            act.wait_ge(s["mem_rstd"], 1)
            for m in range(2):
                act.activation(mem[:, m, :], mem[:, m, :], ACT.Copy, scale=stat[:, 2 + m:3 + m]).then_inc(s["mem_n"], 1)
            act.wait_ge(s["kx_ps"], 1)
            for n in range(2):
                act.activation(kxT[:, 2 * n:2 * n + 2, :], ps[2 + n][:, :].rearrange("p (c n) -> p c n", c=2), ACT.Copy).then_inc(s["kxT"], 1)
            def met():
                act.activation(spare[:, 0:1], ident[:, 0:1], ACT.Copy)

            with act.Fori(0, NT) as t:
                act.wait_ge(s["uTr"], 2 * t)
                met()
                act.activation(xn[:, :], tile_of(t), ACT.Square, scale=1 / 32, accum_out=stat[:, 4:5]).then_inc(s["ss"], 1)
                act.wait_ge(s["rstd"], t + 1)
                met()
                act.activation(xn[:, :], tile_of(t), ACT.Copy, scale=stat[:, 5:6]).then_inc(s["xn"], 1)
                act.wait_ge(s["q_ps"], t + 1)
                act.activation(q_tok[:, :], ps[2][:, :], ACT.Copy).then_inc(s["q_tok"], 1)
                act.wait_ge(s["qT_ps"], t + 1)
                act.activation(qT[:, :, :], c4(ps[3][:, :]), ACT.Copy).then_inc(s["qT"], 1)
                act.wait_ge(s["negm"], t + 1)
                for j in range(XH):
                    act.activation(pr[:, j, :], ps[4 + j // 2][:, MEM * (j % 2):MEM * (j % 2) + MEM], ACT.Exp, scale=XD ** -0.5,
                                   bias=sm[:, 1, j:j + 1], accum_out=sm[:, 2, j:j + 1]).then_inc(s["pexp"], 1)
                act.wait_ge(s["pT_ps"], t + 1)
                act.activation(pT[:, 0, :, :], c4(ps[6][:, :]), ACT.Copy).then_inc(s["pT0"], 1)
                act.wait_ge(s["oT_ps"], t + 1)
                act.activation(oT[:, :, :], c4(ps[2][:, :]), ACT.Copy).then_inc(s["oT"], 1)
                act.wait_ge(s["h2"], 2 * t + 2)
                act.wait_ge(s["rows_out"], 16 * t)
                met()
                act.activation(rows[:, :], tile_of(t), ACT.Square, scale=1 / 32, accum_out=stat[:, 6:7]).then_inc(s["ss2"], 1)
                act.wait_ge(s["rstd2"], t + 1)
                met()
                act.activation(rows[:, :], tile_of(t), ACT.Copy, scale=stat[:, 7:8]).then_inc(s["rows"], 1)
                act.wait_ge(s["neg1"], t + 1)
                act.activation(ge[:, :], mx[:, 0:TOPK], ACT.Exp, bias=stat[:, 8:9], accum_out=stat[:, 9:10]).then_inc(s["ge"], 1)

        @block.tensor
        def _(pe):
            pe.wait_ge(s["consts"], 32)
            pe.wait_ge(s["mem_n"], 2)
            for m in range(2):
                for n in range(2):
                    for k in range(4):
                        i = 4 * n + k
                        tr = pe.transpose(ps[2 * m + n][:, P * k:P * k + P], mem[:, m, P * i:P * i + P], ident[:, :])
            tr.then_inc(s["memT_ps"], 1)
            pe.wait_ge(s["memT"], 4)
            pe.wait_ge(s["w_kv"], 16)
            for j in range(XH):
                for k in range(KD):
                    m = pe.matmul(ps[2 + j // 2][:, MEM * (j % 2):MEM * (j % 2) + MEM], w_kv[:, k, XD * j:XD * j + XD], memT[:, k, :],
                                  start=k == 0, stop=k == KD - 1)
            m.then_inc(s["kx_ps"], 1)
            for half in range(2):
                for k in range(KD):
                    m = pe.matmul(ps[4 + half][:, :], memT[:, k, P * half:P * half + P], w_kv[:, k, XH * XD:],
                                  start=k == 0, stop=k == KD - 1)
            m.then_inc(s["vx_ps"], 1)
            pe.wait_ge(s["kxT"], 2)
            pe.wait_ge(s["vx"], 2)
            pe.wait_ge(s["setup"], 11)
            pe.wait_ge(s["before"], 1)
            with pe.Fori(0, NT) as t:
                pe.wait_ge(s["xn"], t + 1)
                pe.wait_ge(s["uTr"], 2 * t)
                for k in range(KD):
                    m = pe.transpose(ps[k // 4][:, P * (k % 4):P * (k % 4) + P], xn[:, P * k:P * k + P], ident[:, :])
                m.then_inc(s["xnT"], 1)
                pe.wait_ge(s["uT"], 2 * t + 2)
                pe.wait_ge(s["w_q"], 16)
                for k in range(KD):
                    m = pe.matmul(ps[2][:, :], uT[:, k, :], w_q[:, k, :], start=k == 0, stop=k == KD - 1)
                m.then_inc(s["q_ps"], 1)
                pe.wait_ge(s["q_tok"], t + 1)
                pe.wait_ge(s["lg"], t)
                for k in range(XH):
                    m = pe.transpose(ps[3][:, P * k:P * k + P], q_tok[:, P * k:P * k + P], ident[:, :])
                m.then_inc(s["qT_ps"], 1)
                pe.wait_ge(s["qT"], t + 1)
                pe.wait_ge(s["h2"], 2 * t)
                for j in range(XH):
                    m = pe.matmul(ps[4 + j // 2][:, MEM * (j % 2):MEM * (j % 2) + MEM], qT[:, j, :], kxT[:, j, :], start=True, stop=True)
                m.then_inc(s["scores"], 1)
                pe.wait_ge(s["probs"], t + 1)
                pe.wait_ge(s["carry"], t)
                for half in range(2):
                    for j in range(XH):
                        m = pe.transpose(ps[6 + half][:, P * j:P * j + P], pr[:, j, P * half:P * half + P], ident[:, :])
                m.then_inc(s["pT_ps"], 1)
                pe.wait_ge(s["pT0"], t + 1)
                pe.wait_ge(s["pT1"], t + 1)
                for j in range(XH):
                    for half in range(2):
                        m = pe.matmul(ps[2][:, P * j:P * j + P], vx[:, half, XD * j:XD * j + XD], pT[:, half, j, :],
                                      start=half == 0, stop=half == 1)
                m.then_inc(s["oT_ps"], 1)
                pe.wait_ge(s["oT"], t + 1)
                pe.wait_ge(s["w_o"], 16)
                for n in range(2):
                    for k in range(XH):
                        m = pe.matmul(ps[4 + n][:, :], oT[:, k, :], w_o[:, k, 512 * n:512 * n + 512], start=k == 0, stop=k == XH - 1)
                m.then_inc(s["o_ps"], 1)
                pe.wait_ge(s["rows"], t + 1)
                for k in range(KD):
                    m = pe.transpose(ps[k // 4][:, P * (k % 4):P * (k % 4) + P], rows[:, P * k:P * k + P], ident[:, :])
                m.then_inc(s["rowsT"], 1)
                pe.wait_ge(s["uTr"], 2 * t + 2)
                pe.wait_ge(s["w_r"], 32)
                for k in range(KD):
                    m = pe.matmul(ps[3][:, 0:NE], uT[:, k, :], w_r[:, k, :], start=k == 0, stop=k == KD - 1)
                m.then_inc(s["lg_ps"], 1)
                pe.wait_ge(s["mask_b"], t + 1)
                pe.matmul(ps[6][:, 0:NE], before_b[:, :], mask_b[:, :], start=True, stop=True).then_inc(s["rank_ps"], 1)
                pe.matmul(ps[7][:, 0:NE], ones_b[:, :], mask_b[:, :], start=True, stop=True).then_inc(s["count_ps"], 1)

        @block.vector
        def _(dve):
            dve.wait_ge(s["consts"], 32)
            dve.tensor_tensor(before_b[:, :], upper[:, :], ident[:, :], ALU.subtract).then_inc(s["before"], 1)
            dve.wait_ge(s["memT_ps"], 1)
            dve.wait_ge(s["gains"], 48)
            for m in range(2):
                for n in range(2):
                    dve.tensor_tensor(memT[:, 4 * n:4 * n + 4, P * m:P * m + P], c4(ps[2 * m + n][:, :]),
                                      over_heads(gains[:, 0, 4 * n:4 * n + 4], 4, P), ALU.mult).then_inc(s["memT"], 1)
            dve.wait_ge(s["vx_ps"], 1)
            for half in range(2):
                dve.tensor_copy(vx[:, half, :], ps[4 + half][:, :]).then_inc(s["vx"], 1)
            dve.wait_ge(s["bias_all"], 32)
            dve.tensor_copy(bias_parts[:, 0, :], bias_all[:, :]).then_inc(s["bias_parts"], 1)
            for j in range(1, 3):
                dve.wait_ge(s["bias_parts"], 2 * j - 1)
                dve.tensor_tensor(bias_all[:, :], bias_all[:, :], bias_parts[:, j - 1, :],
                                  ALU.subtract).then_inc(s["bias_parts"], 1)
                dve.wait_ge(s["bias_parts"], 2 * j)
                dve.tensor_copy(bias_parts[:, j, :], bias_all[:, :]).then_inc(s["bias_parts"], 1)
            dve.wait_ge(s["setup"], 11)
            dve.wait_ge(s["w_r"], 32)
            def met():
                dve.memset(spare[:, 1:2], 0.0)

            with dve.Fori(0, NT) as t:
                dve.wait_ge(s["xnT"], t + 1)
                for n in range(2):
                    dve.tensor_tensor(uT[:, 4 * n:4 * n + 4, :], c4(ps[n][:, :]), over_heads(gains[:, 1, 4 * n:4 * n + 4], 4, P),
                                      ALU.mult).then_inc(s["uT"], 1)
                dve.wait_ge(s["scores"], t + 1)
                for n in range(2):
                    dve.tensor_reduce(sm[:, 0, 2 * n:2 * n + 2], ps[4 + n][:, :].rearrange("p (c n) -> p c n", c=2), AX_X,
                                      ALU.max).then_inc(s["smax"], 1)
                dve.wait_ge(s["smax"], 2 * t + 2)
                dve.tensor_scalar(sm[:, 1, :], sm[:, 0, :], -XD ** -0.5, None, ALU.mult).then_inc(s["negm"], 1)
                dve.wait_ge(s["pexp"], 4 * t + 4)
                dve.reciprocal(sm[:, 3, :], sm[:, 2, :]).then_inc(s["rden"], 1)
                dve.wait_ge(s["rden"], t + 1)
                dve.tensor_tensor(pr[:, :, :], pr[:, :, :], over_heads(sm[:, 3, :], 4, MEM), ALU.mult).then_inc(s["probs"], 1)
                dve.wait_ge(s["pT_ps"], t + 1)
                dve.tensor_copy(pT[:, 1, :, :], c4(ps[7][:, :])).then_inc(s["pT1"], 1)
                dve.wait_ge(s["o_ps"], t + 1)
                for n in range(2):
                    hn = h[:, bass.ds(t, 1), 512 * n:512 * n + 512].rearrange("p a d -> p (a d)")
                    dve.tensor_tensor(hn, ps[4 + n][:, :], hn, ALU.add).then_inc(s["h2"], 1)
                dve.wait_ge(s["rowsT"], t + 1)
                for n in range(2):
                    dve.tensor_tensor(uT[:, 4 * n:4 * n + 4, :], c4(ps[n][:, :]), over_heads(gains[:, 2, 4 * n:4 * n + 4], 4, P),
                                      ALU.mult).then_inc(s["uTr"], 1)
                dve.wait_ge(s["lg_ps"], t + 1)
                dve.tensor_tensor(lg[:, :], ps[3][:, 0:NE], b_r[:, :], ALU.add).then_inc(s["lg"], 1)
                dve.wait_ge(s["lg"], t + 1)
                met()
                dve.max(mx[:, :], lg[:, :]).then_inc(s["mx"], 1)
                dve.wait_ge(s["mx"], t + 1)
                dve.tensor_scalar(stat[:, 8:9], mx[:, 0:1], -1.0, None, ALU.mult).then_inc(s["neg1"], 1)
                dve.max_index(ix[:, :], mx[:, :], lg[:, :]).then_inc(s["ix"], 1)
                dve.wait_ge(s["ix"], t + 1)
                dve.tensor_copy(ixf[:, :], ix[:, 0:TOPK]).then_inc(s["ixf"], 1)
                dve.wait_ge(s["ixf"], t + 1)
                dve.tensor_tensor(hot[:, :, :], repeated(iota_e[:, :], TOPK, NE), over_heads(ixf[:, :], TOPK, NE),
                                  ALU.is_equal).then_inc(s["hot"], 1)
                dve.wait_ge(s["hot"], t + 1)
                dve.tensor_reduce(mask[:, :], hot[:, :, :].rearrange("p j e -> p e j"), AX_X, ALU.add).then_inc(s["mask"], 1)
                dve.wait_ge(s["mask"], t + 1)
                dve.tensor_copy(mask_b[:, :], mask[:, :]).then_inc(s["mask_b"], 1)
                dve.wait_ge(s["ge"], t + 1)
                dve.reciprocal(stat[:, 10:11], stat[:, 9:10]).then_inc(s["rge"], 1)
                dve.wait_ge(s["rge"], t + 1)
                dve.tensor_scalar(gates[:, bass.ds(t, 1), :].rearrange("p a j -> p (a j)"), ge[:, :], stat[:, 10:11], None,
                                  ALU.mult).then_inc(s["gates"], 1)
                dve.wait_ge(s["rank_ps"], t + 1)
                dve.tensor_tensor(rank[:, :], ps[6][:, 0:NE], carry[:, :], ALU.add).then_inc(s["rank"], 1)
                dve.wait_ge(s["rank"], t + 1)
                dve.wait_ge(s["count_ps"], t + 1)
                dve.tensor_tensor(carry[:, :], ps[7][:, 0:NE], carry[:, :], ALU.add).then_inc(s["carry"], 1)
                dve.tensor_tensor(picked[:, :, :], hot[:, :, :], repeated(rank[:, :], TOPK, NE), ALU.mult).then_inc(s["picked"], 1)
                dve.wait_ge(s["picked"], t + 1)
                dve.tensor_reduce(rank4[:, :], picked[:, :, :], AX_X, ALU.add).then_inc(s["rank4"], 1)
                dve.wait_ge(s["rank4"], t + 1)
                dve.scalar_tensor_tensor(slot_f[:, :], ixf[:, :], float(REGION), rank4[:, :], ALU.mult, ALU.add).then_inc(s["slot_f"], 1)
                dve.wait_ge(s["slot_f"], t + 1)
                dve.tensor_copy(slots[:, bass.ds(t, 1), :].rearrange("p a j -> p (a j)"), slot_f[:, :]).then_inc(s["slots"], 1)
            step = [0]

            def then(ins):
                step[0] += 1
                ins.then_inc(s["plan_step"], 1)
                dve.wait_ge(s["plan_step"], step[0])

            col = lambda i: pv[:, i:i + 1]
            total, expert, first, count, nth, rem, base = (col(i) for i in range(7))
            dve.wait_ge(s["carry"], NT)
            then(dve.tensor_scalar(c_up, carry[:, :], float(PASS - 1), None, ALU.add))
            then(dve.tensor_copy(pi[:, :], c_up))
            then(dve.tensor_scalar(pi[:, :], pi[:, :], int(math.log2(PASS)), None, ALU.logical_shift_right))
            then(dve.tensor_copy(n_pass, pi[:, :]))
            then(dve.tensor_tensor_scan(n_cum, ones_e[:, :], n_pass, 0.0, ALU.mult, ALU.add))
            then(dve.tensor_scalar(before, n_cum, iota_i[:, 0:1], None, ALU.is_le))
            then(dve.tensor_reduce(expert, before, AX_X, ALU.add))
            then(dve.tensor_tensor(tmp, before, n_pass, ALU.mult))
            then(dve.tensor_reduce(first, tmp, AX_X, ALU.add))
            then(dve.tensor_scalar(expert, expert, float(NE - 1), None, ALU.min))
            then(dve.tensor_scalar(e_hot, iota_e[:, :], expert, None, ALU.is_equal))
            then(dve.tensor_tensor(tmp, e_hot, carry[:, :], ALU.mult))
            then(dve.tensor_reduce(count, tmp, AX_X, ALU.add))
            then(dve.tensor_tensor(nth, iota_i[:, :], first, ALU.subtract))
            then(dve.tensor_scalar(nth, nth, float(REGION // PASS - 1), 0.0, ALU.min, ALU.max))
            then(dve.scalar_tensor_tensor(rem, nth, -float(PASS), count, ALU.mult, ALU.add))
            then(dve.tensor_scalar(base, expert, float(REGION), None, ALU.mult))
            then(dve.scalar_tensor_tensor(base, nth, float(PASS), base, ALU.mult, ALU.add))
            dve.tensor_copy(plan[:, 0:1], expert).then_inc(s["plan"], 1)
            dve.tensor_copy(plan[:, 1:2], base).then_inc(s["plan"], 1)
            dve.tensor_scalar(plan[:, 2:3], rem, float(P), None, ALU.is_gt).then_inc(s["plan"], 1)
            dve.tensor_copy(plan[:, 3:4], n_cum[:, NE - 1:NE]).then_inc(s["plan"], 1)


def expert_stage(nc, a, plan_row, scratch):
    with ExitStack() as ctx:
        sb = lambda n, s, d=F32: ctx.enter_context(nc.sbuf_tensor(n, s, d))
        s = Signals(nc, ctx, "ex")
        w1 = sb("w1_sb", [P, FCH, KD, FW])
        w2 = sb("w2_sb", [P, FCH, GK, D])
        ident = sb("ident3", [P, P])
        g_ffn = sb("g_ffn_sb", [P, KD])
        bias3 = sb("bias3", [3, FF2 + D], BF16)
        ones3 = sb("ones3", [3, P], BF16)
        idx = sb("row_index", [P, 2, 2], I32)
        out_idx = sb("out_index", [P, 2, 2], I32)
        spare = sb("spare3", [P, 2])
        got = sb("gathered", [P, 2, D])
        uT = sb("uT3", [P, 2, KD, P])
        glu = sb("glu", [P, 2, FW // 2])
        sig = sb("sig", [P, 2, FW // 2])
        lin = sb("lin", [P, 2, FW // 2])
        actT = sb("actT", [P, 2, GK, P])
        y = sb("y_rows", [P, 2, D])

        ps_h = [ctx.enter_context(nc.psum_tensor(f"ex_h{b}", [P, FW], F32)) for b in range(2)]
        ps_g = ctx.enter_context(nc.psum_tensor("ex_g", [P, 2, GK, P], F32))
        ps_u = ctx.enter_context(nc.psum_tensor("ex_u", [P, 4, P], F32))
        ps_y = [[ctx.enter_context(nc.psum_tensor(f"ex_y{b}{n}", [P, 512], F32)) for n in range(2)] for b in range(2)]
        block = ctx.enter_context(nc.Block())

        w1_v = a["w1"][0].rearrange("e (k p) f -> e p k f", p=P)
        w2_v = a["w2"][0].rearrange("e (c k p) d -> e p c k d", k=GK, p=P)

        def passes(eng):
            return eng.value_load(plan_row[0:1, 3:4], min_val=1, max_val=MAX_PASSES)

        def slots_at(first_slot):
            return scratch["slot_table"][bass.ds(first_slot, PASS), :].rearrange("(b p) a -> p b a", p=P)

        def plan_of(eng, i, what, most):
            return eng.value_load(plan_row[0:1, bass.ds(i * 4 + what, 1)], min_val=0, max_val=most)

        @block.sync
        def _(sp):
            sp.dma_start(ident[:, :], a["c_ident"]).then_inc(s["consts"], 16)
            with nc.allow_non_contiguous_dma("gains on partitions"):
                sp.dma_start(g_ffn[:, :], a["g_ffn"].rearrange("a (k p) -> p (a k)", p=P)).then_inc(s["consts"], 16)
            n = passes(sp)
            with sp.Fori(0, n) as i:
                e = plan_of(sp, i, 0, NE - 1)
                for c in range(FCH):
                    if c == FCH - 1:
                        sp.wait_ge(s["bias_used"], i)
                        sp.dma_start(bias3[:, :], scratch["bias_parts"][bass.ds(e, 1), :, :].rearrange("a j n -> (a j) n")).then_inc(s["bias3"], 16)
                    sp.wait_ge(s[f"done_{c}"] if c < FCH - 1 else s["bias_used"], i)
                    sp.dma_start(w1[:, c, :, :], w1_v[bass.ds(e, 1), :, :, FW * c:FW * c + FW].rearrange("a p k f -> (a p) k f")).then_inc(s[f"w1_{c}"], 16)
                    sp.dma_start(w2[:, c, :, :], w2_v[bass.ds(e, 1), :, c, :, :].rearrange("a p k d -> (a p) k d")).then_inc(s[f"w2_{c}"], 16)

        @block.gpsimd
        def _(pool):
            pool.memset(ones3[:, :], 1.0).then_inc(s["ones3"], 1)
            def met():
                pool.tensor_tensor(spare[:, 0:1], spare[:, 1:2], spare[:, 1:2], ALU.add).then_inc(s["met"], 1)

            pool.memset(spare[:, :], 0.0).then_inc(s["ones3"], 1)
            pool.wait_ge(s["ones3"], 2)
            n = passes(pool)
            def gather(i, mets):
                first_slot = plan_of(pool, i, 1, NE * REGION - PASS)
                pool.wait_ge(s["uT_ps"], 4 * i)
                with nc.allow_non_contiguous_dma("256 row numbers"):
                    pool.dma_start(idx[:, :, :], slots_at(first_slot)).then_inc(s["idx"], 16)
                if mets is not None:
                    pool.wait_ge(s["met"], mets)
                pool.wait_ge(s["idx"], 16 * i + 16)
                met()
                for b in range(2):
                    pool.indirect_dma_start(got[:, b, :], None, scratch["rows"],
                                            bass.IndirectOffsetOnAxis(ap=idx[:, b, 0:1], axis=0)).then_inc(s["got"], 16)

            pool.memset(y[:, :, :], 0.0).then_inc(s["ones3"], 1)
            gather(0, None)
            with pool.Fori(0, n) as i:
                gather(i + 1, 2 * i + 1)
                first_slot = plan_of(pool, i, 1, NE * REGION - PASS)
                pool.wait_ge(s["stored"], 32 * i)
                with nc.allow_non_contiguous_dma("256 row numbers"):
                    pool.dma_start(out_idx[:, :, :], slots_at(first_slot)).then_inc(s["out_idx"], 16)
                pool.wait_ge(s["met"], 2 * i + 2)
                pool.wait_ge(s["out_idx"], 16 * i + 16)
                pool.wait_ge(s["y_left"], 2 * i + 2)
                met()
                for b in range(2):
                    pool.indirect_dma_start(scratch["y"], bass.IndirectOffsetOnAxis(ap=out_idx[:, b, 1:2], axis=0), y[:, b, :], None,
                                            bounds_check=SEQ * TOPK - 1, oob_is_err=False).then_inc(s["stored"], 16)
            pool.wait_ge(s["stored"], 32 * n)

        @block.tensor
        def _(pe):
            def row_transposes(i, r):
                if r == 0:
                    pe.wait_ge(s["got"], 32 * i + 32)
                pe.wait_ge(s["uT"], 4 * i + r)
                for k in range(4):
                    m = pe.transpose(ps_u[:, k, :], got[:, r // 2, P * (4 * (r % 2) + k):P * (4 * (r % 2) + k) + P], ident[:, :])
                m.then_inc(s["uT_ps"], 1)

            def hidden(i, c, nb):
                pe.wait_ge(s[f"w1_{c}"], 16 * i + 16)
                if c == 0:
                    pe.wait_ge(s["uT"], 4 * i + 4)
                    pe.wait_ge(s["bias3"], 16 * i + 16)
                for b in range(nb):
                    for k in range(KD):
                        pe.matmul(ps_h[b][:, :], uT[:, b, k, :], w1[:, c, k, :], start=k == 0, stop=False)
                    m = pe.matmul(ps_h[b][:, :], ones3[:, :], bias3[:, FW * c:FW * c + FW], start=False, stop=True)
                    m.then_inc(s["h"], 1 if nb == 2 else 2)

            def out(i, c, b, n, last):
                for k in range(GK):
                    m = pe.matmul(ps_y[b][n][:, :], actT[:, b, k, :], w2[:, c, k, 512 * n:512 * n + 512],
                                  start=c == 0 and k == 0, stop=False)
                if c == FCH - 1:
                    m = pe.matmul(ps_y[b][n][:, :], ones3[:, :], bias3[:, FF2 + 512 * n:FF2 + 512 * n + 512], start=False, stop=True)
                    if last:
                        m.then_inc(s["bias_used"], 1)
                elif last:
                    m.then_inc(s[f"done_{c}"], 1)

            def step_out(i, c, nb, between=None):
                pe.wait_ge(s["actT"], 4 * i + c + 1)
                pe.wait_ge(s[f"w2_{c}"], 16 * i + 16)
                if c == 0:
                    pe.wait_ge(s["y_left"], 2 * i)
                for n in range(2):
                    for b in range(nb):
                        out(i, c, b, n, last=(n, b) == (1, nb - 1))
                    if n == 0 and between:
                        between()

            def body(i, nb):
                for c in range(FCH):
                    hidden(i, c, nb)
                    if c == FCH - 1:
                        row_transposes(i + 1, 0)
                    if c:
                        step_out(i, c - 1, nb)
                    if c == FCH - 1:
                        row_transposes(i + 1, 1)
                    pe.wait_ge(s["act"], 8 * i + 2 * c + 2)
                    for b in range(nb):
                        for k in range(GK):
                            m = pe.transpose(ps_g[:, b, k, :], lin[:, b, P * k:P * k + P], ident[:, :])
                    m.then_inc(s["gT"], 1)
                row_transposes(i + 1, 2)
                step_out(i, FCH - 1, nb, lambda: row_transposes(i + 1, 3))

            pe.wait_ge(s["consts"], 32)
            pe.wait_ge(s["ones3"], 2)
            for r in range(4):
                row_transposes(0, r)
            n = passes(pe)
            with pe.Fori(0, n) as i:
                two = plan_of(pe, i, 2, 1)
                with pe.If(two > 0):
                    body(i, 2)
                with pe.Else():
                    body(i, 1)

        @block.scalar
        def _(act):
            def body(i, nb):
                for c in range(FCH):
                    for b in range(nb):
                        act.wait_ge(s["glu"], 8 * i + 2 * c + (b + 1 if nb == 2 else 2))
                        act.activation(sig[:, b, :], glu[:, b, :], ACT.Sigmoid, scale=ALPHA).then_inc(s["sig"], 1 if nb == 2 else 2)
                    act.wait_ge(s["gT"], 4 * i + c + 1)
                    act.activation(actT[:, 0:nb, :, :].rearrange("p b k n -> p (b k n)"),
                                   ps_g[:, 0:nb, :, :].rearrange("p b k n -> p (b k n)"), ACT.Copy).then_inc(s["actT"], 1)
                act.wait_ge(s["bias_used"], i + 1)
                act.wait_ge(s["stored"], 32 * i)
                for b in range(nb):
                    m = act.activation(y[:, b, 0:512], ps_y[b][0][:, :], ACT.Copy)
                m.then_inc(s["y_left"], 1)

            act.wait_ge(s["ones3"], 3)
            n = passes(act)
            with act.Fori(0, n) as i:
                two = plan_of(act, i, 2, 1)
                with act.If(two > 0):
                    body(i, 2)
                with act.Else():
                    body(i, 1)

        @block.vector
        def _(dve):
            def rows_out(i, r):
                dve.wait_ge(s["uT_ps"], 4 * i + r + 1)
                k = 4 * (r % 2)
                dve.tensor_tensor(uT[:, r // 2, k:k + 4, :], ps_u[:, :, :], over_heads(g_ffn[:, k:k + 4], 4, P),
                                  ALU.mult).then_inc(s["uT"], 1)

            def body(i, nb):
                inc = 1 if nb == 2 else 2
                for c in range(FCH):
                    for b in range(nb):
                        at = 8 * i + 2 * c + (b + 1 if nb == 2 else 2)
                        dve.wait_ge(s["h"], at)
                        dve.tensor_scalar(glu[:, b, :], ps_h[b][:, 0::2], LIMIT, None, ALU.min).then_inc(s["glu"], inc)
                        dve.tensor_scalar(lin[:, b, :], ps_h[b][:, 1::2], LIMIT, -LIMIT, ALU.min, ALU.max).then_inc(s["lin"], inc)
                        dve.wait_ge(s["lin"], at)
                        dve.scalar_tensor_tensor(lin[:, b, :], lin[:, b, :], 1.0, glu[:, b, :], ALU.add, ALU.mult).then_inc(s["lin_glu"], inc)
                        dve.wait_ge(s["lin_glu"], at)
                        dve.wait_ge(s["sig"], at)
                        dve.tensor_tensor(lin[:, b, :], lin[:, b, :], sig[:, b, :], ALU.mult).then_inc(s["act"], inc)
                for r in range(4):
                    rows_out(i + 1, r)
                dve.wait_ge(s["bias_used"], i + 1)
                dve.wait_ge(s["stored"], 32 * i)
                for b in range(nb):
                    m = dve.tensor_copy(y[:, b, 512:D], ps_y[b][1][:, :])
                m.then_inc(s["y_left"], 1)

            dve.wait_ge(s["consts"], 32)
            dve.wait_ge(s["ones3"], 3)
            for r in range(4):
                rows_out(0, r)
            n = passes(dve)
            with dve.Fori(0, n) as i:
                two = plan_of(dve, i, 2, 1)
                with dve.If(two > 0):
                    body(i, 2)
                with dve.Else():
                    body(i, 1)


def combine_stage(nc, a, h, gates, scratch, out):
    with ExitStack() as ctx:
        sb = lambda n, s, d=F32: ctx.enter_context(nc.sbuf_tensor(n, s, d))
        s = Signals(nc, ctx, "cb")
        got = [sb(f"expert_rows{i}", [P, TOPK, D]) for i in range(3)]
        junk = sb("junk", [P, D])
        res = [sb(f"result{i}", [P, D]) for i in range(2)]
        g_fin = sb("g_final_sb", [P, D])
        stat = sb("stat4", [P, 2 * NT])
        norm_c = sb("norm_c4", [P, 2, 2])
        block = ctx.enter_context(nc.Block())

        @block.gpsimd
        def _(pool):
            pool.memset(norm_c[:, 0, :], EPS).then_inc(s["norm_c"], 1)
            pool.memset(norm_c[:, 1, :], -0.5).then_inc(s["norm_c"], 1)
            pool.wait_ge(s["norm_c"], 2)

            for t in range(NT):
                pool.wait_ge(s["ss"], t + 1)
                rstd_of(pool, norm_c, stat[:, 2 * t + 1:2 * t + 2], stat[:, 2 * t:2 * t + 1], 1, s["rstd_ms"], s["rstd"], t + 1)

        @block.vector
        def _(dve):
            for t in range(NT):
                dve.wait_ge(s[f"got{t % 3}"], 16 * (t // 3 + 1))
                for j in range(TOPK):
                    if j:
                        dve.wait_ge(s["summed"], TOPK * t + j)
                    dve.scalar_tensor_tensor(h[:, t, :], got[t % 3][:, j, :], gates[:, t, j:j + 1], h[:, t, :],
                                             ALU.mult, ALU.add).then_inc(s["summed"], 1)
                dve.wait_ge(s["rstd"], t + 1)
                dve.wait_ge(s["g_fin"], 16)
                if t >= 2:
                    dve.wait_ge(s[f"stored{t % 2}"], 16 * (t // 2))
                dve.scalar_tensor_tensor(res[t % 2][:, :], h[:, t, :], stat[:, 2 * t + 1:2 * t + 2], g_fin[:, :],
                                         ALU.mult, ALU.mult).then_inc(s["result"], 1)

        @block.scalar
        def _(act):
            for t in range(NT):
                act.wait_ge(s["summed"], TOPK * t + TOPK)
                act.activation(junk[:, :], h[:, t, :], ACT.Square, scale=1 / 32, accum_out=stat[:, 2 * t:2 * t + 1]).then_inc(s["ss"], 1)

        @block.sync
        def _(sp):
            sp.dma_start(g_fin[:, :], a["g_final"].partition_broadcast(P)).then_inc(s["g_fin"], 16)


            def load(t):
                sp.dma_start(got[t % 3][:, :, :], scratch["y"][TOPK * P * t:TOPK * P * (t + 1), :].rearrange(
                    "(p j) d -> p j d", j=TOPK)).then_inc(s[f"got{t % 3}"], 16)

            for t in range(3):
                load(t)
            for t in range(NT):
                if t + 3 < NT:
                    sp.wait_ge(s["summed"], TOPK * (t + 1))
                    load(t + 3)
                sp.wait_ge(s["result"], t + 1)
                sp.dma_start(out[0, P * t:P * t + P, :], res[t % 2][:, :]).then_inc(s[f"stored{t % 2}"], 16)
            for i in range(2):
                sp.wait_ge(s[f"stored{i}"], 16 * NT // 2)


def build_program(nc, a, out):
    with ExitStack() as ctx:
        sb = lambda n, s, d=F32: ctx.enter_context(nc.sbuf_tensor(n, s, d))
        h = sb("h_rows", [P, NT, D])
        gates = sb("gates", [P, NT, TOPK])
        plan_row = sb("plan_row", [1, 4 * (MAX_PASSES + 1)], I32)
        dram = lambda n, s, d=F32: nc.dram_tensor(n, s, d).ap()
        scratch = {
            "bias_rows": dram("bias_rows_dram", [8, P, 3 * P]),
            "rows": dram("moe_rows_dram", [SEQ, D]),
            "slot_table": dram("slot_table_dram", [NE * REGION, 2], I32),
            "plan": dram("plan_dram", [MAX_PASSES + 1, 4], I32),
            "bias_parts": dram("bias_parts_dram", [NE, 3, FF2 + D], BF16),
            "y": dram("expert_y_dram", [SEQ * TOPK, D]),
        }
        mixer_stage(nc, a, h, scratch)
        cross_stage(nc, a, h, gates, plan_row, scratch)
        expert_stage(nc, a, plan_row, scratch)
        combine_stage(nc, a, h, gates, scratch, out)


def shape_constants():
    dist = np.arange(P - 1, -1, -1)
    exact = BUCKETS // 2
    ratio = np.maximum(dist, exact).astype(np.float32) / exact
    large = exact + (np.log(ratio) / math.log(MAX_DIST / exact) * (BUCKETS - exact)).astype(np.int32)
    bucket = np.where(dist < exact, dist, np.minimum(large, BUCKETS - 1))
    return {
        "c_ident": np.eye(P, dtype=np.float32),
        "c_upper": np.triu(np.ones((P, P), np.float32)),
        "c_bucket": (np.arange(BUCKETS)[:, None] == bucket[None, :]).astype(np.float32),
    }


_INS = ["x", "mem", "g_mix", "w_in", "b_qkv", "conv_w", "conv_b", "dt_bias", "a_log", "d_skip", "g_ssm_out",
        "attn_sinks", "rel_bias", "w_out", "b_out", "g_cross", "g_mem", "w_q_cross", "w_kv_cross", "w_o_cross",
        "g_ffn", "w_router", "b_router", "w1", "b1", "w2", "b2", "g_final"]


def kernel(**inputs):
    import concourse.bacc as bacc
    from concourse.bass_utils import run_bass_kernel_spmd

    nc = bacc.Bacc("TRN2", target_bir_lowering=False, num_devices=1)
    arrays, aps = {}, {}
    given = {n: np.ascontiguousarray(inputs[n]) for n in _INS} | shape_constants()
    for name, v in given.items():
        arrays[f"in_{name}"] = v
        aps[name] = nc.dram_tensor(f"in_{name}", v.shape, mybir.dt.from_np(v.dtype), kind="ExternalInput").ap()
    out = nc.dram_tensor("out_rows", (1, SEQ, D), F32, kind="ExternalOutput").ap()
    build_program(nc, aps, out)
    r = run_bass_kernel_spmd(nc, [arrays], core_ids=[0])
    return r.results[0]["out_rows"]
```

```python
from contextlib import ExitStack
import math

import numpy as np
import concourse.bass as bass
from concourse import mybir

F32 = mybir.dt.float32
F32R = mybir.dt.float32r
BF16 = mybir.dt.bfloat16
I32 = mybir.dt.int32
U32 = mybir.dt.uint32
ALU = mybir.AluOpType
ACT = mybir.ActivationFunctionType
AX_X = mybir.AxisListType.X

P = 128
D = 1024
SEQ = 1024
NT = SEQ // P
KD = D // P
MEM = 256
EPS = 1e-5
NEG = -1e30

SH, SP_, SW = 8, 64, 512
CH = 1024
CW = 4
NC_ = CH // P
HD = 64
COL_XBC, COL_DT, COL_Q, COL_K, COL_V = 512, 1536, 1544, 2056, 2184
IN_COLS = 2312
BUCKETS, MAX_DIST = 32, 128

XH, XD = 4, 128
NE, TOPK = 32, 4
FF2 = 2048
ALPHA, LIMIT = 1.702, 7.0
PASS = 256
REGION = 1024
MAX_PASSES = NE + SEQ * TOPK // PASS
FCH = 4
FW = FF2 // FCH
GK = FW // 2 // P


B2_AT = 32
RING = 4


class Signals:

    def __init__(self, nc, ctx, stage):
        self.nc, self.stage, self.made = nc, stage, {}
        ctx.callback(self.give_back)

    def give_back(self):
        self.nc.clear_and_free_semaphores(list(self.made.values()))
        self.nc.all_engine_barrier()

    def __getitem__(self, name):
        if name not in self.made:
            self.made[name] = self.nc.alloc_semaphore(f"{self.stage}_{name}")
        return self.made[name]


def is_first(i):
    return isinstance(i, int) and i == 0


def each_tile(eng, a_tile):
    a_tile(0)
    with eng.Fori(1, NT) as t:
        a_tile(t)


def over_heads(ap, n, width):
    return ap.unsqueeze(2).to_broadcast([P, n, width])


def repeated(ap, n, width):
    return ap.unsqueeze(1).to_broadcast([P, n, width])


def row_bcast(ap, n):
    return ap.partition_broadcast(P)


def rstd_of(pool, consts, out, mean_square, n, step, done, at):
    pool.tensor_tensor(out, mean_square, consts[:, 0, 0:n], ALU.add).then_inc(step, 1)
    pool.wait_ge(step, at)
    pool.tensor_tensor(out, out, consts[:, 1, 0:n], ALU.pow).then_inc(done, 1)


def mixer_stage(nc, a, h, scratch):
    with ExitStack() as ctx:
        sb = lambda n, s, d=F32: ctx.enter_context(nc.sbuf_tensor(n, s, d))
        s = Signals(nc, ctx, "mx")

        w_in = sb("w_in_sb", [P, KD, IN_COLS])
        w_out = sb("w_out_sb", [P, KD, D])
        ident = sb("ident", [P, P])
        upper = sb("upper", [P, P])
        ones = sb("ones", [P, P])
        ident_b = sb("ident_b", [P, P], BF16)
        negmask_b = sb("negmask_b", [P, 4, P], BF16)
        bucket_hot = sb("bucket_hot", [BUCKETS, P])
        rel_bias = sb("rel_bias_sb", [BUCKETS, 8])
        bias_rows = sb("bias_rows", [8, 3 * P])
        bias = sb("win_bias", [P, 8, 2 * P])
        g_mix = sb("g_mix_sb", [P, KD])
        conv_w = sb("conv_w_sb", [P, CW, NC_])
        conv_b = sb("conv_b_sb", [P, NC_])
        g_ssm = sb("g_ssm_sb", [P, 4])
        b_qkv = sb("b_qkv_sb", [P, 768])
        b_out = sb("b_out_sb", [P, D])
        small = sb("head_rows", [P, 4, 8])
        dt_bias, a_head, d_skip, sinks = (small[:, i, :] for i in range(4))

        row = sb("row", [P, D])
        uT = sb("uT", [P, KD, P])
        zg = sb("zg", [P, SW])
        ext = sb("conv_in", [P, NC_, P + CW - 1])
        cv = sb("conv_out", [P, NC_, P])
        xs = sb("xs_tok", [P, SW])
        bt = sb("b_tok", [P, 2 * P])
        xdt = sb("xdt", [P, SW])
        xw = sb("x_to_end", [P, SW])
        decay = sb("decay", [P, SH, P])
        state = sb("state", [P, SW])
        y = sb("y", [P, SW])
        y2 = sb("y2", [P, SW])
        d8 = sb("dt_steps", [P, 14, 8])
        (draw, nabs, ex, w1p, rest, rw, lnw, dt, av, acs, nacs, ea, te, cd) = (d8[:, i, :] for i in range(14))
        stat = sb("stat", [P, 8])
        norm_c = sb("norm_c", [P, 2, 2])
        spare = sb("spare", [P, 2])
        q_tok = sb("q_tok", [P, 4, 2, HD])
        k_tok = sb("k_tok", [P, P])
        qT = sb("qT", [P, 4, P])
        kT = sb("kT", [P, 2, P])
        v = sb("v_tok", [P, 2, P])
        sc = sb("scores", [P, 4, 2 * P])
        pT = sb("probs_t", [P, 2, 4, P])
        sm = sb("softmax", [P, 6, 8])
        prevmask = sb("prevmask", [P, 1])
        catT = pT[:, :, :, :].rearrange("p a c n -> p (a c) n")

        ps = [ctx.enter_context(nc.psum_tensor(f"mx_b{i}", [P, 512], F32)) for i in range(8)]
        block = ctx.enter_context(nc.Block())

        w_in_d = a["w_in"].rearrange("a (k p) n -> p (a k) n", p=P)
        w_out_d = a["w_out"][0]

        @block.sync
        def _(sp):
            sp.dma_start(h[:, 0, :], a["x"][0, 0:P, :]).then_inc(s["x0"], 16)
            sp.dma_start(ident[:, :], a["c_ident"]).then_inc(s["consts"], 16)
            sp.dma_start(upper[:, :], a["c_upper"]).then_inc(s["consts"], 16)
            sp.dma_start(bucket_hot[:, :], a["c_bucket"]).then_inc(s["consts"], 16)
            sp.dma_start(rel_bias[:, :], a["rel_bias"]).then_inc(s["consts"], 16)
            sp.dma_start(w_in[:, :, COL_XBC:IN_COLS], w_in_d[:, :, COL_XBC:IN_COLS]).then_inc(s["w_in"], 16)
            sp.dma_start(w_in[:, :, 0:COL_XBC], w_in_d[:, :, 0:COL_XBC]).then_inc(s["w_in"], 16)
            sp.dma_start(h[:, 1:NT, :], a["x"][0, P:SEQ, :].rearrange("(t p) d -> p t d", p=P)).then_inc(s["x"], 16)
            sp.dma_start(w_out[:, 0:4, :], w_out_d[0:SW, :].rearrange("(k p) n -> p k n", p=P)).then_inc(s["w_out"], 16)
            for g in range(2):
                rows = w_out_d[SW + 256 * g:SW + 256 * (g + 1), :]
                sp.dma_start(w_out[64 * g:64 * g + 64, 4:8, :],
                             rows.rearrange("(j d) n -> d j n", d=HD)).then_inc(s["w_out"], 16)

        @block.gpsimd
        def _(pool):
            pool.memset(kT[:, :, :], 0.0).then_inc(s["cleared"], 1)
            pool.memset(v[:, :, :], 0.0).then_inc(s["cleared"], 1)
            pool.memset(ext[:, :, :], 0.0).then_inc(s["cleared"], 1)
            pool.memset(state[:, :], 0.0).then_inc(s["cleared"], 1)
            pool.memset(ones[:, :], 1.0).then_inc(s["cleared"], 1)
            pool.memset(prevmask[:, :], NEG).then_inc(s["cleared"], 1)
            pool.memset(bias_rows[:, :], NEG).then_inc(s["cleared"], 1)
            pool.memset(norm_c[:, 0, :], EPS).then_inc(s["cleared"], 1)
            pool.memset(norm_c[:, 1, :], -0.5).then_inc(s["cleared"], 1)
            pool.wait_ge(s["cleared"], 9)
            def met():
                pool.tensor_tensor(spare[:, 1:2], norm_c[:, 0, 0:1], norm_c[:, 0, 0:1], ALU.add)

            def a_tile(t):
                pool.wait_ge(s["ss"], t + 1)
                rstd_of(pool, norm_c, stat[:, 1:2], stat[:, 0:1], 1, s["rstd_ms"], s["rstd"], t + 1)
                pool.wait_ge(s["xn"], t + 1)
                pool.wait_ge(s["x"], 16)
                pool.wait_ge(s["rows_in"], 96)
                ht = h[:, bass.ds(t, 1), :].rearrange("p a d -> p (a d)")
                pool.tensor_tensor(ht, ht, b_out[:, :], ALU.add).then_inc(s["resid"], 1)
                pool.wait_ge(s["av"], t + 1)
                pool.tensor_tensor(decay[:, :, :], over_heads(av, 8, P), repeated(upper[:, :], 8, P),
                                   ALU.mult).then_inc(s["au"], 1)
                pool.wait_ge(s["xdt"], t + 1)
                pool.wait_ge(s["te"], t + 1)
                pool.tensor_tensor(xw[:, :].rearrange("p (h d) -> p h d", h=SH),
                                   xdt[:, :].rearrange("p (h d) -> p h d", h=SH),
                                   over_heads(te, 8, SP_), ALU.mult).then_inc(s["xw"], 1)
                pool.wait_ge(s["oT1"], t + 1)
                met()
                pool.tensor_copy(kT[:, 0, :], kT[:, 1, :]).then_inc(s["shift"], 1)
                pool.tensor_copy(v[:, 0, :], v[:, 1, :]).then_inc(s["shift"], 1)
                pool.memset(prevmask[:, :], 0.0).then_inc(s["shift"], 1)
                pool.wait_ge(s["ssg"], 2 * t + 2)
                rstd_of(pool, norm_c, stat[:, 4:6], stat[:, 2:4], 2, s["rstd_g_ms"], s["rstd_g"], t + 1)
            each_tile(pool, a_tile)

        @block.scalar
        def _(act):
            def small_row(dst, src):
                act.dma_start(dst, src).then_inc(s["rows_in"], 16)
            with nc.allow_non_contiguous_dma("gains on partitions"):
                act.dma_start(g_mix[:, :], a["g_mix"].rearrange("a (k p) -> p (a k)", p=P)).then_inc(s["cols_in"], 16)
                act.dma_start(conv_b[:, :], a["conv_b"].rearrange("a (k p) -> p (a k)", p=P)).then_inc(s["cols_in"], 16)
                act.dma_start(g_ssm[:, :], a["g_ssm_out"].rearrange("a (k p) -> p (a k)", p=P)).then_inc(s["cols_in"], 16)
                for j in range(CW):
                    act.dma_start(conv_w[:, j, :], a["conv_w"][0, j, :].rearrange("(k p) -> p k", p=P)).then_inc(s["cols_in"], 16)
            small_row(b_qkv[:, :], a["b_qkv"][0, :].partition_broadcast(P))
            small_row(b_out[:, :], a["b_out"][0, :].partition_broadcast(P))
            for i, n in enumerate(["dt_bias", "a_log", "d_skip", "attn_sinks"]):
                small_row(small[:, i, :], a[n][0, :].partition_broadcast(P))
            act.wait_ge(s["bias_rows"], 1)
            act.dma_start(scratch["bias_rows"], bias_rows[:, :].unsqueeze(1).to_broadcast([8, P, 3 * P])).then_inc(s["bias_out"], 16)
            act.wait_ge(s["bias_out"], 16)
            src = scratch["bias_rows"]
            act.dma_start(bias[:, :, :], bass.AP(src.tensor, P - 1, [[3 * P - 1, P], [3 * P * P, 8], [1, 2 * P]])).then_inc(s["bias"], 16)
            act.wait_ge(s["rows_in"], 96)
            act.activation(a_head, a_head, ACT.Exp).then_inc(s["a_exp"], 1)
            act.wait_ge(s["x0"], 16)
            act.wait_ge(s["cols_in"], 16 * 7)
            act.wait_ge(s["consts"], 64)
            act.wait_ge(s["x"], 16)
            def met():
                act.activation(spare[:, 0:1], ident[:, 0:1], ACT.Copy)

            def a_tile(t):
                ht = h[:, bass.ds(t, 1), :].rearrange("p a d -> p (a d)")
                if not is_first(t):
                    act.wait_ge(s["xbcT"], t)
                met()
                act.activation(row[:, :], ht, ACT.Square, scale=1 / 32, accum_out=stat[:, 0:1]).then_inc(s["ss"], 1)
                act.wait_ge(s["rstd"], t + 1)
                met()
                act.activation(row[:, :], ht, ACT.Copy, scale=stat[:, 1:2]).then_inc(s["xn"], 1)
                act.wait_ge(s["p_xbc"], t + 1)
                act.activation(row[:, 0:512], ps[2][:, :], ACT.Copy).then_inc(s["xbc0"], 1)
                act.wait_ge(s["p_z"], t + 1)
                act.activation(zg[:, :], ps[6][:, :], ACT.Silu).then_inc(s["zg"], 1)
                act.wait_ge(s["xbcT"], t + 1)
                if not is_first(t):
                    act.wait_ge(s["conv"], t)
                act.activation(ext[:, 0:4, CW - 1:], ps[0][:, :].rearrange("p (c n) -> p c n", c=4), ACT.Copy).then_inc(s["ext0"], 1)
                act.wait_ge(s["qkT_ps"], t + 1)
                act.activation(qT[:, :, :], ps[7][:, :].rearrange("p (c n) -> p c n", c=4), ACT.Copy).then_inc(s["qT"], 1)
                act.wait_ge(s["nabs"], t + 1)
                act.activation(ex, nabs, ACT.Exp, scale=-1.0).then_inc(s["ex"], 1)
                act.wait_ge(s["w1p"], t + 1)
                act.activation(lnw, w1p, ACT.Ln).then_inc(s["lnw"], 1)
                for g in range(2):
                    if g == 1:
                        act.wait_ge(s["acsB"], t + 1)
                        act.wait_ge(s["te_in"], t + 1)
                        act.activation(ea, acs, ACT.Exp).then_inc(s["ea"], 1)
                        act.activation(te, te, ACT.Exp).then_inc(s["te"], 1)
                        act.activation(cd, cd, ACT.Exp).then_inc(s["cd"], 1)
                        for hh in range(8):
                            act.activation(decay[:, hh, :], ps[2 + hh // 4][:, P * (hh % 4):P * (hh % 4) + P], ACT.Exp,
                                           bias=nacs[:, hh:hh + 1]).then_inc(s["decay"], 1)
                    act.wait_ge(s["negm"], 2 * t + g + 1)
                    for j in range(4):
                        act.activation(sc[:, j, :], sc[:, j, :], ACT.Exp, bias=sm[:, 1, 4 * g + j:4 * g + j + 1],
                                       accum_out=sm[:, 2, 4 * g + j:4 * g + j + 1]).then_inc(s["pexp"], 1)
                    act.activation(sm[:, 3, 4 * g:4 * g + 4], sm[:, 5, 4 * g:4 * g + 4], ACT.Exp).then_inc(s["sinkexp"], 1)
                    act.wait_ge(s["pT_ps"], 2 * t + g + 1)
                    act.activation(pT[:, 0, :, :], ps[6][:, :].rearrange("p (c n) -> p c n", c=4), ACT.Copy).then_inc(s["pT0"], 1)
                act.wait_ge(s["conv"], t + 1)
                for c in range(NC_):
                    act.activation(cv[:, c, :], cv[:, c, :], ACT.Silu, bias=conv_b[:, c:c + 1]).then_inc(s["cv"], 1)
                act.wait_ge(s["xsbT"], t + 1)
                act.activation(xs[:, :], ps[0][:, :], ACT.Copy).then_inc(s["xs"], 1)
                act.activation(bt[:, :], ps[1][:, 0:256], ACT.Copy).then_inc(s["bt"], 1)
                act.wait_ge(s["oT1"], t + 1)
                act.activation(catT[:, 4:8, :], ps[5][:, :].rearrange("p (c n) -> p c n", c=4), ACT.Copy).then_inc(s["cat1"], 1)
                act.wait_ge(s["yg"], t + 1)
                for g in range(2):
                    act.activation(y2[:, 256 * g:256 * g + 256], y[:, 256 * g:256 * g + 256], ACT.Square, scale=1 / 16,
                                   accum_out=stat[:, 2 + g:3 + g]).then_inc(s["ssg"], 1)
            each_tile(act, a_tile)

        @block.tensor
        def _(pe):
            pe.wait_ge(s["consts"], 64)
            pe.matmul(ps[0][0:8, 0:P], rel_bias[:, :], bucket_hot[:, :], start=True, stop=True).then_inc(s["bias_ps"], 1)
            pe.wait_ge(s["bias_rows"], 1)
            pe.wait_ge(s["cleared"], 9)
            pe.wait_ge(s["masks"], 2)
            def a_tile(t):
                pe.wait_ge(s["xn"], t + 1)
                if not is_first(t):
                    pe.wait_ge(s["state"], t)
                for k in range(KD):
                    m = pe.transpose(ps[k // 4][:, P * (k % 4):P * (k % 4) + P], row[:, P * k:P * k + P], ident[:, :])
                m.then_inc(s["xnT"], 1)
                pe.wait_ge(s["uT"], 2 * t + 2)
                pe.wait_ge(s["w_in"], 32)
                for n in range(2):
                    for k in range(KD):
                        m = pe.matmul(ps[2 + n][:, :], uT[:, k, :], w_in[:, k, COL_XBC + 512 * n:COL_XBC + 512 * n + 512],
                                      start=k == 0, stop=k == KD - 1)
                m.then_inc(s["p_xbc"], 1)
                for k in range(KD):
                    pe.matmul(ps[4][:, 0:8], uT[:, k, :], w_in[:, k, COL_DT:COL_Q], start=k == 0, stop=k == KD - 1)
                for k in range(KD):
                    m = pe.matmul(ps[4][:, 8:264], uT[:, k, :], w_in[:, k, COL_K:IN_COLS], start=k == 0, stop=k == KD - 1)
                m.then_inc(s["p_kv"], 1)
                if not is_first(t):
                    pe.wait_ge(s["cat1"], t)
                for k in range(KD):
                    m = pe.matmul(ps[5][:, :], uT[:, k, :], w_in[:, k, COL_Q:COL_K], start=k == 0, stop=k == KD - 1)
                m.then_inc(s["p_q"], 1)
                if not is_first(t):
                    pe.wait_ge(s["h1"], 2 * t)
                for k in range(KD):
                    m = pe.matmul(ps[6][:, :], uT[:, k, :], w_in[:, k, 0:COL_XBC], start=k == 0, stop=k == KD - 1)
                m.then_inc(s["p_z"], 1)
                pe.wait_ge(s["xbc0"], t + 1)
                pe.wait_ge(s["xbc1"], t + 1)
                for k in range(NC_):
                    m = pe.transpose(ps[k // 4][:, P * (k % 4):P * (k % 4) + P], row[:, P * k:P * k + P], ident[:, :])
                m.then_inc(s["xbcT"], 1)
                pe.wait_ge(s["q_tok"], t + 1)
                for j in range(4):
                    pe.transpose(ps[7][:, P * j:P * j + P], q_tok[:, j, :, :].rearrange("p g d -> p (g d)"), ident[:, :])
                m = pe.transpose(ps[2][:, 0:P], k_tok[:, :], ident[:, :])
                m.then_inc(s["qkT_ps"], 1)
                pe.wait_ge(s["qT"], t + 1)
                pe.wait_ge(s["kT"], t + 1)
                pe.wait_ge(s["zg"], t + 1)
                for g in range(2):
                    if g == 1:
                        pe.wait_ge(s["pT1"], 2 * t + 1)
                    for j in range(4):
                        m = pe.matmul(ps[6 + j // 2][:, 256 * (j % 2):256 * (j % 2) + 256], qT[64 * g:64 * g + 64, j, :],
                                      kT[64 * g:64 * g + 64, :, :].rearrange("p a n -> p (a n)"), start=True, stop=True)
                    m.then_inc(s["scores"], 1)
                    if g == 0:
                        pe.wait_ge(s["av"], t + 1)
                        pe.matmul(ps[4][:, 0:8], upper[:, :], av, start=True, stop=True).then_inc(s["acs_ps"], 1)
                        pe.wait_ge(s["au"], t + 1)
                        for n in range(2):
                            pe.matmul(ps[2 + n][:, :], ones[:, :], decay[:, 4 * n:4 * n + 4, :].rearrange("p h n -> p (h n)"),
                                      start=True, stop=False)
                            m = pe.matmul(ps[2 + n][:, :], ident_b[:, :], negmask_b[:, :, :].rearrange("p h n -> p (h n)"),
                                          start=False, stop=True)
                        m.then_inc(s["acsB"], 1)
                    pe.wait_ge(s["probs"], 2 * t + g + 1)
                    for half in range(2):
                        for j in range(4):
                            m = pe.transpose(ps[6 + half][:, P * j:P * j + P], sc[:, j, P * half:P * half + P], ident[:, :])
                    m.then_inc(s["pT_ps"], 1)
                    pe.wait_ge(s["pT0"], 2 * t + g + 1)
                    pe.wait_ge(s["pT1"], 2 * t + g + 1)
                    for half in range(2):
                        m = pe.matmul(ps[5][64 * g:64 * g + 64, :], v[:, half, 64 * g:64 * g + 64],
                                      pT[:, half, :, :].rearrange("p c n -> p (c n)"), start=half == 0, stop=half == 1)
                    m.then_inc(s["oT0" if g == 0 else "oT1"], 1)
                pe.wait_ge(s["cv"], 8 * t + 8)
                pe.wait_ge(s["acs"], t + 1)
                for g in range(2):
                    m = pe.matmul(ps[4][:, P + P * g:2 * P + P * g], cv[:, 4 + g, :], cv[:, 6 + g, :], start=True, stop=True)
                m.then_inc(s["cb"], 1)
                pe.wait_ge(s["ext1"], t + 1)
                for k in range(4):
                    pe.transpose(ps[0][:, P * k:P * k + P], cv[:, k, :], ident[:, :])
                for k in range(2):
                    m = pe.transpose(ps[1][:, P * k:P * k + P], cv[:, 4 + k, :], ident[:, :])
                m.then_inc(s["xsbT"], 1)
                pe.wait_ge(s["decay"], 8 * t + 8)
                for g in range(2):
                    m = pe.matmul(ps[3][:, 256 * g:256 * g + 256], cv[:, 6 + g, :], state[:, 256 * g:256 * g + 256],
                                  start=True, stop=True)
                m.then_inc(s["yoff"], 1)
                pe.wait_ge(s["mt"], 2 * t + 2)
                pe.wait_ge(s["xdt"], t + 1)
                pe.wait_ge(s["cd"], t + 1)
                for hh in range(SH):
                    m = pe.matmul(ps[2][:, SP_ * hh:SP_ * hh + SP_], decay[:, hh, :], xdt[:, SP_ * hh:SP_ * hh + SP_],
                                  start=True, stop=True)
                m.then_inc(s["ydiag"], 1)
                pe.wait_ge(s["bt"], t + 1)
                pe.wait_ge(s["xw"], t + 1)
                for g in range(2):
                    m = pe.matmul(ps[0][:, 256 * g:256 * g + 256], bt[:, P * g:P * g + P], xw[:, 256 * g:256 * g + 256],
                                  start=True, stop=True)
                m.then_inc(s["st_ps"], 1)
                pe.wait_ge(s["yn"], t + 1)
                for k in range(4):
                    m = pe.transpose(ps[1][:, P * k:P * k + P], y2[:, P * k:P * k + P], ident[:, :])
                m.then_inc(s["yT_ps"], 1)
                pe.wait_ge(s["cat0"], t + 1)
                pe.wait_ge(s["cat1"], t + 1)
                pe.wait_ge(s["w_out"], 48)
                for n in range(2):
                    for k in range(KD):
                        m = pe.matmul(ps[6 + n][:, :], catT[:, k, :], w_out[:, k, 512 * n:512 * n + 512],
                                      start=k == 0, stop=k == KD - 1)
                m.then_inc(s["mixed"], 1)
            each_tile(pe, a_tile)

        @block.vector
        def _(dve):
            dve.wait_ge(s["consts"], 64)
            dve.tensor_copy(ident_b[:, :], ident[:, :]).then_inc(s["masks"], 1)
            dve.tensor_scalar(negmask_b[:, :, :], repeated(upper[:, :], 4, P), -1.0, -NEG, ALU.add, ALU.mult).then_inc(s["masks"], 1)
            dve.wait_ge(s["cleared"], 9)
            dve.wait_ge(s["bias_ps"], 1)
            dve.tensor_copy(bias_rows[:, P:2 * P], ps[0][0:8, 0:P]).then_inc(s["bias_rows"], 1)
            dve.wait_ge(s["a_exp"], 1)
            dve.tensor_scalar(a_head, a_head, -1.0, None, ALU.mult).then_inc(s["a_head"], 1)
            dve.wait_ge(s["bias"], 16)
            def a_tile(t):
                dve.wait_ge(s["xnT"], t + 1)
                for n in range(2):
                    dve.tensor_tensor(uT[:, 4 * n:4 * n + 4, :], ps[n][:, :].rearrange("p (c n) -> p c n", c=4),
                                      over_heads(g_mix[:, 4 * n:4 * n + 4], 4, P), ALU.mult).then_inc(s["uT"], 1)
                dve.wait_ge(s["p_xbc"], t + 1)
                dve.tensor_copy(row[:, 512:1024], ps[3][:, :]).then_inc(s["xbc1"], 1)
                dve.wait_ge(s["p_kv"], t + 1)
                dve.tensor_tensor(draw, ps[4][:, 0:8], dt_bias, ALU.add).then_inc(s["draw"], 1)
                if not is_first(t):
                    dve.wait_ge(s["shift"], 3 * t)
                dve.tensor_tensor(k_tok[:, :], ps[4][:, 8:136], b_qkv[:, 512:640], ALU.add).then_inc(s["k_tok"], 1)
                dve.tensor_tensor(v[:, 1, :], ps[4][:, 136:264], b_qkv[:, 640:768], ALU.add).then_inc(s["v_tok"], 1)
                dve.wait_ge(s["draw"], t + 1)
                dve.scalar_tensor_tensor(nabs, draw, -1.0, draw, ALU.mult, ALU.max).then_inc(s["nabs"], 1)
                dve.wait_ge(s["p_q"], t + 1)
                dve.tensor_tensor(q_tok[:, :, :, :].rearrange("p j g d -> p g j d"),
                                  ps[5][:, :].rearrange("p (g j d) -> p g j d", g=2, j=4),
                                  b_qkv[:, 0:512].rearrange("p (g j d) -> p g j d", g=2, j=4), ALU.add).then_inc(s["q_tok"], 1)
                dve.wait_ge(s["ex"], t + 1)
                dve.tensor_scalar(w1p, ex, 1.0, None, ALU.add).then_inc(s["w1p"], 1)
                dve.wait_ge(s["w1p"], t + 1)
                dve.scalar_tensor_tensor(rest, w1p, -1.0, ex, ALU.add, ALU.subtract).then_inc(s["rest"], 1)
                dve.reciprocal(rw, w1p).then_inc(s["rw"], 1)
                dve.wait_ge(s["rw"], t + 1)
                dve.tensor_tensor(rest, rest, rw, ALU.mult).then_inc(s["rest2"], 1)
                dve.wait_ge(s["rest2"], t + 1)
                dve.wait_ge(s["lnw"], t + 1)
                dve.tensor_tensor(lnw, lnw, rest, ALU.subtract).then_inc(s["ln1p"], 1)
                dve.wait_ge(s["ln1p"], t + 1)
                dve.scalar_tensor_tensor(dt, draw, 0.0, lnw, ALU.max, ALU.add).then_inc(s["dt"], 1)
                dve.wait_ge(s["dt"], t + 1)
                dve.tensor_tensor(av, dt, a_head, ALU.mult).then_inc(s["av"], 1)
                dve.wait_ge(s["xbcT"], t + 1)
                dve.tensor_copy(ext[:, 4:8, CW - 1:], ps[1][:, :].rearrange("p (c n) -> p c n", c=4)).then_inc(s["ext1"], 1)
                dve.wait_ge(s["qkT_ps"], t + 1)
                dve.tensor_copy(kT[:, 1, :], ps[2][:, 0:P]).then_inc(s["kT"], 1)
                dve.wait_ge(s["acs_ps"], t + 1)
                dve.tensor_copy(acs, ps[4][:, 0:8]).then_inc(s["acs"], 1)
                dve.wait_ge(s["acs"], t + 1)
                dve.tensor_scalar(nacs, acs, -1.0, None, ALU.mult).then_inc(s["nacs"], 1)
                for g in range(2):
                    dve.wait_ge(s["scores"], 2 * t + g + 1)
                    for n in range(2):
                        dve.scalar_tensor_tensor(sc[:, 2 * n:2 * n + 2, :], ps[6 + n][:, :].rearrange("p (c n) -> p c n", c=2),
                                                 HD ** -0.5, bias[:, 4 * g + 2 * n:4 * g + 2 * n + 2, :],
                                                 ALU.mult, ALU.add).then_inc(s["sc"], 1)
                    dve.wait_ge(s["sc"], 4 * t + 2 * g + 2)
                    dve.tensor_scalar(sc[:, :, 0:P], sc[:, :, 0:P], prevmask[:, 0:1], None, ALU.add).then_inc(s["scm"], 1)
                    dve.wait_ge(s["scm"], 2 * t + g + 1)
                    hs = slice(4 * g, 4 * g + 4)
                    dve.tensor_reduce(sm[:, 0, hs], sc[:, :, :], AX_X, ALU.max).then_inc(s["smax"], 1)
                    dve.wait_ge(s["smax"], 2 * t + g + 1)
                    dve.tensor_tensor(sm[:, 0, hs], sm[:, 0, hs], sinks[:, hs], ALU.max).then_inc(s["smax2"], 1)
                    dve.wait_ge(s["smax2"], 2 * t + g + 1)
                    dve.tensor_tensor(sm[:, 5, hs], sinks[:, hs], sm[:, 0, hs], ALU.subtract).then_inc(s["sinkd"], 1)
                    dve.wait_ge(s["sinkd"], 2 * t + g + 1)
                    dve.tensor_scalar(sm[:, 1, hs], sm[:, 0, hs], -1.0, None, ALU.mult).then_inc(s["negm"], 1)
                    if g == 0:
                        dve.wait_ge(s["acsB"], t + 1)
                        dve.wait_ge(s["nacs"], t + 1)
                        dve.tensor_copy(cd[:, 0:4], ps[2][:, P - 1::P]).then_inc(s["last"], 1)
                        dve.tensor_copy(cd[:, 4:8], ps[3][:, P - 1::P]).then_inc(s["last"], 1)
                        dve.wait_ge(s["last"], 2 * t + 2)
                        dve.tensor_tensor(te, cd, nacs, ALU.add).then_inc(s["te_in"], 1)
                        dve.wait_ge(s["ext0"], t + 1)
                        dve.wait_ge(s["ext1"], t + 1)
                        for j in range(CW):
                            if j:
                                dve.wait_ge(s["tap"], (CW * NC_) * t + NC_ * j)
                            for c in range(NC_):
                                if j == 0:
                                    m = dve.tensor_scalar(cv[:, c, :], ext[:, c, 0:P], conv_w[:, 0, c:c + 1], None, ALU.mult)
                                else:
                                    m = dve.scalar_tensor_tensor(cv[:, c, :], ext[:, c, j:j + P], conv_w[:, j, c:c + 1],
                                                                 cv[:, c, :], ALU.mult, ALU.add)
                                m.then_inc(s["tap"], 1)
                        dve.wait_ge(s["tap"], (CW * NC_) * t + CW * NC_)
                        dve.tensor_copy(ext[:, :, 0:CW - 1], ext[:, :, P:P + CW - 1]).then_inc(s["conv"], 1)
                    dve.wait_ge(s["pexp"], 8 * t + 4 * g + 4)
                    dve.wait_ge(s["sinkexp"], 2 * t + g + 1)
                    dve.tensor_tensor(sm[:, 4, hs], sm[:, 2, hs], sm[:, 3, hs], ALU.add).then_inc(s["den"], 1)
                    dve.wait_ge(s["den"], 2 * t + g + 1)
                    dve.reciprocal(sm[:, 4, hs], sm[:, 4, hs]).then_inc(s["rden"], 1)
                    dve.wait_ge(s["rden"], 2 * t + g + 1)
                    dve.tensor_tensor(sc[:, :, :], sc[:, :, :], over_heads(sm[:, 4, hs], 4, 2 * P), ALU.mult).then_inc(s["probs"], 1)
                    dve.wait_ge(s["pT_ps"], 2 * t + g + 1)
                    dve.tensor_copy(pT[:, 1, :, :], ps[7][:, :].rearrange("p (c n) -> p c n", c=4)).then_inc(s["pT1"], 1)
                dve.wait_ge(s["cb"], t + 1)
                for g in range(2):
                    dve.tensor_tensor(decay[:, 4 * g:4 * g + 4, :], decay[:, 4 * g:4 * g + 4, :],
                                      repeated(ps[4][:, P + P * g:2 * P + P * g], 4, P), ALU.mult).then_inc(s["mt"], 1)
                dve.wait_ge(s["xs"], t + 1)
                hd = lambda ap: ap.rearrange("p (h d) -> p h d", h=SH)
                dve.tensor_tensor(hd(xdt[:, :]), hd(xs[:, :]), over_heads(dt, 8, SP_), ALU.mult).then_inc(s["xdt"], 1)
                dve.tensor_tensor(hd(xs[:, :]), hd(xs[:, :]), over_heads(d_skip, 8, SP_), ALU.mult).then_inc(s["skip"], 1)
                dve.wait_ge(s["yoff"], t + 1)
                dve.wait_ge(s["ea"], t + 1)
                dve.tensor_tensor(hd(y[:, :]), hd(ps[3][:, :]), over_heads(ea, 8, SP_), ALU.mult).then_inc(s["y0"], 1)
                dve.wait_ge(s["y0"], t + 1)
                dve.wait_ge(s["skip"], t + 1)
                dve.tensor_tensor(y[:, :], y[:, :], xs[:, :], ALU.add).then_inc(s["y1"], 1)
                dve.wait_ge(s["y1"], t + 1)
                dve.wait_ge(s["ydiag"], t + 1)
                dve.tensor_tensor(y[:, :], y[:, :], ps[2][:, :], ALU.add).then_inc(s["y2"], 1)
                dve.wait_ge(s["y2"], t + 1)
                dve.tensor_tensor(y[:, :], y[:, :], zg[:, :], ALU.mult).then_inc(s["yg"], 1)
                dve.wait_ge(s["cd"], t + 1)
                dve.tensor_tensor(hd(state[:, :]), hd(state[:, :]), over_heads(cd, 8, SP_), ALU.mult).then_inc(s["st_dec"], 1)
                dve.wait_ge(s["st_dec"], t + 1)
                dve.wait_ge(s["st_ps"], t + 1)
                dve.tensor_tensor(state[:, :], state[:, :], ps[0][:, :], ALU.add).then_inc(s["state"], 1)
                dve.wait_ge(s["rstd_g"], t + 1)
                dve.tensor_tensor(y2[:, :].rearrange("p (g n) -> p g n", g=2), y[:, :].rearrange("p (g n) -> p g n", g=2),
                                  over_heads(stat[:, 4:6], 2, 256), ALU.mult).then_inc(s["yn"], 1)
                dve.wait_ge(s["yT_ps"], t + 1)
                dve.tensor_tensor(catT[:, 0:4, :], ps[1][:, :].rearrange("p (c n) -> p c n", c=4),
                                  over_heads(g_ssm[:, :], 4, P), ALU.mult).then_inc(s["cat0"], 1)
                dve.wait_ge(s["mixed"], t + 1)
                dve.wait_ge(s["resid"], t + 1)
                for n in range(2):
                    hn = h[:, bass.ds(t, 1), 512 * n:512 * n + 512].rearrange("p a d -> p (a d)")
                    dve.tensor_tensor(hn, ps[6 + n][:, :], hn, ALU.add).then_inc(s["h1"], 1)
            each_tile(dve, a_tile)


def cross_stage(nc, a, h, gates, plan_row, scratch):
    with ExitStack() as ctx:
        sb = lambda n, s, d=F32: ctx.enter_context(nc.sbuf_tensor(n, s, d))
        s = Signals(nc, ctx, "cx")
        w_kv = sb("w_kv_sb", [P, KD, 2 * XH * XD])
        w_q = sb("w_q_sb", [P, KD, XH * XD])
        w_o = sb("w_o_sb", [P, XH, D])
        w_r = sb("w_router_sb", [P, KD, NE])
        ident = sb("ident2", [P, P])
        upper = sb("upper2", [P, P])
        before_b = sb("before_b", [P, P], BF16)
        ones_b = sb("ones_b", [P, P], BF16)
        gains = sb("gains", [P, 2, KD])
        g_ffn = sb("g_ffn_sb", [P, D])
        b_r = sb("b_router_sb", [P, NE])
        iota_e = sb("iota_e", [P, NE])
        entry = sb("slot_entries", [P, NT, TOPK, 2], I32)
        slots = sb("slots", [P, NT, TOPK], I32)
        zero_slots = sb("zero_slots", [P, NE * REGION // P, 2], I32)

        mem = sb("mem_rows", [P, 2, D])
        memT = sb("memT", [P, KD, MEM])
        kxT = sb("kxT", [P, XH, MEM])
        vx = sb("vx", [P, 2, XH * XD])
        stat = sb("stat2", [P, 12])
        norm_c = sb("norm_c2", [P, 2, 2])
        spare = sb("spare2", [P, 2])
        xn = sb("xn", [P, D])
        uT = sb("uT2", [P, KD, P])
        q_tok = sb("qx_tok", [P, XH * XD])
        qT = sb("qxT", [P, XH, P])
        pr = sb("px", [P, XH, MEM])
        pT = sb("pxT", [P, 2, XH, P])
        oT = sb("oxT", [P, XH, P])
        sm = sb("softmax2", [P, 4, XH])
        rows = sb("moe_rows", [P, D])
        lg = sb("logits", [P, NE])
        mx = sb("top8", [P, 8])
        ix = sb("top8_index", [P, 8], U32)
        ixf = sb("top_index", [P, TOPK])
        ge = sb("gate_exp", [P, TOPK])
        hot = sb("chosen", [P, TOPK, NE])
        picked = sb("picked", [P, TOPK, NE])
        mask = sb("mask", [P, NE])
        mask_b = sb("mask_b", [P, NE], BF16)
        carry = sb("carry", [P, NE])
        rank = sb("rank", [P, NE])
        rank4 = sb("rank4", [P, TOPK])
        slot_f = sb("slot_f", [P, TOPK])
        pl = sb("plan_work", [P, 8, NE])
        (c_up, n_pass, n_cum, before, tmp, e_hot) = (pl[:, i, :] for i in range(6))
        pi = sb("plan_int", [P, NE], I32)
        ones_e = sb("ones_e", [P, NE])
        iota_i = sb("iota_i", [P, 1])
        pv = sb("plan_values", [P, 12])
        plan = sb("plan", [P, 4], I32)

        bias_all = sb("bias_all", [NE, FF2 + D])
        bias_parts = sb("bias_parts", [NE, 3, FF2 + D], BF16)

        ps = [ctx.enter_context(nc.psum_tensor(f"cx_b{i}", [P, 512], F32)) for i in range(8)]
        block = ctx.enter_context(nc.Block())
        c4 = lambda ap: ap.rearrange("p (c n) -> p c n", c=4)
        tile_of = lambda t: h[:, bass.ds(t, 1), :].rearrange("p a d -> p (a d)")

        @block.sync
        def _(sp):
            sp.dma_start(ident[:, :], a["c_ident"]).then_inc(s["consts"], 16)
            sp.dma_start(upper[:, :], a["c_upper"]).then_inc(s["consts"], 16)
            sp.dma_start(mem[:, :, :], a["mem"][0].rearrange("(m p) d -> p m d", p=P)).then_inc(s["mem"], 16)
            sp.dma_start(w_kv[:, :, :], a["w_kv_cross"][0].rearrange("(k p) n -> p k n", p=P)).then_inc(s["w_kv"], 16)
            sp.dma_start(w_q[:, :, :], a["w_q_cross"][0].rearrange("(k p) n -> p k n", p=P)).then_inc(s["w_q"], 16)
            sp.dma_start(w_o[:, :, :], a["w_o_cross"][0].rearrange("(k p) n -> p k n", p=P)).then_inc(s["w_o"], 16)
            with nc.allow_non_contiguous_dma("gains on partitions"):
                for i, n in enumerate(["g_mem", "g_cross"]):
                    sp.dma_start(gains[:, i, :], a[n].rearrange("a (k p) -> p (a k)", p=P)).then_inc(s["gains"], 16)
                sp.dma_start(w_r[:, :, :], a["w_router"][0].rearrange("(k p) n -> p k n", p=P)).then_inc(s["w_r"], 16)
            sp.dma_start(g_ffn[:, :], a["g_ffn"][0, :].partition_broadcast(P)).then_inc(s["w_r"], 16)
            sp.dma_start(b_r[:, :], a["b_router"][0, :].partition_broadcast(P)).then_inc(s["w_r"], 16)
            sp.dma_start(bias_all[:, 0:FF2], a["b1"][0]).then_inc(s["bias_all"], 16)
            sp.dma_start(bias_all[:, FF2:], a["b2"][0]).then_inc(s["bias_all"], 16)
            sp.wait_ge(s["bias_parts"], 5)
            sp.dma_start(scratch["bias_parts"].rearrange("e j n -> e (j n)"), bias_parts[:, :, :].rearrange("e j n -> e (j n)")).then_inc(s["parts_out"], 16)
            def a_tile(t):
                sp.wait_ge(s["rows"], t + 1)
                sp.dma_start(scratch["rows"][bass.ds(t * P, P), :], rows[:, :]).then_inc(s["rows_out"], 16)
            each_tile(sp, a_tile)
            sp.wait_ge(s["rows_out"], 16 * NT)
            sp.wait_ge(s["parts_out"], 16)
            sp.wait_ge(s["plan"], 4)
            sp.dma_start(scratch["plan"], plan[0:MAX_PASSES + 1, :]).then_inc(s["plan_out"], 16)
            sp.wait_ge(s["plan_out"], 16)
            sp.dma_start(plan_row[0:1, :], scratch["plan"].rearrange("(a p) c -> a (p c)", a=1)).then_inc(s["plan_in"], 16)
            sp.wait_ge(s["plan_in"], 16)

        @block.gpsimd
        def _(pool):
            pool.memset(zero_slots[:, :, 0:1], 0).then_inc(s["setup"], 1)
            pool.memset(zero_slots[:, :, 1:2], SEQ * TOPK).then_inc(s["setup"], 1)
            pool.memset(ones_b[:, :], 1.0).then_inc(s["setup"], 1)
            pool.memset(ones_e[:, :], 1.0).then_inc(s["setup"], 1)
            pool.memset(carry[:, :], 0.0).then_inc(s["setup"], 1)
            pool.iota(iota_e[:, :], [[1, NE]], base=0, channel_multiplier=0, allow_small_or_imprecise_dtypes=True).then_inc(s["setup"], 1)
            pool.iota(iota_i[:, :], [[0, 1]], base=0, channel_multiplier=1, allow_small_or_imprecise_dtypes=True).then_inc(s["setup"], 1)
            pool.iota(entry[:, :, :, 0], [[P, NT], [0, TOPK]], base=0, channel_multiplier=1).then_inc(s["setup"], 1)
            pool.iota(entry[:, :, :, 1], [[TOPK * P, NT], [1, TOPK]], base=0, channel_multiplier=TOPK).then_inc(s["setup"], 1)
            pool.memset(norm_c[:, 0, :], EPS).then_inc(s["setup"], 1)
            pool.memset(norm_c[:, 1, :], -0.5).then_inc(s["setup"], 1)
            pool.wait_ge(s["setup"], 11)
            pool.dma_start(scratch["slot_table"].rearrange("(p f) a -> p (f a)", p=P), zero_slots[:, :, :].rearrange("p f a -> p (f a)")).then_inc(s["table_clear"], 16)
            pool.wait_ge(s["mem_ss"], 2)
            rstd_of(pool, norm_c, stat[:, 2:4], stat[:, 0:2], 2, s["mem_rstd_ms"], s["mem_rstd"], 1)
            pool.wait_ge(s["table_clear"], 16)
            for t in range(NT):
                pool.wait_ge(s["ss"], t + 1)
                rstd_of(pool, norm_c, stat[:, 5:6], stat[:, 4:5], 1, s["rstd_ms"], s["rstd"], t + 1)
                pool.wait_ge(s["ss2"], t + 1)
                rstd_of(pool, norm_c, stat[:, 7:8], stat[:, 6:7], 1, s["rstd2_ms"], s["rstd2"], t + 1)
                pool.wait_ge(s["slots"], t + 1)
                for j in range(TOPK):
                    pool.indirect_dma_start(scratch["slot_table"], bass.IndirectOffsetOnAxis(ap=slots[:, t, j:j + 1], axis=0),
                                            entry[:, t, j, :], None).then_inc(s["table"], 16)
            pool.wait_ge(s["table"], 16 * NT * TOPK)

        @block.scalar
        def _(act):
            act.wait_ge(s["mem"], 16)
            for m in range(2):
                act.activation((xn, rows)[m][:, :], mem[:, m, :], ACT.Square, scale=1 / 32, accum_out=stat[:, m:m + 1]).then_inc(s["mem_ss"], 1)
            act.wait_ge(s["mem_rstd"], 1)
            for m in range(2):
                act.activation(mem[:, m, :], mem[:, m, :], ACT.Copy, scale=stat[:, 2 + m:3 + m]).then_inc(s["mem_n"], 1)
            act.wait_ge(s["kx_ps"], 1)
            for n in range(2):
                act.activation(kxT[:, 2 * n:2 * n + 2, :], ps[2 + n][:, :].rearrange("p (c n) -> p c n", c=2), ACT.Copy).then_inc(s["kxT"], 1)
            def met():
                act.activation(spare[:, 0:1], ident[:, 0:1], ACT.Copy)

            def a_tile(t):
                if not is_first(t):
                    act.wait_ge(s["uTr"], 2 * t)
                met()
                act.activation(xn[:, :], tile_of(t), ACT.Square, scale=1 / 32, accum_out=stat[:, 4:5]).then_inc(s["ss"], 1)
                act.wait_ge(s["rstd"], t + 1)
                met()
                act.activation(xn[:, :], tile_of(t), ACT.Copy, scale=stat[:, 5:6]).then_inc(s["xn"], 1)
                act.wait_ge(s["q_ps"], t + 1)
                act.activation(q_tok[:, :], ps[2][:, :], ACT.Copy).then_inc(s["q_tok"], 1)
                act.wait_ge(s["qT_ps"], t + 1)
                act.activation(qT[:, :, :], c4(ps[3][:, :]), ACT.Copy).then_inc(s["qT"], 1)
                act.wait_ge(s["negm"], t + 1)
                for j in range(XH):
                    act.activation(pr[:, j, :], ps[4 + j // 2][:, MEM * (j % 2):MEM * (j % 2) + MEM], ACT.Exp, scale=XD ** -0.5,
                                   bias=sm[:, 1, j:j + 1], accum_out=sm[:, 2, j:j + 1]).then_inc(s["pexp"], 1)
                act.wait_ge(s["pT_ps"], t + 1)
                act.activation(pT[:, 0, :, :], c4(ps[6][:, :]), ACT.Copy).then_inc(s["pT0"], 1)
                act.wait_ge(s["oT_ps"], t + 1)
                act.activation(oT[:, :, :], c4(ps[2][:, :]), ACT.Copy).then_inc(s["oT"], 1)
                act.wait_ge(s["h2"], 2 * t + 2)
                if not is_first(t):
                    act.wait_ge(s["rows_out"], 16 * t)
                met()
                act.activation(rows[:, :], tile_of(t), ACT.Square, scale=1 / 32, accum_out=stat[:, 6:7]).then_inc(s["ss2"], 1)
                act.wait_ge(s["neg1"], t + 1)
                act.activation(ge[:, :], mx[:, 0:TOPK], ACT.Exp, bias=stat[:, 8:9], accum_out=stat[:, 9:10]).then_inc(s["ge"], 1)
            each_tile(act, a_tile)

        @block.tensor
        def _(pe):
            pe.wait_ge(s["consts"], 32)
            pe.wait_ge(s["mem_n"], 2)
            for m in range(2):
                for n in range(2):
                    for k in range(4):
                        i = 4 * n + k
                        tr = pe.transpose(ps[2 * m + n][:, P * k:P * k + P], mem[:, m, P * i:P * i + P], ident[:, :])
            tr.then_inc(s["memT_ps"], 1)
            pe.wait_ge(s["memT"], 4)
            pe.wait_ge(s["w_kv"], 16)
            for j in range(XH):
                for k in range(KD):
                    m = pe.matmul(ps[2 + j // 2][:, MEM * (j % 2):MEM * (j % 2) + MEM], w_kv[:, k, XD * j:XD * j + XD], memT[:, k, :],
                                  start=k == 0, stop=k == KD - 1)
            m.then_inc(s["kx_ps"], 1)
            for half in range(2):
                for k in range(KD):
                    m = pe.matmul(ps[4 + half][:, :], memT[:, k, P * half:P * half + P], w_kv[:, k, XH * XD:],
                                  start=k == 0, stop=k == KD - 1)
            m.then_inc(s["vx_ps"], 1)
            pe.wait_ge(s["kxT"], 2)
            pe.wait_ge(s["vx"], 2)
            pe.wait_ge(s["setup"], 11)
            pe.wait_ge(s["before"], 1)
            def a_tile(t):
                pe.wait_ge(s["xn"], t + 1)
                if not is_first(t):
                    pe.wait_ge(s["uTr"], 2 * t)
                for k in range(KD):
                    m = pe.transpose(ps[k // 4][:, P * (k % 4):P * (k % 4) + P], xn[:, P * k:P * k + P], ident[:, :])
                m.then_inc(s["xnT"], 1)
                pe.wait_ge(s["uT"], 2 * t + 2)
                pe.wait_ge(s["w_q"], 16)
                for k in range(KD):
                    m = pe.matmul(ps[2][:, :], uT[:, k, :], w_q[:, k, :], start=k == 0, stop=k == KD - 1)
                m.then_inc(s["q_ps"], 1)
                pe.wait_ge(s["q_tok"], t + 1)
                if not is_first(t):
                    pe.wait_ge(s["lg"], t)
                for k in range(XH):
                    m = pe.transpose(ps[3][:, P * k:P * k + P], q_tok[:, P * k:P * k + P], ident[:, :])
                m.then_inc(s["qT_ps"], 1)
                pe.wait_ge(s["qT"], t + 1)
                if not is_first(t):
                    pe.wait_ge(s["h2"], 2 * t)
                for j in range(XH):
                    m = pe.matmul(ps[4 + j // 2][:, MEM * (j % 2):MEM * (j % 2) + MEM], qT[:, j, :], kxT[:, j, :], start=True, stop=True)
                m.then_inc(s["scores"], 1)
                pe.wait_ge(s["probs"], t + 1)
                if not is_first(t):
                    pe.wait_ge(s["carry"], t)
                for half in range(2):
                    for j in range(XH):
                        m = pe.transpose(ps[6 + half][:, P * j:P * j + P], pr[:, j, P * half:P * half + P], ident[:, :])
                m.then_inc(s["pT_ps"], 1)
                pe.wait_ge(s["pT0"], t + 1)
                pe.wait_ge(s["pT1"], t + 1)
                for j in range(XH):
                    for half in range(2):
                        m = pe.matmul(ps[2][:, P * j:P * j + P], vx[:, half, XD * j:XD * j + XD], pT[:, half, j, :],
                                      start=half == 0, stop=half == 1)
                m.then_inc(s["oT_ps"], 1)
                pe.wait_ge(s["oT"], t + 1)
                pe.wait_ge(s["w_o"], 16)
                for n in range(2):
                    for k in range(XH):
                        m = pe.matmul(ps[4 + n][:, :], oT[:, k, :], w_o[:, k, 512 * n:512 * n + 512], start=k == 0, stop=k == XH - 1)
                m.then_inc(s["o_ps"], 1)
                pe.wait_ge(s["rows"], t + 1)
                for k in range(KD):
                    m = pe.transpose(ps[k // 4][:, P * (k % 4):P * (k % 4) + P], rows[:, P * k:P * k + P], ident[:, :])
                m.then_inc(s["rowsT"], 1)
                pe.wait_ge(s["uTr"], 2 * t + 2)
                pe.wait_ge(s["w_r"], 48)
                for k in range(KD):
                    m = pe.matmul(ps[3][:, 0:NE], uT[:, k, :], w_r[:, k, :], start=k == 0, stop=k == KD - 1)
                m.then_inc(s["lg_ps"], 1)
                pe.wait_ge(s["mask_b"], t + 1)
                pe.matmul(ps[6][:, 0:NE], before_b[:, :], mask_b[:, :], start=True, stop=True).then_inc(s["rank_ps"], 1)
                pe.matmul(ps[7][:, 0:NE], ones_b[:, :], mask_b[:, :], start=True, stop=True).then_inc(s["count_ps"], 1)
            each_tile(pe, a_tile)

        @block.vector
        def _(dve):
            dve.wait_ge(s["consts"], 32)
            dve.tensor_tensor(before_b[:, :], upper[:, :], ident[:, :], ALU.subtract).then_inc(s["before"], 1)
            dve.wait_ge(s["memT_ps"], 1)
            dve.wait_ge(s["gains"], 32)
            for m in range(2):
                for n in range(2):
                    dve.tensor_tensor(memT[:, 4 * n:4 * n + 4, P * m:P * m + P], c4(ps[2 * m + n][:, :]),
                                      over_heads(gains[:, 0, 4 * n:4 * n + 4], 4, P), ALU.mult).then_inc(s["memT"], 1)
            dve.wait_ge(s["vx_ps"], 1)
            for half in range(2):
                dve.tensor_copy(vx[:, half, :], ps[4 + half][:, :]).then_inc(s["vx"], 1)
            dve.wait_ge(s["bias_all"], 32)
            dve.tensor_copy(bias_parts[:, 0, :], bias_all[:, :]).then_inc(s["bias_parts"], 1)
            for j in range(1, 3):
                dve.wait_ge(s["bias_parts"], 2 * j - 1)
                dve.tensor_tensor(bias_all[:, :], bias_all[:, :], bias_parts[:, j - 1, :],
                                  ALU.subtract).then_inc(s["bias_parts"], 1)
                dve.wait_ge(s["bias_parts"], 2 * j)
                dve.tensor_copy(bias_parts[:, j, :], bias_all[:, :]).then_inc(s["bias_parts"], 1)
            dve.wait_ge(s["setup"], 11)
            dve.wait_ge(s["w_r"], 48)
            def met():
                dve.memset(spare[:, 1:2], 0.0)

            def a_tile(t):
                dve.wait_ge(s["xnT"], t + 1)
                for n in range(2):
                    dve.tensor_tensor(uT[:, 4 * n:4 * n + 4, :], c4(ps[n][:, :]), over_heads(gains[:, 1, 4 * n:4 * n + 4], 4, P),
                                      ALU.mult).then_inc(s["uT"], 1)
                dve.wait_ge(s["scores"], t + 1)
                for n in range(2):
                    dve.tensor_reduce(sm[:, 0, 2 * n:2 * n + 2], ps[4 + n][:, :].rearrange("p (c n) -> p c n", c=2), AX_X,
                                      ALU.max).then_inc(s["smax"], 1)
                dve.wait_ge(s["smax"], 2 * t + 2)
                dve.tensor_scalar(sm[:, 1, :], sm[:, 0, :], -XD ** -0.5, None, ALU.mult).then_inc(s["negm"], 1)
                dve.wait_ge(s["pexp"], 4 * t + 4)
                dve.reciprocal(sm[:, 3, :], sm[:, 2, :]).then_inc(s["rden"], 1)
                dve.wait_ge(s["rden"], t + 1)
                dve.tensor_tensor(pr[:, :, :], pr[:, :, :], over_heads(sm[:, 3, :], 4, MEM), ALU.mult).then_inc(s["probs"], 1)
                dve.wait_ge(s["pT_ps"], t + 1)
                dve.tensor_copy(pT[:, 1, :, :], c4(ps[7][:, :])).then_inc(s["pT1"], 1)
                dve.wait_ge(s["o_ps"], t + 1)
                for n in range(2):
                    hn = h[:, bass.ds(t, 1), 512 * n:512 * n + 512].rearrange("p a d -> p (a d)")
                    dve.tensor_tensor(hn, ps[4 + n][:, :], hn, ALU.add).then_inc(s["h2"], 1)
                dve.wait_ge(s["rstd2"], t + 1)
                dve.scalar_tensor_tensor(rows[:, :], tile_of(t), stat[:, 7:8], g_ffn[:, :], ALU.mult, ALU.mult).then_inc(s["rows"], 1)
                dve.wait_ge(s["rowsT"], t + 1)
                for n in range(2):
                    dve.tensor_copy(uT[:, 4 * n:4 * n + 4, :], c4(ps[n][:, :])).then_inc(s["uTr"], 1)
                dve.wait_ge(s["lg_ps"], t + 1)
                dve.tensor_tensor(lg[:, :], ps[3][:, 0:NE], b_r[:, :], ALU.add).then_inc(s["lg"], 1)
                dve.wait_ge(s["lg"], t + 1)
                met()
                dve.max(mx[:, :], lg[:, :]).then_inc(s["mx"], 1)
                dve.wait_ge(s["mx"], t + 1)
                dve.tensor_scalar(stat[:, 8:9], mx[:, 0:1], -1.0, None, ALU.mult).then_inc(s["neg1"], 1)
                dve.max_index(ix[:, :], mx[:, :], lg[:, :]).then_inc(s["ix"], 1)
                dve.wait_ge(s["ix"], t + 1)
                dve.tensor_copy(ixf[:, :], ix[:, 0:TOPK]).then_inc(s["ixf"], 1)
                dve.wait_ge(s["ixf"], t + 1)
                dve.tensor_tensor(hot[:, :, :], repeated(iota_e[:, :], TOPK, NE), over_heads(ixf[:, :], TOPK, NE),
                                  ALU.is_equal).then_inc(s["hot"], 1)
                dve.wait_ge(s["hot"], t + 1)
                dve.tensor_reduce(mask[:, :], hot[:, :, :].rearrange("p j e -> p e j"), AX_X, ALU.add).then_inc(s["mask"], 1)
                dve.wait_ge(s["mask"], t + 1)
                dve.tensor_copy(mask_b[:, :], mask[:, :]).then_inc(s["mask_b"], 1)
                dve.wait_ge(s["ge"], t + 1)
                dve.reciprocal(stat[:, 10:11], stat[:, 9:10]).then_inc(s["rge"], 1)
                dve.wait_ge(s["rge"], t + 1)
                dve.tensor_scalar(gates[:, bass.ds(t, 1), :].rearrange("p a j -> p (a j)"), ge[:, :], stat[:, 10:11], None,
                                  ALU.mult).then_inc(s["gates"], 1)
                dve.wait_ge(s["rank_ps"], t + 1)
                dve.tensor_tensor(rank[:, :], ps[6][:, 0:NE], carry[:, :], ALU.add).then_inc(s["rank"], 1)
                dve.wait_ge(s["rank"], t + 1)
                dve.wait_ge(s["count_ps"], t + 1)
                dve.tensor_tensor(carry[:, :], ps[7][:, 0:NE], carry[:, :], ALU.add).then_inc(s["carry"], 1)
                dve.tensor_tensor(picked[:, :, :], hot[:, :, :], repeated(rank[:, :], TOPK, NE), ALU.mult).then_inc(s["picked"], 1)
                dve.wait_ge(s["picked"], t + 1)
                dve.tensor_reduce(rank4[:, :], picked[:, :, :], AX_X, ALU.add).then_inc(s["rank4"], 1)
                dve.wait_ge(s["rank4"], t + 1)
                dve.scalar_tensor_tensor(slot_f[:, :], ixf[:, :], float(REGION), rank4[:, :], ALU.mult, ALU.add).then_inc(s["slot_f"], 1)
                dve.wait_ge(s["slot_f"], t + 1)
                dve.tensor_copy(slots[:, bass.ds(t, 1), :].rearrange("p a j -> p (a j)"), slot_f[:, :]).then_inc(s["slots"], 1)
            each_tile(dve, a_tile)
            step = [0]

            def then(ins):
                step[0] += 1
                ins.then_inc(s["plan_step"], 1)
                dve.wait_ge(s["plan_step"], step[0])

            col = lambda i: pv[:, i:i + 1]
            total, expert, first, count, nth, rem, base = (col(i) for i in range(7))
            dve.wait_ge(s["carry"], NT)
            then(dve.tensor_scalar(c_up, carry[:, :], float(PASS - 1), None, ALU.add))
            then(dve.tensor_copy(pi[:, :], c_up))
            then(dve.tensor_scalar(pi[:, :], pi[:, :], int(math.log2(PASS)), None, ALU.logical_shift_right))
            then(dve.tensor_copy(n_pass, pi[:, :]))
            then(dve.tensor_tensor_scan(n_cum, ones_e[:, :], n_pass, 0.0, ALU.mult, ALU.add))
            then(dve.tensor_scalar(before, n_cum, iota_i[:, 0:1], None, ALU.is_le))
            then(dve.tensor_reduce(expert, before, AX_X, ALU.add))
            then(dve.tensor_tensor(tmp, before, n_pass, ALU.mult))
            then(dve.tensor_reduce(first, tmp, AX_X, ALU.add))
            then(dve.tensor_scalar(expert, expert, float(NE - 1), None, ALU.min))
            then(dve.tensor_scalar(e_hot, iota_e[:, :], expert, None, ALU.is_equal))
            then(dve.tensor_tensor(tmp, e_hot, carry[:, :], ALU.mult))
            then(dve.tensor_reduce(count, tmp, AX_X, ALU.add))
            then(dve.tensor_tensor(nth, iota_i[:, :], first, ALU.subtract))
            then(dve.tensor_scalar(nth, nth, float(REGION // PASS - 1), 0.0, ALU.min, ALU.max))
            then(dve.scalar_tensor_tensor(rem, nth, -float(PASS), count, ALU.mult, ALU.add))
            then(dve.tensor_scalar(base, expert, float(REGION), None, ALU.mult))
            then(dve.scalar_tensor_tensor(base, nth, float(PASS), base, ALU.mult, ALU.add))
            dve.tensor_copy(plan[:, 0:1], expert).then_inc(s["plan"], 1)
            dve.tensor_copy(plan[:, 1:2], base).then_inc(s["plan"], 1)
            dve.tensor_scalar(plan[:, 2:3], rem, float(P), None, ALU.is_gt).then_inc(s["plan"], 1)
            dve.tensor_copy(plan[:, 3:4], n_cum[:, NE - 1:NE]).then_inc(s["plan"], 1)


def expert_stage(nc, a, plan_row, scratch):
    with ExitStack() as ctx:
        sb = lambda n, s, d=F32: ctx.enter_context(nc.sbuf_tensor(n, s, d))
        s = Signals(nc, ctx, "ex")
        raw = sb("raw_pieces", [P, RING, KD // 2 * FW])
        w1 = sb("w1_parts", [P, 2, 2, KD, FW], F32R)
        w2 = sb("w2_parts", [P, 2, 2, GK, D], F32R)
        ident = sb("ident3", [P, P])
        bias3 = sb("bias3", [B2_AT + 3, FF2], BF16)
        ones3 = sb("ones3", [B2_AT + 3, P], BF16)
        idx = sb("row_index", [P, 2, 2], I32)
        out_idx = sb("out_index", [P, 2, 2], I32)
        spare = sb("spare3", [P, 2])
        got = sb("gathered", [P, 2, D])
        uT = sb("uT3", [P, 2, 2, KD, P], F32R)
        glu = sb("glu", [P, 2, FW // 2])
        sig = sb("sig", [P, 2, FW // 2])
        lin = sb("lin", [P, 2, FW // 2])
        actT = sb("actT", [P, 2, 2, GK, P], F32R)
        y = sb("y_rows", [P, 2, D])

        ps_h = [ctx.enter_context(nc.psum_tensor(f"ex_h{b}", [P, FW], F32)) for b in range(2)]
        ps_g = ctx.enter_context(nc.psum_tensor("ex_g", [P, 2, GK, P], F32))
        ps_u = ctx.enter_context(nc.psum_tensor("ex_u", [P, 4, P], F32))
        ps_y = [[ctx.enter_context(nc.psum_tensor(f"ex_y{b}{n}", [P, 512], F32)) for n in range(2)] for b in range(2)]
        block = ctx.enter_context(nc.Block())

        w1_v = a["w1"][0].rearrange("e (k p) f -> e p k f", p=P)
        w2_v = a["w2"][0].rearrange("e (c k p) d -> e p c k d", k=GK, p=P)

        pieces = [("w1", 0, 0), ("w1", 0, 1)]
        for c in range(1, FCH):
            pieces += [("w1", c, 0), ("w1", c, 1), ("w2", c - 1, 0)]
        pieces += [("w2", FCH - 1, 0)]
        NQ = len(pieces)
        place = {piece: q for q, piece in enumerate(pieces)}

        def rounded_count(i, *piece):
            return i * NQ + (place[piece] + 1)

        def split(i, q):
            back, q = (1, q + NQ) if q < 0 else (0, q)
            kind = pieces[q][0]
            same = [p for p in pieces if p[0] == kind]
            return s[f"split_{kind}"], i * len(same) + (same.index(pieces[q]) + 1 - back * len(same))

        def rest_of(eng, i, *piece):
            kind, c, half = piece
            q = place[piece]
            eng.wait_ge(s["rounded"], rounded_count(i, *piece))
            if kind == "w1":
                part = [w1[:, c % 2, j, 4 * half:4 * half + 4, :].rearrange("p k f -> p (k f)") for j in range(2)]
            else:
                part = [w2[:, c % 2, j, :, :].rearrange("p k f -> p (k f)") for j in range(2)]
            eng.tensor_tensor(part[1], raw[:, q % RING, :], part[0].bitcast(F32), ALU.subtract).then_inc(s[f"split_{kind}"], 1)

        def slots_at(first_slot):
            return scratch["slot_table"][bass.ds(first_slot, PASS), :].rearrange("(b p) a -> p b a", p=P)

        def passes(eng):
            return eng.value_load(plan_row[0:1, 3:4], min_val=1, max_val=MAX_PASSES)

        def plan_of(eng, i, what, most):
            return eng.value_load(plan_row[0:1, bass.ds(i * 4 + what, 1)], min_val=0, max_val=most)

        def each_pass(eng, n, body):
            body(0)
            with eng.Fori(1, n) as i:
                body(i)

        def by_blocks(eng, body):
            def choose(i):
                two = plan_of(eng, i, 2, 1)
                with eng.If(two > 0):
                    body(i, 2)
                with eng.Else():
                    body(i, 1)
            return choose

        @block.sync
        def _(sp):
            def load(e, q):
                kind, c, half = pieces[q]
                if kind == "w1":
                    src = w1_v[bass.ds(e, 1), :, 4 * half:4 * half + 4, FW * c:FW * c + FW].rearrange("a p k f -> (a p) k f")
                else:
                    src = w2_v[bass.ds(e, 1), :, c, :, :].rearrange("a p k d -> (a p) k d")
                sp.dma_start(raw[:, q % RING, :].rearrange("p (k f) -> p k f", f=src.shape[-1]), src).then_inc(s[f"raw_{q % RING}"], 16)

            def body(i):
                e = plan_of(sp, i, 0, NE - 1)
                for q in range(NQ):
                    if q >= RING or not is_first(i):
                        sp.wait_ge(*split(i, q - RING))
                    load(e, q)

            sp.dma_start(ident[:, :], a["c_ident"]).then_inc(s["consts"], 16)
            n = passes(sp)
            each_pass(sp, n, body)
            e = plan_of(sp, n, 0, NE - 1)
            sp.wait_ge(*split(n, 1 - RING))
            for q in range(2):
                load(e, q)

        @block.gpsimd
        def _(pool):
            pool.memset(ones3[:, :], 1.0).then_inc(s["cleared"], 1)
            pool.memset(spare[:, :], 0.0).then_inc(s["cleared"], 1)
            pool.memset(y[:, :, :], 0.0).then_inc(s["cleared"], 1)
            pool.wait_ge(s["cleared"], 3)

            def met():
                pool.tensor_tensor(spare[:, 0:1], spare[:, 1:2], spare[:, 1:2], ALU.add).then_inc(s["met"], 1)

            def gather(i, mets):
                first_slot = plan_of(pool, i, 1, NE * REGION - PASS)
                if not is_first(i):
                    pool.wait_ge(s["uT_ps"], 4 * i)
                with nc.allow_non_contiguous_dma("256 row numbers"):
                    pool.dma_start(idx[:, :, :], slots_at(first_slot)).then_inc(s["idx"], 16)
                if not is_first(i):
                    pool.wait_ge(s["met"], mets)
                pool.wait_ge(s["idx"], 16 * i + 16)
                met()
                for b in range(2):
                    pool.indirect_dma_start(got[:, b, :], None, scratch["rows"],
                                            bass.IndirectOffsetOnAxis(ap=idx[:, b, 0:1], axis=0)).then_inc(s["got"], 16)

            def body(i):
                gather(i + 1, 2 * i + 1)
                for c in range(FCH):
                    rest_of(pool, i, "w2", c, 0)
                first_slot = plan_of(pool, i, 1, NE * REGION - PASS)
                if not is_first(i):
                    pool.wait_ge(s["stored"], 32 * i)
                with nc.allow_non_contiguous_dma("256 row numbers"):
                    pool.dma_start(out_idx[:, :, :], slots_at(first_slot)).then_inc(s["out_idx"], 16)
                pool.wait_ge(s["met"], 2 * i + 2)
                pool.wait_ge(s["out_idx"], 16 * i + 16)
                pool.wait_ge(s["y_left"], 2 * i + 2)
                met()
                for b in range(2):
                    pool.indirect_dma_start(scratch["y"], bass.IndirectOffsetOnAxis(ap=out_idx[:, b, 1:2], axis=0), y[:, b, :], None,
                                            bounds_check=SEQ * TOPK - 1, oob_is_err=False).then_inc(s["stored"], 16)

            gather(0, None)
            n = passes(pool)
            each_pass(pool, n, body)
            pool.wait_ge(s["stored"], 32 * n)

        @block.tensor
        def _(pe):
            def product(ps, lhsT, rhs, start):
                pe.matmul(ps, lhsT[0], rhs[0], start=start, stop=False)
                pe.matmul(ps, lhsT[0], rhs[1], start=False, stop=False)
                pe.matmul(ps, lhsT[1], rhs[0], start=False, stop=False)

            def row_transposes(i, r):
                if r == 0:
                    pe.wait_ge(s["got"], 32 * i + 32)
                if r or not is_first(i):
                    pe.wait_ge(s["uT"], 4 * i + r)
                for k in range(4):
                    m = pe.transpose(ps_u[:, k, :], got[:, r // 2, P * (4 * (r % 2) + k):P * (4 * (r % 2) + k) + P], ident[:, :])
                m.then_inc(s["uT_ps"], 1)

            def hidden(i, c, nb):
                for b in range(nb):
                    if c == 0:
                        pe.wait_ge(s["uT"], 4 * i + 2 * b + 2)
                    for k in range(KD):
                        if b == 0 and k % 4 == 0:
                            pe.wait_ge(*split(i, place["w1", c, k // 4]))
                        product(ps_h[b][:, :], [uT[:, j, b, k, :] for j in range(2)], [w1[:, c % 2, j, k, :] for j in range(2)], k == 0)
                    if b == 0 and c == 0:
                        pe.wait_ge(s["bias3"], 32 * i + 32)
                    m = pe.matmul(ps_h[b][:, :], ones3[0:3, :], bias3[0:3, FW * c:FW * c + FW], start=False, stop=True)
                    m.then_inc(s["h"], 1 if nb == 2 else 2)

            def out(i, c, nb, between=None):
                pe.wait_ge(s["actT"], 4 * i + (c + 1))
                pe.wait_ge(*split(i, place["w2", c, 0]))
                if c == 0 and not is_first(i):
                    pe.wait_ge(s["y_left"], 2 * i)
                for n in range(2):
                    for b in range(nb):
                        for k in range(GK):
                            cols = slice(512 * n, 512 * n + 512)
                            product(ps_y[b][n][:, :], [actT[:, j, b, k, :] for j in range(2)], [w2[:, c % 2, j, k, cols] for j in range(2)],
                                    c == 0 and k == 0)
                        if c == FCH - 1:
                            m = pe.matmul(ps_y[b][n][:, :], ones3[B2_AT:, :], bias3[B2_AT:, 512 * n:512 * n + 512], start=False, stop=True)
                            if (n, b) == (1, nb - 1):
                                m.then_inc(s["out"], 1)
                    if n == 0 and between:
                        between()

            def body(i, nb):
                for c in range(FCH):
                    hidden(i, c, nb)
                    if c == FCH - 1:
                        row_transposes(i + 1, 0)
                    if c:
                        out(i, c - 1, nb)
                    if c == FCH - 1:
                        row_transposes(i + 1, 1)
                    pe.wait_ge(s["act"], 8 * i + (2 * c + 2))
                    for b in range(nb):
                        for k in range(GK):
                            m = pe.transpose(ps_g[:, b, k, :], lin[:, b, P * k:P * k + P], ident[:, :])
                    m.then_inc(s["gT"], 1)
                row_transposes(i + 1, 2)
                out(i, FCH - 1, nb, lambda: row_transposes(i + 1, 3))

            pe.wait_ge(s["consts"], 16)
            pe.wait_ge(s["cleared"], 3)
            for r in range(4):
                row_transposes(0, r)
            n = passes(pe)
            each_pass(pe, n, by_blocks(pe, body))
            pe.wait_ge(s["bias3"], 32 * n + 32)

        @block.scalar
        def _(act):
            def bias_in(i):
                parts = scratch["bias_parts"][bass.ds(plan_of(act, i, 0, NE - 1), 1), :, :].rearrange("a j n -> (a j) n")
                act.dma_start(bias3[0:3, :], parts[:, 0:FF2]).then_inc(s["bias3"], 16)
                act.dma_start(bias3[B2_AT:, 0:D], parts[:, FF2:]).then_inc(s["bias3"], 16)

            def rounded(i, *piece):
                kind, c, half = piece
                q = place[piece]
                act.wait_ge(s[f"raw_{q % RING}"], 16 * (NQ // RING) * i + 16 * (q // RING + 1))
                if kind == "w1":
                    if c >= 2 or not is_first(i):
                        act.wait_ge(s["h"], 8 * i + (2 * c - 2))
                    dst = w1[:, c % 2, 0, 4 * half:4 * half + 4, :].rearrange("p k f -> p (k f)")
                else:
                    if c >= 2 or not is_first(i):
                        act.wait_ge(s["gT"], 4 * i + c)
                    dst = w2[:, c % 2, 0, :, :].rearrange("p k f -> p (k f)")
                act.activation(dst, raw[:, q % RING, :], ACT.Copy).then_inc(s["rounded"], 1)

            def rows_rounded(i, r):
                act.wait_ge(s["uT_ps"], 4 * i + (r + 1))
                k = 4 * (r % 2)
                act.activation(uT[:, 0, r // 2, k:k + 4, :].rearrange("p k n -> p (k n)"), ps_u[:, :, :].rearrange("p k n -> p (k n)"),
                               ACT.Copy).then_inc(s["uT_rounded"], 1)

            def body(i, nb):
                for c in range(FCH):
                    if c < FCH - 1:
                        rounded(i, "w1", c + 1, 0)
                    else:
                        rounded(i, "w2", c, 0)
                    for b in range(nb):
                        act.wait_ge(s["glu"], 8 * i + (2 * c + (b + 1 if nb == 2 else 2)))
                        act.activation(sig[:, b, :], glu[:, b, :], ACT.Sigmoid, scale=ALPHA).then_inc(s["sig"], 1 if nb == 2 else 2)
                    if c < FCH - 1:
                        rounded(i, "w1", c + 1, 1)
                        rounded(i, "w2", c, 0)
                    else:
                        rows_rounded(i + 1, 0)
                        rounded(i + 1, "w1", 0, 0)
                        rows_rounded(i + 1, 1)
                    act.wait_ge(s["gT"], 4 * i + (c + 1))
                    act.activation(actT[:, 0, 0:nb, :, :].rearrange("p b k n -> p (b k n)"),
                                   ps_g[:, 0:nb, :, :].rearrange("p b k n -> p (b k n)"), ACT.Copy).then_inc(s["actT_rounded"], 1)
                rows_rounded(i + 1, 2)
                rows_rounded(i + 1, 3)
                rounded(i + 1, "w1", 0, 1)
                act.wait_ge(s["out"], i + 1)
                if not is_first(i):
                    act.wait_ge(s["stored"], 32 * i)
                for b in range(nb):
                    m = act.activation(y[:, b, 0:512], ps_y[b][0][:, :], ACT.Copy)
                m.then_inc(s["y_left"], 1)
                bias_in(i + 1)

            act.wait_ge(s["cleared"], 3)
            bias_in(0)
            rounded(0, "w1", 0, 0)
            rounded(0, "w1", 0, 1)
            for r in range(4):
                rows_rounded(0, r)
            n = passes(act)
            each_pass(act, n, by_blocks(act, body))

        @block.vector
        def _(dve):
            def rows_rest(i, r):
                dve.wait_ge(s["uT_rounded"], 4 * i + (r + 1))
                k = 4 * (r % 2)
                dve.tensor_tensor(uT[:, 1, r // 2, k:k + 4, :], ps_u[:, :, :], uT[:, 0, r // 2, k:k + 4, :].bitcast(F32),
                                  ALU.subtract).then_inc(s["uT"], 1)

            def gated(i, c, b, nb):
                inc = 1 if nb == 2 else 2
                at = 8 * i + (2 * c + (b + 1 if nb == 2 else 2))
                dve.wait_ge(s["h"], at)
                dve.tensor_scalar(glu[:, b, :], ps_h[b][:, 0::2], LIMIT, None, ALU.min).then_inc(s["glu"], inc)
                dve.tensor_scalar(lin[:, b, :], ps_h[b][:, 1::2], LIMIT, -LIMIT, ALU.min, ALU.max).then_inc(s["lin"], inc)
                dve.wait_ge(s["lin"], at)
                dve.scalar_tensor_tensor(lin[:, b, :], lin[:, b, :], 1.0, glu[:, b, :], ALU.add, ALU.mult).then_inc(s["lin_glu"], inc)
                dve.wait_ge(s["lin_glu"], at)
                dve.wait_ge(s["sig"], at)
                dve.tensor_tensor(lin[:, b, :], lin[:, b, :], sig[:, b, :], ALU.mult).then_inc(s["act"], inc)

            def body(i, nb):
                for c in range(FCH):
                    if c < FCH - 1:
                        rest_of(dve, i, "w1", c + 1, 0)
                    for b in range(nb):
                        gated(i, c, b, nb)
                    if c < FCH - 1:
                        rest_of(dve, i, "w1", c + 1, 1)
                    else:
                        rows_rest(i + 1, 0)
                        rest_of(dve, i + 1, "w1", 0, 0)
                        rows_rest(i + 1, 1)
                    dve.wait_ge(s["actT_rounded"], 4 * i + (c + 1))
                    dve.tensor_tensor(actT[:, 1, 0:nb, :, :].rearrange("p b k n -> p (b k n)"), ps_g[:, 0:nb, :, :].rearrange("p b k n -> p (b k n)"),
                                      actT[:, 0, 0:nb, :, :].rearrange("p b k n -> p (b k n)").bitcast(F32), ALU.subtract).then_inc(s["actT"], 1)
                rows_rest(i + 1, 2)
                rows_rest(i + 1, 3)
                rest_of(dve, i + 1, "w1", 0, 1)
                dve.wait_ge(s["out"], i + 1)
                if not is_first(i):
                    dve.wait_ge(s["stored"], 32 * i)
                for b in range(nb):
                    m = dve.tensor_copy(y[:, b, 512:D], ps_y[b][1][:, :])
                m.then_inc(s["y_left"], 1)

            dve.wait_ge(s["cleared"], 3)
            rest_of(dve, 0, "w1", 0, 0)
            rest_of(dve, 0, "w1", 0, 1)
            for r in range(4):
                rows_rest(0, r)
            n = passes(dve)
            each_pass(dve, n, by_blocks(dve, body))


def combine_stage(nc, a, h, gates, scratch, out):
    with ExitStack() as ctx:
        sb = lambda n, s, d=F32: ctx.enter_context(nc.sbuf_tensor(n, s, d))
        s = Signals(nc, ctx, "cb")
        got = [sb(f"expert_rows{i}", [P, TOPK, D]) for i in range(3)]
        junk = sb("junk", [P, D])
        res = [sb(f"result{i}", [P, D]) for i in range(2)]
        g_fin = sb("g_final_sb", [P, D])
        stat = sb("stat4", [P, 2 * NT])
        norm_c = sb("norm_c4", [P, 2, 2])
        block = ctx.enter_context(nc.Block())

        @block.gpsimd
        def _(pool):
            pool.memset(norm_c[:, 0, :], EPS).then_inc(s["norm_c"], 1)
            pool.memset(norm_c[:, 1, :], -0.5).then_inc(s["norm_c"], 1)
            pool.wait_ge(s["norm_c"], 2)

            for t in range(NT):
                pool.wait_ge(s["ss"], t + 1)
                rstd_of(pool, norm_c, stat[:, 2 * t + 1:2 * t + 2], stat[:, 2 * t:2 * t + 1], 1, s["rstd_ms"], s["rstd"], t + 1)

        @block.vector
        def _(dve):
            for t in range(NT):
                dve.wait_ge(s[f"got{t % 3}"], 16 * (t // 3 + 1))
                for j in range(TOPK):
                    if j:
                        dve.wait_ge(s["summed"], TOPK * t + j)
                    dve.scalar_tensor_tensor(h[:, t, :], got[t % 3][:, j, :], gates[:, t, j:j + 1], h[:, t, :],
                                             ALU.mult, ALU.add).then_inc(s["summed"], 1)
                dve.wait_ge(s["rstd"], t + 1)
                dve.wait_ge(s["g_fin"], 16)
                if t >= 2:
                    dve.wait_ge(s[f"stored{t % 2}"], 16 * (t // 2))
                dve.scalar_tensor_tensor(res[t % 2][:, :], h[:, t, :], stat[:, 2 * t + 1:2 * t + 2], g_fin[:, :],
                                         ALU.mult, ALU.mult).then_inc(s["result"], 1)

        @block.scalar
        def _(act):
            for t in range(NT):
                act.wait_ge(s["summed"], TOPK * t + TOPK)
                act.activation(junk[:, :], h[:, t, :], ACT.Square, scale=1 / 32, accum_out=stat[:, 2 * t:2 * t + 1]).then_inc(s["ss"], 1)

        @block.sync
        def _(sp):
            sp.dma_start(g_fin[:, :], a["g_final"].partition_broadcast(P)).then_inc(s["g_fin"], 16)


            def load(t):
                sp.dma_start(got[t % 3][:, :, :], scratch["y"][TOPK * P * t:TOPK * P * (t + 1), :].rearrange(
                    "(p j) d -> p j d", j=TOPK)).then_inc(s[f"got{t % 3}"], 16)

            for t in range(3):
                load(t)
            for t in range(NT):
                if t + 3 < NT:
                    sp.wait_ge(s["summed"], TOPK * (t + 1))
                    load(t + 3)
                sp.wait_ge(s["result"], t + 1)
                sp.dma_start(out[0, P * t:P * t + P, :], res[t % 2][:, :]).then_inc(s[f"stored{t % 2}"], 16)
            for i in range(2):
                sp.wait_ge(s[f"stored{i}"], 16 * NT // 2)


def build_program(nc, a, out):
    with ExitStack() as ctx:
        sb = lambda n, s, d=F32: ctx.enter_context(nc.sbuf_tensor(n, s, d))
        h = sb("h_rows", [P, NT, D])
        gates = sb("gates", [P, NT, TOPK])
        plan_row = sb("plan_row", [1, 4 * (MAX_PASSES + 1)], I32)
        dram = lambda n, s, d=F32: nc.dram_tensor(n, s, d).ap()
        scratch = {
            "bias_rows": dram("bias_rows_dram", [8, P, 3 * P]),
            "rows": dram("moe_rows_dram", [SEQ, D]),
            "slot_table": dram("slot_table_dram", [NE * REGION, 2], I32),
            "plan": dram("plan_dram", [MAX_PASSES + 1, 4], I32),
            "bias_parts": dram("bias_parts_dram", [NE, 3, FF2 + D], BF16),
            "y": dram("expert_y_dram", [SEQ * TOPK, D]),
        }
        mixer_stage(nc, a, h, scratch)
        cross_stage(nc, a, h, gates, plan_row, scratch)
        expert_stage(nc, a, plan_row, scratch)
        combine_stage(nc, a, h, gates, scratch, out)


def shape_constants():
    dist = np.arange(P - 1, -1, -1)
    exact = BUCKETS // 2
    ratio = np.maximum(dist, exact).astype(np.float32) / exact
    large = exact + (np.log(ratio) / math.log(MAX_DIST / exact) * (BUCKETS - exact)).astype(np.int32)
    bucket = np.where(dist < exact, dist, np.minimum(large, BUCKETS - 1))
    return {
        "c_ident": np.eye(P, dtype=np.float32),
        "c_upper": np.triu(np.ones((P, P), np.float32)),
        "c_bucket": (np.arange(BUCKETS)[:, None] == bucket[None, :]).astype(np.float32),
    }


_INS = ["x", "mem", "g_mix", "w_in", "b_qkv", "conv_w", "conv_b", "dt_bias", "a_log", "d_skip", "g_ssm_out",
        "attn_sinks", "rel_bias", "w_out", "b_out", "g_cross", "g_mem", "w_q_cross", "w_kv_cross", "w_o_cross",
        "g_ffn", "w_router", "b_router", "w1", "b1", "w2", "b2", "g_final"]


def kernel(**inputs):
    import concourse.bacc as bacc
    from concourse.bass_utils import run_bass_kernel_spmd

    nc = bacc.Bacc("TRN2", target_bir_lowering=False, num_devices=1)
    arrays, aps = {}, {}
    given = {n: np.ascontiguousarray(inputs[n]) for n in _INS} | shape_constants()
    for name, v in given.items():
        arrays[f"in_{name}"] = v
        aps[name] = nc.dram_tensor(f"in_{name}", v.shape, mybir.dt.from_np(v.dtype), kind="ExternalInput").ap()
    out = nc.dram_tensor("out_rows", (1, SEQ, D), F32, kind="ExternalOutput").ap()
    build_program(nc, aps, out)
    r = run_bass_kernel_spmd(nc, [arrays], core_ids=[0])
    return r.results[0]["out_rows"]
```

```python
from contextlib import ExitStack
import math

import numpy as np
import concourse.bass as bass
from concourse import mybir

F32 = mybir.dt.float32
F32R = mybir.dt.float32r
BF16 = mybir.dt.bfloat16
I32 = mybir.dt.int32
U32 = mybir.dt.uint32
ALU = mybir.AluOpType
ACT = mybir.ActivationFunctionType
AX_X = mybir.AxisListType.X

P = 128
D = 1024
SEQ = 1024
NT = SEQ // P
KD = D // P
MEM = 256
EPS = 1e-5
NEG = -1e30

SH, SP_, SW = 8, 64, 512
CH = 1024
CW = 4
NC_ = CH // P
HD = 64
COL_XBC, COL_DT, COL_Q, COL_K, COL_V = 512, 1536, 1544, 2056, 2184
IN_COLS = 2312
BUCKETS, MAX_DIST = 32, 128

XH, XD = 4, 128
NE, TOPK = 32, 4
FF2 = 2048
ALPHA, LIMIT = 1.702, 7.0
PASS = 256
REGION = 1024
MAX_PASSES = NE + SEQ * TOPK // PASS
FCH = 4
FW = FF2 // FCH
GK = FW // 2 // P


B2_AT = 32
RING = 6


class Signals:

    def __init__(self, nc, ctx, stage):
        self.nc, self.stage, self.made = nc, stage, {}
        ctx.callback(self.give_back)

    def give_back(self):
        self.nc.clear_and_free_semaphores(list(self.made.values()))
        self.nc.all_engine_barrier()

    def __getitem__(self, name):
        if name not in self.made:
            self.made[name] = self.nc.alloc_semaphore(f"{self.stage}_{name}")
        return self.made[name]


def is_first(i):
    return isinstance(i, int) and i == 0


def each_tile(eng, a_tile):
    a_tile(0)
    with eng.Fori(1, NT) as t:
        a_tile(t)


def tiles_ahead(eng, body):
    body(0, True, True)
    with eng.Fori(1, NT - 2) as t:
        body(t, True, True)
    body(NT - 2, True, False)
    body(NT - 1, False, False)


def over_heads(ap, n, width):
    return ap.unsqueeze(2).to_broadcast([P, n, width])


def repeated(ap, n, width):
    return ap.unsqueeze(1).to_broadcast([P, n, width])


def row_bcast(ap, n):
    return ap.partition_broadcast(P)


def rstd_of(pool, consts, out, mean_square, n, step, done, at):
    pool.tensor_tensor(out, mean_square, consts[:, 0, 0:n], ALU.add).then_inc(step, 1)
    pool.wait_ge(step, at)
    pool.tensor_tensor(out, out, consts[:, 1, 0:n], ALU.pow).then_inc(done, 1)


def mixer_stage(nc, a, h, scratch):
    with ExitStack() as ctx:
        sb = lambda n, s, d=F32: ctx.enter_context(nc.sbuf_tensor(n, s, d))
        s = Signals(nc, ctx, "mx")

        w_in = sb("w_in_sb", [P, KD, IN_COLS])
        w_out = sb("w_out_sb", [P, KD, D])
        ident = sb("ident", [P, P])
        upper = sb("upper", [P, P])
        ones = sb("ones", [P, P])
        ident_b = sb("ident_b", [P, P], BF16)
        negmask_b = sb("negmask_b", [P, 4, P], BF16)
        bucket_hot = sb("bucket_hot", [BUCKETS, P])
        rel_bias = sb("rel_bias_sb", [BUCKETS, 8])
        bias = sb("win_bias", [P, 8, 2 * P])
        g_mix = sb("g_mix_sb", [P, KD])
        conv_w = sb("conv_w_sb", [P, CW, NC_])
        conv_b = sb("conv_b_sb", [P, NC_])
        g_ssm = sb("g_ssm_sb", [P, 4])
        b_qkv = sb("b_qkv_sb", [P, 768])
        b_out = sb("b_out_sb", [P, D])
        small = sb("head_rows", [P, 4, 8])
        dt_bias, a_head, d_skip, sinks = (small[:, i, :] for i in range(4))

        row = sb("row", [P, D])
        uT = sb("uT", [P, KD, P])
        zg = sb("zg", [P, SW])
        ext = sb("conv_in", [P, NC_, P + CW - 1])
        cv = sb("conv_out", [P, NC_, P])
        xs = sb("xs_tok", [P, SW])
        bt = sb("b_tok", [P, 2 * P])
        xdt = sb("xdt", [P, SW])
        xw = sb("x_to_end", [P, SW])
        bias_rows = xw[0:8, 0:3 * P]
        decay = sb("decay", [P, SH, P])
        state = sb("state", [P, SW])
        y = sb("y", [P, SW])
        y2 = sb("y2", [P, SW])
        d8 = sb("dt_steps", [P, 14, 8])
        (draw, nabs, ex, w1p, rest, rw, lnw, dt, av, acs, nacs, ea, te, cd) = (d8[:, i, :] for i in range(14))
        stat = sb("stat", [P, 8])
        norm_c = sb("norm_c", [P, 2, 2])
        spare = sb("spare", [P, 4])
        q_tok = sb("q_tok", [P, 4, 2, HD])
        k_tok = sb("k_tok", [P, P])
        qT = sb("qT", [P, 4, P])
        kT = sb("kT", [P, 2, P])
        v = sb("v_tok", [P, 3, P])
        sc = sb("scores", [P, 4, 2 * P])
        pT = sb("probs_t", [P, 2, 4, P])
        sm = sb("softmax", [P, 6, 8])
        prevmask = sb("prevmask", [P, 1])
        catT = pT[:, :, :, :].rearrange("p a c n -> p (a c) n")

        ps = [ctx.enter_context(nc.psum_tensor(f"mx_b{i}", [P, 512], F32)) for i in range(8)]
        block = ctx.enter_context(nc.Block())

        w_in_d = a["w_in"].rearrange("a (k p) n -> p (a k) n", p=P)
        w_out_d = a["w_out"][0]

        @block.sync
        def _(sp):
            sp.dma_start(h[:, 0, :], a["x"][0, 0:P, :]).then_inc(s["x0"], 16)
            sp.dma_start(ident[:, :], a["c_ident"]).then_inc(s["consts"], 16)
            sp.dma_start(upper[:, :], a["c_upper"]).then_inc(s["consts"], 16)
            sp.dma_start(bucket_hot[:, :], a["c_bucket"]).then_inc(s["consts"], 16)
            sp.dma_start(rel_bias[:, :], a["rel_bias"]).then_inc(s["consts"], 16)
            for name, cols in (("xbc0", slice(COL_XBC, COL_XBC + 512)), ("xbc1", slice(COL_XBC + 512, COL_DT)),
                               ("kvq", slice(COL_DT, IN_COLS)), ("z", slice(0, COL_XBC))):
                sp.dma_start(w_in[:, :, cols], w_in_d[:, :, cols]).then_inc(s[f"w_in_{name}"], 16)
                if name == "xbc0":
                    sp.wait_ge(s["rows_in"], 96)
                if name == "xbc1":
                    sp.wait_ge(s["bias_rows"], 1)
                    sp.dma_start(scratch["bias_rows"], bias_rows[:, :].unsqueeze(1).to_broadcast([8, P, 3 * P])).then_inc(s["bias_out"], 16)
            sp.wait_ge(s["bias_out"], 16)
            src = scratch["bias_rows"]
            sp.dma_start(bias[:, :, :], bass.AP(src.tensor, P - 1, [[3 * P - 1, P], [3 * P * P, 8], [1, 2 * P]])).then_inc(s["bias"], 16)
            sp.dma_start(h[:, 1:NT, :], a["x"][0, P:SEQ, :].rearrange("(t p) d -> p t d", p=P)).then_inc(s["x"], 16)
            sp.dma_start(w_out[:, 0:4, :], w_out_d[0:SW, :].rearrange("(k p) n -> p k n", p=P)).then_inc(s["w_out"], 16)
            for g in range(2):
                rows = w_out_d[SW + 256 * g:SW + 256 * (g + 1), :]
                sp.dma_start(w_out[64 * g:64 * g + 64, 4:8, :],
                             rows.rearrange("(j d) n -> d j n", d=HD)).then_inc(s["w_out"], 16)

        @block.gpsimd
        def _(pool):
            pool.memset(kT[:, :, :], 0.0).then_inc(s["cleared"], 1)
            pool.memset(v[:, :, :], 0.0).then_inc(s["cleared"], 1)
            pool.memset(ext[:, :, :], 0.0).then_inc(s["cleared"], 1)
            pool.memset(state[:, :], 0.0).then_inc(s["cleared"], 1)
            pool.memset(ones[:, :], 1.0).then_inc(s["cleared"], 1)
            pool.memset(prevmask[:, :], NEG).then_inc(s["cleared"], 1)
            pool.memset(bias_rows[:, :], NEG).then_inc(s["cleared"], 1)
            pool.memset(norm_c[:, 0, :], EPS).then_inc(s["cleared"], 1)
            pool.memset(norm_c[:, 1, :], -0.5).then_inc(s["cleared"], 1)
            pool.wait_ge(s["cleared"], 9)

            def met(column):
                pool.tensor_tensor(spare[:, column:column + 1], norm_c[:, 0, 0:1], norm_c[:, 0, 0:1], ALU.add)

            def row_rstd(f):
                pool.wait_ge(s["ss"], f + 1)
                rstd_of(pool, norm_c, stat[:, 1:2], stat[:, 0:1], 1, s["rstd_ms"], s["rstd"], f + 1)

            def residual(f):
                pool.wait_ge(s["xn"], f + 1)
                if is_first(f):
                    pool.wait_ge(s["rows_in"], 96)
                hf = h[:, bass.ds(f, 1), :].rearrange("p a d -> p (a d)")
                pool.tensor_tensor(hf, hf, b_out[:, :], ALU.add).then_inc(s["resid"], 1)

            def values_in(f):
                pool.wait_ge(s["kv_out"], 3 * f + 3)
                if not is_first(f):
                    met(3)
                    pool.wait_ge(s["shift"], 3 * f)
                met(2)
                pool.tensor_copy(v[:, 1, :], v[:, 2, :]).then_inc(s["v_cur"], 1)

            def body(t, next_in, norm_in):
                pool.wait_ge(s["av"], t + 1)
                pool.tensor_tensor(decay[:, :, :], over_heads(av, 8, P), repeated(upper[:, :], 8, P),
                                   ALU.mult).then_inc(s["au"], 1)
                if next_in:
                    residual(t + 1)
                pool.wait_ge(s["xdt"], t + 1)
                pool.wait_ge(s["te"], t + 1)
                pool.tensor_tensor(xw[:, :].rearrange("p (h d) -> p h d", h=SH),
                                   xdt[:, :].rearrange("p (h d) -> p h d", h=SH),
                                   over_heads(te, 8, SP_), ALU.mult).then_inc(s["xw"], 1)
                pool.wait_ge(s["oT1"], t + 1)
                met(1)
                pool.tensor_copy(kT[:, 0, :], kT[:, 1, :]).then_inc(s["shift"], 1)
                pool.tensor_copy(v[:, 0, :], v[:, 1, :]).then_inc(s["shift"], 1)
                pool.memset(prevmask[:, :], 0.0).then_inc(s["shift"], 1)
                if next_in:
                    values_in(t + 1)
                pool.wait_ge(s["ssg"], 2 * t + 2)
                rstd_of(pool, norm_c, stat[:, 4:6], stat[:, 2:4], 2, s["rstd_g_ms"], s["rstd_g"], t + 1)
                if norm_in:
                    row_rstd(t + 2)

            row_rstd(0)
            residual(0)
            row_rstd(1)
            values_in(0)
            tiles_ahead(pool, body)

        @block.scalar
        def _(act):
            def small_row(dst, src):
                act.dma_start(dst, src).then_inc(s["rows_in"], 16)
            with nc.allow_non_contiguous_dma("gains on partitions"):
                act.dma_start(g_mix[:, :], a["g_mix"].rearrange("a (k p) -> p (a k)", p=P)).then_inc(s["cols_in"], 16)
                act.dma_start(conv_b[:, :], a["conv_b"].rearrange("a (k p) -> p (a k)", p=P)).then_inc(s["cols_in"], 16)
                act.dma_start(g_ssm[:, :], a["g_ssm_out"].rearrange("a (k p) -> p (a k)", p=P)).then_inc(s["cols_in"], 16)
                for j in range(CW):
                    act.dma_start(conv_w[:, j, :], a["conv_w"][0, j, :].rearrange("(k p) -> p k", p=P)).then_inc(s["cols_in"], 16)
            small_row(b_qkv[:, :], a["b_qkv"][0, :].partition_broadcast(P))
            small_row(b_out[:, :], a["b_out"][0, :].partition_broadcast(P))
            for i, n in enumerate(["dt_bias", "a_log", "d_skip", "attn_sinks"]):
                small_row(small[:, i, :], a[n][0, :].partition_broadcast(P))
            def met():
                act.activation(spare[:, 0:1], ident[:, 0:1], ACT.Copy)

            def norm(f):
                hf = h[:, bass.ds(f, 1), :].rearrange("p a d -> p (a d)")
                if not is_first(f):
                    act.wait_ge(s["xbcT"], 2 * f)
                met()
                act.activation(row[:, :], hf, ACT.Square, scale=1 / 32, accum_out=stat[:, 0:1]).then_inc(s["ss"], 1)
                act.wait_ge(s["rstd"], f + 1)
                met()
                act.activation(row[:, :], hf, ACT.Copy, scale=stat[:, 1:2]).then_inc(s["xn"], 1)

            def xbc_out(f):
                act.wait_ge(s["p_xbc"], 2 * f + 1)
                act.activation(row[:, 0:512], ps[0][:, :], ACT.Copy).then_inc(s["xbc0"], 1)

            def conv_in(f):
                act.wait_ge(s["xbcT"], 2 * f + 1)
                if not is_first(f):
                    act.wait_ge(s["conv"], f)
                act.activation(ext[:, 0:4, CW - 1:], ps[0][:, :].rearrange("p (c n) -> p c n", c=4), ACT.Copy).then_inc(s["ext0"], 1)

            def gate_in(f):
                act.wait_ge(s["p_z"], f + 1)
                if not is_first(f):
                    act.wait_ge(s["yg"], f)
                act.activation(zg[:, :], ps[0][:, :], ACT.Silu).then_inc(s["zg"], 1)

            def body(t, next_in, norm_in):
                act.wait_ge(s["qkT_ps"], t + 1)
                act.activation(qT[:, :, :], ps[7][:, :].rearrange("p (c n) -> p c n", c=4), ACT.Copy).then_inc(s["qT"], 1)
                act.wait_ge(s["nabs"], t + 1)
                act.activation(ex, nabs, ACT.Exp, scale=-1.0).then_inc(s["ex"], 1)
                for g in range(2):
                    act.wait_ge(s["negm"], 2 * t + g + 1)
                    for j in range(4):
                        act.activation(sc[:, j, :], sc[:, j, :], ACT.Exp, bias=sm[:, 1, 4 * g + j:4 * g + j + 1],
                                       accum_out=sm[:, 2, 4 * g + j:4 * g + j + 1]).then_inc(s["pexp"], 1)
                    act.activation(sm[:, 3, 4 * g:4 * g + 4], sm[:, 5, 4 * g:4 * g + 4], ACT.Exp).then_inc(s["sinkexp"], 1)
                    if g == 0:
                        act.wait_ge(s["w1p"], t + 1)
                        act.activation(lnw, w1p, ACT.Ln).then_inc(s["lnw"], 1)
                        if next_in:
                            xbc_out(t + 1)
                    act.wait_ge(s["pT_ps"], 2 * t + g + 1)
                    act.activation(pT[:, 0, :, :], ps[6][:, :].rearrange("p (c n) -> p c n", c=4), ACT.Copy).then_inc(s["pT0"], 1)
                    if g == 0:
                        act.wait_ge(s["acsB"], t + 1)
                        act.wait_ge(s["te_in"], t + 1)
                        act.activation(ea, acs, ACT.Exp).then_inc(s["ea"], 1)
                        act.activation(te, te, ACT.Exp).then_inc(s["te"], 1)
                        act.activation(cd, cd, ACT.Exp).then_inc(s["cd"], 1)
                        for hh in range(8):
                            act.activation(decay[:, hh, :], ps[2 + hh // 4][:, P * (hh % 4):P * (hh % 4) + P], ACT.Exp,
                                           bias=nacs[:, hh:hh + 1]).then_inc(s["decay"], 1)
                    else:
                        act.wait_ge(s["conv"], t + 1)
                        for c in range(NC_):
                            act.activation(cv[:, c, :], cv[:, c, :], ACT.Silu, bias=conv_b[:, c:c + 1]).then_inc(s["cv"], 1)
                act.wait_ge(s["xsbT"], t + 1)
                act.activation(xs[:, :], ps[6][:, :], ACT.Copy).then_inc(s["xs"], 1)
                act.activation(bt[:, :], ps[7][:, 0:256], ACT.Copy).then_inc(s["bt"], 1)
                act.wait_ge(s["oT1"], t + 1)
                act.activation(catT[:, 4:8, :], ps[5][:, :].rearrange("p (c n) -> p c n", c=4), ACT.Copy).then_inc(s["cat1"], 1)
                if next_in:
                    conv_in(t + 1)
                act.wait_ge(s["yg"], t + 1)
                for g in range(2):
                    act.activation(y2[:, 256 * g:256 * g + 256], y[:, 256 * g:256 * g + 256], ACT.Square, scale=1 / 16,
                                   accum_out=stat[:, 2 + g:3 + g]).then_inc(s["ssg"], 1)
                if next_in:
                    gate_in(t + 1)
                if norm_in:
                    norm(t + 2)

            act.wait_ge(s["x0"], 16)
            act.wait_ge(s["consts"], 64)
            norm(0)
            act.wait_ge(s["rows_in"], 96)
            act.activation(a_head, a_head, ACT.Exp).then_inc(s["a_exp"], 1)
            xbc_out(0)
            act.wait_ge(s["cols_in"], 16 * 7)
            conv_in(0)
            act.wait_ge(s["x"], 16)
            norm(1)
            gate_in(0)
            tiles_ahead(act, body)

        @block.tensor
        def _(pe):
            pe.wait_ge(s["consts"], 64)
            pe.matmul(ps[0][0:8, 0:P], rel_bias[:, :], bucket_hot[:, :], start=True, stop=True).then_inc(s["bias_ps"], 1)
            pe.wait_ge(s["bias_rows"], 1)
            pe.wait_ge(s["cleared"], 9)
            pe.wait_ge(s["masks"], 2)

            def row_transposes(f):
                pe.wait_ge(s["xn"], f + 1)
                if not is_first(f):
                    pe.wait_ge(s["zg"], f)
                    pe.wait_ge(s["ext1"], f)
                for k in range(KD):
                    m = pe.transpose(ps[k // 4][:, P * (k % 4):P * (k % 4) + P], row[:, P * k:P * k + P], ident[:, :])
                m.then_inc(s["xnT"], 1)

            def project(dst, cols):
                for k in range(KD):
                    m = pe.matmul(dst, uT[:, k, :], w_in[:, k, cols], start=k == 0, stop=k == KD - 1)
                return m

            def project_xbc(f, n):
                if n == 0:
                    pe.wait_ge(s["uT"], 2 * f + 2)
                if is_first(f):
                    pe.wait_ge(s[f"w_in_xbc{n}"], 16)
                project(ps[n][:, :], slice(COL_XBC + 512 * n, COL_XBC + 512 * n + 512)).then_inc(s["p_xbc"], 1)

            def project_kv(f):
                if is_first(f):
                    pe.wait_ge(s["w_in_kvq"], 16)
                pe.wait_ge(s["xbc0"], f + 1)
                project(ps[0][:, 0:8], slice(COL_DT, COL_Q))
                project(ps[0][:, 8:264], slice(COL_K, IN_COLS)).then_inc(s["p_kv"], 1)

            def project_q(f):
                pe.wait_ge(s["xbc1"], f + 1)
                project(ps[1][:, :], slice(COL_Q, COL_K)).then_inc(s["p_q"], 1)

            def xbc_transposes(f):
                pe.wait_ge(s["kv_out"], 3 * f + 3)
                for k in range(NC_):
                    if k == 4:
                        pe.wait_ge(s["q_tok"], f + 1)
                    m = pe.transpose(ps[k // 4][:, P * (k % 4):P * (k % 4) + P], row[:, P * k:P * k + P], ident[:, :])
                    if k % 4 == 3:
                        m.then_inc(s["xbcT"], 1)

            def project_z(f):
                if is_first(f):
                    pe.wait_ge(s["w_in_z"], 16)
                pe.wait_ge(s["ext0"], f + 1)
                project(ps[0][:, :], slice(0, COL_XBC)).then_inc(s["p_z"], 1)

            def body(t, next_in, norm_in):
                if next_in:
                    row_transposes(t + 1)
                pe.wait_ge(s["q_tok"], t + 1)
                pe.wait_ge(s["kv_out"], 3 * t + 3)
                if not is_first(t):
                    pe.wait_ge(s["h1"], 2 * t)
                for j in range(4):
                    pe.transpose(ps[7][:, P * j:P * j + P], q_tok[:, j, :, :].rearrange("p g d -> p (g d)"), ident[:, :])
                m = pe.transpose(ps[2][:, 0:P], k_tok[:, :], ident[:, :])
                m.then_inc(s["qkT_ps"], 1)
                pe.wait_ge(s["qT"], t + 1)
                pe.wait_ge(s["kT"], t + 1)
                for g in range(2):
                    if g == 1:
                        pe.wait_ge(s["pT1"], 2 * t + 1)
                    for j in range(4):
                        m = pe.matmul(ps[6 + j // 2][:, 256 * (j % 2):256 * (j % 2) + 256], qT[64 * g:64 * g + 64, j, :],
                                      kT[64 * g:64 * g + 64, :, :].rearrange("p a n -> p (a n)"), start=True, stop=True)
                    m.then_inc(s["scores"], 1)
                    if next_in:
                        if g == 0:
                            project_xbc(t + 1, 0)
                        else:
                            project_kv(t + 1)
                    pe.wait_ge(s["probs"], 2 * t + g + 1)
                    for half in range(2):
                        for j in range(4):
                            m = pe.transpose(ps[6 + half][:, P * j:P * j + P], sc[:, j, P * half:P * half + P], ident[:, :])
                    m.then_inc(s["pT_ps"], 1)
                    if g == 0:
                        pe.wait_ge(s["av"], t + 1)
                        pe.matmul(ps[4][:, 0:8], upper[:, :], av, start=True, stop=True).then_inc(s["acs_ps"], 1)
                        pe.wait_ge(s["au"], t + 1)
                        for n in range(2):
                            pe.matmul(ps[2 + n][:, :], ones[:, :], decay[:, 4 * n:4 * n + 4, :].rearrange("p h n -> p (h n)"),
                                      start=True, stop=False)
                            m = pe.matmul(ps[2 + n][:, :], ident_b[:, :], negmask_b[:, :, :].rearrange("p h n -> p (h n)"),
                                          start=False, stop=True)
                        m.then_inc(s["acsB"], 1)
                    if next_in:
                        if g == 0:
                            project_xbc(t + 1, 1)
                        else:
                            project_q(t + 1)
                    pe.wait_ge(s["pT0"], 2 * t + g + 1)
                    pe.wait_ge(s["pT1"], 2 * t + g + 1)
                    if g == 0:
                        pe.wait_ge(s["v_cur"], t + 1)
                    for half in range(2):
                        m = pe.matmul(ps[5][64 * g:64 * g + 64, :], v[:, half, 64 * g:64 * g + 64],
                                      pT[:, half, :, :].rearrange("p c n -> p (c n)"), start=half == 0, stop=half == 1)
                    m.then_inc(s["oT0" if g == 0 else "oT1"], 1)
                pe.wait_ge(s["cv"], 8 * t + 8)
                pe.wait_ge(s["acs"], t + 1)
                for g in range(2):
                    m = pe.matmul(ps[4][:, P + P * g:2 * P + P * g], cv[:, 4 + g, :], cv[:, 6 + g, :], start=True, stop=True)
                m.then_inc(s["cb"], 1)
                for k in range(4):
                    pe.transpose(ps[6][:, P * k:P * k + P], cv[:, k, :], ident[:, :])
                for k in range(2):
                    m = pe.transpose(ps[7][:, P * k:P * k + P], cv[:, 4 + k, :], ident[:, :])
                m.then_inc(s["xsbT"], 1)
                pe.wait_ge(s["decay"], 8 * t + 8)
                if not is_first(t):
                    pe.wait_ge(s["state"], t)
                for g in range(2):
                    m = pe.matmul(ps[3][:, 256 * g:256 * g + 256], cv[:, 6 + g, :], state[:, 256 * g:256 * g + 256],
                                  start=True, stop=True)
                m.then_inc(s["yoff"], 1)
                if next_in:
                    xbc_transposes(t + 1)
                pe.wait_ge(s["mt"], 2 * t + 2)
                pe.wait_ge(s["xdt"], t + 1)
                pe.wait_ge(s["cd"], t + 1)
                for hh in range(SH):
                    m = pe.matmul(ps[2][:, SP_ * hh:SP_ * hh + SP_], decay[:, hh, :], xdt[:, SP_ * hh:SP_ * hh + SP_],
                                  start=True, stop=True)
                m.then_inc(s["ydiag"], 1)
                pe.wait_ge(s["bt"], t + 1)
                pe.wait_ge(s["xw"], t + 1)
                for g in range(2):
                    m = pe.matmul(ps[6][:, 256 * g:256 * g + 256], bt[:, P * g:P * g + P], xw[:, 256 * g:256 * g + 256],
                                  start=True, stop=True)
                m.then_inc(s["st_ps"], 1)
                if next_in:
                    project_z(t + 1)
                pe.wait_ge(s["yn"], t + 1)
                for k in range(4):
                    m = pe.transpose(ps[7][:, P * k:P * k + P], y2[:, P * k:P * k + P], ident[:, :])
                m.then_inc(s["yT_ps"], 1)
                pe.wait_ge(s["cat0"], t + 1)
                pe.wait_ge(s["cat1"], t + 1)
                pe.wait_ge(s["state"], t + 1)
                if is_first(t):
                    pe.wait_ge(s["w_out"], 48)
                for n in range(2):
                    for k in range(KD):
                        m = pe.matmul(ps[6 + n][:, :], catT[:, k, :], w_out[:, k, 512 * n:512 * n + 512],
                                      start=k == 0, stop=k == KD - 1)
                m.then_inc(s["mixed"], 1)

            row_transposes(0)
            project_xbc(0, 0)
            project_xbc(0, 1)
            project_kv(0)
            project_q(0)
            xbc_transposes(0)
            project_z(0)
            tiles_ahead(pe, body)

        @block.vector
        def _(dve):
            dve.wait_ge(s["consts"], 64)
            dve.tensor_copy(ident_b[:, :], ident[:, :]).then_inc(s["masks"], 1)
            dve.tensor_scalar(negmask_b[:, :, :], repeated(upper[:, :], 4, P), -1.0, -NEG, ALU.add, ALU.mult).then_inc(s["masks"], 1)
            dve.wait_ge(s["cleared"], 9)
            dve.wait_ge(s["bias_ps"], 1)
            dve.tensor_copy(bias_rows[:, P:2 * P], ps[0][0:8, 0:P]).then_inc(s["bias_rows"], 1)

            def rows_in(f):
                dve.wait_ge(s["xnT"], f + 1)
                for n in range(2):
                    dve.tensor_tensor(uT[:, 4 * n:4 * n + 4, :], ps[n][:, :].rearrange("p (c n) -> p c n", c=4),
                                      over_heads(g_mix[:, 4 * n:4 * n + 4], 4, P), ALU.mult).then_inc(s["uT"], 1)

            def xbc_out(f):
                dve.wait_ge(s["p_xbc"], 2 * f + 2)
                dve.tensor_copy(row[:, 512:1024], ps[1][:, :]).then_inc(s["xbc1"], 1)

            def keys_out(f):
                dve.wait_ge(s["p_kv"], f + 1)
                dve.tensor_tensor(draw, ps[0][:, 0:8], dt_bias, ALU.add).then_inc(s["kv_out"], 1)
                dve.tensor_tensor(k_tok[:, :], ps[0][:, 8:136], b_qkv[:, 512:640], ALU.add).then_inc(s["kv_out"], 1)
                if not is_first(f):
                    dve.wait_ge(s["v_cur"], f)
                dve.tensor_tensor(v[:, 2, :], ps[0][:, 136:264], b_qkv[:, 640:768], ALU.add).then_inc(s["kv_out"], 1)

            def queries_out(f):
                dve.wait_ge(s["p_q"], f + 1)
                dve.tensor_tensor(q_tok[:, :, :, :].rearrange("p j g d -> p g j d"),
                                  ps[1][:, :].rearrange("p (g j d) -> p g j d", g=2, j=4),
                                  b_qkv[:, 0:512].rearrange("p (g j d) -> p g j d", g=2, j=4), ALU.add).then_inc(s["q_tok"], 1)

            def conv_in(f):
                dve.wait_ge(s["xbcT"], 2 * f + 2)
                dve.tensor_copy(ext[:, 4:8, CW - 1:], ps[1][:, :].rearrange("p (c n) -> p c n", c=4)).then_inc(s["ext1"], 1)

            def taps(t, js):
                if 0 in js:
                    dve.wait_ge(s["ext0"], t + 1)
                    dve.wait_ge(s["ext1"], t + 1)
                for j in js:
                    if j:
                        dve.wait_ge(s["tap"], (CW * NC_) * t + NC_ * j)
                    for c in range(NC_):
                        if j == 0:
                            m = dve.tensor_scalar(cv[:, c, :], ext[:, c, 0:P], conv_w[:, 0, c:c + 1], None, ALU.mult)
                        else:
                            m = dve.scalar_tensor_tensor(cv[:, c, :], ext[:, c, j:j + P], conv_w[:, j, c:c + 1],
                                                         cv[:, c, :], ALU.mult, ALU.add)
                        m.then_inc(s["tap"], 1)

            def softplus(t):
                dve.wait_ge(s["rw"], t + 1)
                dve.tensor_tensor(rest, rest, rw, ALU.mult).then_inc(s["rest2"], 1)
                dve.wait_ge(s["rest2"], t + 1)
                dve.wait_ge(s["lnw"], t + 1)
                dve.tensor_tensor(lnw, lnw, rest, ALU.subtract).then_inc(s["ln1p"], 1)
                dve.wait_ge(s["ln1p"], t + 1)
                dve.scalar_tensor_tensor(dt, draw, 0.0, lnw, ALU.max, ALU.add).then_inc(s["dt"], 1)
                dve.wait_ge(s["dt"], t + 1)
                dve.tensor_tensor(av, dt, a_head, ALU.mult).then_inc(s["av"], 1)

            def body(t, next_in, norm_in):
                if next_in:
                    rows_in(t + 1)
                dve.scalar_tensor_tensor(nabs, draw, -1.0, draw, ALU.mult, ALU.max).then_inc(s["nabs"], 1)
                dve.wait_ge(s["qkT_ps"], t + 1)
                if not is_first(t):
                    dve.wait_ge(s["shift"], 3 * t)
                dve.tensor_copy(kT[:, 1, :], ps[2][:, 0:P]).then_inc(s["kT"], 1)
                dve.wait_ge(s["ex"], t + 1)
                dve.tensor_scalar(w1p, ex, 1.0, None, ALU.add).then_inc(s["w1p"], 1)
                dve.wait_ge(s["w1p"], t + 1)
                dve.scalar_tensor_tensor(rest, w1p, -1.0, ex, ALU.add, ALU.subtract).then_inc(s["rest"], 1)
                dve.reciprocal(rw, w1p).then_inc(s["rw"], 1)
                for g in range(2):
                    dve.wait_ge(s["scores"], 2 * t + g + 1)
                    for n in range(2):
                        dve.scalar_tensor_tensor(sc[:, 2 * n:2 * n + 2, :], ps[6 + n][:, :].rearrange("p (c n) -> p c n", c=2),
                                                 HD ** -0.5, bias[:, 4 * g + 2 * n:4 * g + 2 * n + 2, :],
                                                 ALU.mult, ALU.add).then_inc(s["sc"], 1)
                    dve.wait_ge(s["sc"], 4 * t + 2 * g + 2)
                    dve.tensor_scalar(sc[:, :, 0:P], sc[:, :, 0:P], prevmask[:, 0:1], None, ALU.add).then_inc(s["scm"], 1)
                    dve.wait_ge(s["scm"], 2 * t + g + 1)
                    hs = slice(4 * g, 4 * g + 4)
                    dve.tensor_reduce(sm[:, 0, hs], sc[:, :, :], AX_X, ALU.max).then_inc(s["smax"], 1)
                    dve.wait_ge(s["smax"], 2 * t + g + 1)
                    dve.tensor_tensor(sm[:, 0, hs], sm[:, 0, hs], sinks[:, hs], ALU.max).then_inc(s["smax2"], 1)
                    dve.wait_ge(s["smax2"], 2 * t + g + 1)
                    dve.tensor_tensor(sm[:, 5, hs], sinks[:, hs], sm[:, 0, hs], ALU.subtract).then_inc(s["sinkd"], 1)
                    dve.wait_ge(s["sinkd"], 2 * t + g + 1)
                    dve.tensor_scalar(sm[:, 1, hs], sm[:, 0, hs], -1.0, None, ALU.mult).then_inc(s["negm"], 1)
                    if g == 0:
                        taps(t, [0])
                    elif next_in:
                        keys_out(t + 1)
                    dve.wait_ge(s["pexp"], 8 * t + 4 * g + 4)
                    dve.wait_ge(s["sinkexp"], 2 * t + g + 1)
                    dve.tensor_tensor(sm[:, 4, hs], sm[:, 2, hs], sm[:, 3, hs], ALU.add).then_inc(s["den"], 1)
                    dve.wait_ge(s["den"], 2 * t + g + 1)
                    dve.reciprocal(sm[:, 4, hs], sm[:, 4, hs]).then_inc(s["rden"], 1)
                    dve.wait_ge(s["rden"], 2 * t + g + 1)
                    dve.tensor_tensor(sc[:, :, :], sc[:, :, :], over_heads(sm[:, 4, hs], 4, 2 * P), ALU.mult).then_inc(s["probs"], 1)
                    if g == 0:
                        softplus(t)
                        taps(t, [1])
                    dve.wait_ge(s["pT_ps"], 2 * t + g + 1)
                    dve.tensor_copy(pT[:, 1, :, :], ps[7][:, :].rearrange("p (c n) -> p c n", c=4)).then_inc(s["pT1"], 1)
                    if g == 0:
                        dve.wait_ge(s["acs_ps"], t + 1)
                        dve.tensor_copy(acs, ps[4][:, 0:8]).then_inc(s["acs"], 1)
                        dve.wait_ge(s["acs"], t + 1)
                        dve.tensor_scalar(nacs, acs, -1.0, None, ALU.mult).then_inc(s["nacs"], 1)
                        dve.wait_ge(s["acsB"], t + 1)
                        dve.wait_ge(s["nacs"], t + 1)
                        dve.tensor_copy(cd[:, 0:4], ps[2][:, P - 1::P]).then_inc(s["last"], 1)
                        dve.tensor_copy(cd[:, 4:8], ps[3][:, P - 1::P]).then_inc(s["last"], 1)
                        dve.wait_ge(s["last"], 2 * t + 2)
                        dve.tensor_tensor(te, cd, nacs, ALU.add).then_inc(s["te_in"], 1)
                        taps(t, [2, 3])
                        dve.wait_ge(s["tap"], (CW * NC_) * t + CW * NC_)
                        dve.tensor_copy(ext[:, :, 0:CW - 1], ext[:, :, P:P + CW - 1]).then_inc(s["conv"], 1)
                        if next_in:
                            xbc_out(t + 1)
                dve.wait_ge(s["cb"], t + 1)
                for g in range(2):
                    dve.tensor_tensor(decay[:, 4 * g:4 * g + 4, :], decay[:, 4 * g:4 * g + 4, :],
                                      repeated(ps[4][:, P + P * g:2 * P + P * g], 4, P), ALU.mult).then_inc(s["mt"], 1)
                if next_in:
                    queries_out(t + 1)
                dve.wait_ge(s["xs"], t + 1)
                hd = lambda ap: ap.rearrange("p (h d) -> p h d", h=SH)
                dve.tensor_tensor(hd(xdt[:, :]), hd(xs[:, :]), over_heads(dt, 8, SP_), ALU.mult).then_inc(s["xdt"], 1)
                dve.tensor_tensor(hd(xs[:, :]), hd(xs[:, :]), over_heads(d_skip, 8, SP_), ALU.mult).then_inc(s["skip"], 1)
                if next_in:
                    conv_in(t + 1)
                dve.wait_ge(s["yoff"], t + 1)
                dve.wait_ge(s["ea"], t + 1)
                dve.tensor_tensor(hd(y[:, :]), hd(ps[3][:, :]), over_heads(ea, 8, SP_), ALU.mult).then_inc(s["y0"], 1)
                dve.wait_ge(s["y0"], t + 1)
                dve.wait_ge(s["skip"], t + 1)
                dve.tensor_tensor(y[:, :], y[:, :], xs[:, :], ALU.add).then_inc(s["y1"], 1)
                dve.wait_ge(s["y1"], t + 1)
                dve.wait_ge(s["ydiag"], t + 1)
                dve.tensor_tensor(y[:, :], y[:, :], ps[2][:, :], ALU.add).then_inc(s["y2"], 1)
                dve.wait_ge(s["y2"], t + 1)
                dve.tensor_tensor(y[:, :], y[:, :], zg[:, :], ALU.mult).then_inc(s["yg"], 1)
                dve.wait_ge(s["cd"], t + 1)
                dve.tensor_tensor(hd(state[:, :]), hd(state[:, :]), over_heads(cd, 8, SP_), ALU.mult).then_inc(s["st_dec"], 1)
                dve.wait_ge(s["st_dec"], t + 1)
                dve.wait_ge(s["st_ps"], t + 1)
                dve.tensor_tensor(state[:, :], state[:, :], ps[6][:, :], ALU.add).then_inc(s["state"], 1)
                dve.wait_ge(s["rstd_g"], t + 1)
                dve.tensor_tensor(y2[:, :].rearrange("p (g n) -> p g n", g=2), y[:, :].rearrange("p (g n) -> p g n", g=2),
                                  over_heads(stat[:, 4:6], 2, 256), ALU.mult).then_inc(s["yn"], 1)
                dve.wait_ge(s["yT_ps"], t + 1)
                dve.tensor_tensor(catT[:, 0:4, :], ps[7][:, :].rearrange("p (c n) -> p c n", c=4),
                                  over_heads(g_ssm[:, :], 4, P), ALU.mult).then_inc(s["cat0"], 1)
                dve.wait_ge(s["mixed"], t + 1)
                dve.wait_ge(s["resid"], t + 1)
                for n in range(2):
                    hn = h[:, bass.ds(t, 1), 512 * n:512 * n + 512].rearrange("p a d -> p (a d)")
                    dve.tensor_tensor(hn, ps[6 + n][:, :], hn, ALU.add).then_inc(s["h1"], 1)

            dve.wait_ge(s["cols_in"], 16 * 7)
            rows_in(0)
            dve.wait_ge(s["a_exp"], 1)
            dve.tensor_scalar(a_head, a_head, -1.0, None, ALU.mult).then_inc(s["a_head"], 1)
            xbc_out(0)
            keys_out(0)
            queries_out(0)
            conv_in(0)
            dve.wait_ge(s["bias"], 16)
            tiles_ahead(dve, body)


def cross_stage(nc, a, h, gates, plan_row, scratch):
    with ExitStack() as ctx:
        sb = lambda n, s, d=F32: ctx.enter_context(nc.sbuf_tensor(n, s, d))
        s = Signals(nc, ctx, "cx")
        w_kv = sb("w_kv_sb", [P, KD, 2 * XH * XD])
        w_q = sb("w_q_sb", [P, KD, XH * XD])
        w_o = sb("w_o_sb", [P, XH, D])
        w_r = sb("w_router_sb", [P, KD, NE])
        ident = sb("ident2", [P, P])
        upper = sb("upper2", [P, P])
        before_b = sb("before_b", [P, P], BF16)
        ones_b = sb("ones_b", [P, P], BF16)
        gains = sb("gains", [P, 2, KD])
        g_ffn = sb("g_ffn_sb", [P, D])
        b_r = sb("b_router_sb", [P, NE])
        iota_e = sb("iota_e", [P, NE])
        entry = sb("slot_entries", [P, NT, TOPK, 2], I32)
        slots = sb("slots", [P, NT, TOPK], I32)
        zero_slots = sb("zero_slots", [P, NE * REGION // P, 2], I32)

        mem = sb("mem_rows", [P, 2, D])
        memT = sb("memT", [P, KD, MEM])
        kxT = sb("kxT", [P, XH, MEM])
        vx = sb("vx", [P, 2, XH * XD])
        stat = sb("stat2", [P, 12])
        norm_c = sb("norm_c2", [P, 2, 2])
        spare = sb("spare2", [P, 4])
        xn = sb("xn", [P, D])
        uT = sb("uT2", [P, KD, P])
        rT = sb("moe_rows_t", [P, KD, P])
        q_tok = sb("qx_tok", [P, XH * XD])
        qT = sb("qxT", [P, XH, P])
        pr = sb("px", [P, XH, MEM])
        pT = sb("pxT", [P, 2, XH, P])
        oT = sb("oxT", [P, XH, P])
        sm = sb("softmax2", [P, 4, XH])
        rows = sb("moe_rows", [P, D])
        lg = sb("logits", [P, NE])
        mx = sb("top8", [P, 8])
        ix = sb("top8_index", [P, 8], U32)
        ixf = sb("top_index", [P, TOPK])
        ge = sb("gate_exp", [P, TOPK])
        hot = sb("chosen", [P, TOPK, NE])
        picked = sb("picked", [P, TOPK, NE])
        mask = sb("mask", [P, NE])
        mask_b = sb("mask_b", [P, NE], BF16)
        carry = sb("carry", [P, NE])
        rank = sb("rank", [P, NE])
        rank4 = sb("rank4", [P, TOPK])
        slot_f = sb("slot_f", [P, TOPK])
        pl = sb("plan_work", [P, 8, NE])
        (c_up, n_pass, n_cum, before, tmp, e_hot) = (pl[:, i, :] for i in range(6))
        pi = sb("plan_int", [P, NE], I32)
        ones_e = sb("ones_e", [P, NE])
        iota_i = sb("iota_i", [P, 1])
        pv = sb("plan_values", [P, 12])
        plan = sb("plan", [P, 4], I32)

        bias_all = sb("bias_all", [NE, FF2 + D])
        bias_parts = sb("bias_parts", [NE, 3, FF2 + D], BF16)

        ps = [ctx.enter_context(nc.psum_tensor(f"cx_b{i}", [P, 512], F32)) for i in range(8)]
        block = ctx.enter_context(nc.Block())
        c4 = lambda ap: ap.rearrange("p (c n) -> p c n", c=4)
        tile_of = lambda t: h[:, bass.ds(t, 1), :].rearrange("p a d -> p (a d)")

        @block.sync
        def _(sp):
            sp.dma_start(ident[:, :], a["c_ident"]).then_inc(s["consts"], 16)
            sp.dma_start(upper[:, :], a["c_upper"]).then_inc(s["consts"], 16)
            sp.dma_start(mem[:, :, :], a["mem"][0].rearrange("(m p) d -> p m d", p=P)).then_inc(s["mem"], 16)
            with nc.allow_non_contiguous_dma("gains on partitions"):
                for i, n in enumerate(["g_mem", "g_cross"]):
                    sp.dma_start(gains[:, i, :], a[n].rearrange("a (k p) -> p (a k)", p=P)).then_inc(s["gains"], 16)
            w_kv_d = a["w_kv_cross"][0].rearrange("(k p) n -> p k n", p=P)
            for i in range(2):
                cols = slice(XH * XD * i, XH * XD * (i + 1))
                sp.dma_start(w_kv[:, :, cols], w_kv_d[:, :, cols]).then_inc(s[f"w_kv{i}"], 16)
            sp.dma_start(w_q[:, :, :], a["w_q_cross"][0].rearrange("(k p) n -> p k n", p=P)).then_inc(s["w_q"], 16)
            sp.dma_start(w_o[:, :, :], a["w_o_cross"][0].rearrange("(k p) n -> p k n", p=P)).then_inc(s["w_o"], 16)
            with nc.allow_non_contiguous_dma("32 columns a row"):
                sp.dma_start(w_r[:, :, :], a["w_router"][0].rearrange("(k p) n -> p k n", p=P)).then_inc(s["w_r"], 16)
            sp.dma_start(g_ffn[:, :], a["g_ffn"][0, :].partition_broadcast(P)).then_inc(s["w_r"], 16)
            sp.dma_start(b_r[:, :], a["b_router"][0, :].partition_broadcast(P)).then_inc(s["w_r"], 16)
            sp.dma_start(bias_all[:, 0:FF2], a["b1"][0]).then_inc(s["bias_all"], 16)
            sp.dma_start(bias_all[:, FF2:], a["b2"][0]).then_inc(s["bias_all"], 16)
            sp.wait_ge(s["bias_parts"], 5)
            sp.dma_start(scratch["bias_parts"].rearrange("e j n -> e (j n)"), bias_parts[:, :, :].rearrange("e j n -> e (j n)")).then_inc(s["parts_out"], 16)
            def a_tile(t):
                sp.wait_ge(s["h2"], 2 * t + 2)
                sp.dma_start(scratch["h"][bass.ds(t * P, P), :], tile_of(t)).then_inc(s["h_out"], 16)
                sp.wait_ge(s["rows"], t + 1)
                sp.dma_start(scratch["rows"][bass.ds(t * P, P), :], rows[:, :]).then_inc(s["rows_out"], 16)
            each_tile(sp, a_tile)
            sp.wait_ge(s["rows_out"], 16 * NT)
            sp.wait_ge(s["h_out"], 16 * NT)
            sp.wait_ge(s["parts_out"], 16)
            sp.wait_ge(s["plan"], 4)
            sp.dma_start(scratch["plan"], plan[0:MAX_PASSES + 1, :]).then_inc(s["plan_out"], 16)
            sp.wait_ge(s["plan_out"], 16)
            sp.dma_start(plan_row[0:1, :], scratch["plan"].rearrange("(a p) c -> a (p c)", a=1)).then_inc(s["plan_in"], 16)
            sp.wait_ge(s["plan_in"], 16)

        @block.gpsimd
        def _(pool):
            pool.memset(zero_slots[:, :, 0:1], SEQ).then_inc(s["setup"], 1)
            pool.memset(zero_slots[:, :, 1:2], SEQ * TOPK).then_inc(s["setup"], 1)
            pool.memset(ones_b[:, :], 1.0).then_inc(s["setup"], 1)
            pool.memset(ones_e[:, :], 1.0).then_inc(s["setup"], 1)
            pool.memset(carry[:, :], 0.0).then_inc(s["setup"], 1)
            pool.iota(iota_e[:, :], [[1, NE]], base=0, channel_multiplier=0, allow_small_or_imprecise_dtypes=True).then_inc(s["setup"], 1)
            pool.iota(iota_i[:, :], [[0, 1]], base=0, channel_multiplier=1, allow_small_or_imprecise_dtypes=True).then_inc(s["setup"], 1)
            pool.iota(entry[:, :, :, 0], [[P, NT], [0, TOPK]], base=0, channel_multiplier=1).then_inc(s["setup"], 1)
            pool.iota(entry[:, :, :, 1], [[TOPK * P, NT], [1, TOPK]], base=0, channel_multiplier=TOPK).then_inc(s["setup"], 1)
            pool.memset(norm_c[:, 0, :], EPS).then_inc(s["setup"], 1)
            pool.memset(norm_c[:, 1, :], -0.5).then_inc(s["setup"], 1)
            pool.wait_ge(s["setup"], 11)
            pool.dma_start(scratch["slot_table"].rearrange("(p f) a -> p (f a)", p=P), zero_slots[:, :, :].rearrange("p f a -> p (f a)")).then_inc(s["table_clear"], 16)
            pool.wait_ge(s["mem_ss"], 2)
            rstd_of(pool, norm_c, stat[:, 2:4], stat[:, 0:2], 2, s["mem_rstd_ms"], s["mem_rstd"], 1)
            pool.wait_ge(s["table_clear"], 16)

            def row_rstd(f):
                pool.wait_ge(s["ss"], f + 1)
                rstd_of(pool, norm_c, stat[:, 5:6], stat[:, 4:5], 1, s["rstd_ms"], s["rstd"], f + 1)

            def enter(t):
                pool.wait_ge(s["slots"], t + 1)
                for j in range(TOPK):
                    pool.indirect_dma_start(scratch["slot_table"], bass.IndirectOffsetOnAxis(ap=slots[:, t, j:j + 1], axis=0),
                                            entry[:, t, j, :], None).then_inc(s["table"], 16)

            row_rstd(0)
            row_rstd(1)
            for t in range(NT):
                pool.wait_ge(s["ss2"], t + 1)
                rstd_of(pool, norm_c, stat[:, 7:8], stat[:, 6:7], 1, s["rstd2_ms"], s["rstd2"], t + 1)
                if t + 2 < NT:
                    row_rstd(t + 2)
                if t:
                    enter(t - 1)
            enter(NT - 1)
            pool.wait_ge(s["table"], 16 * NT * TOPK)

        @block.scalar
        def _(act):
            act.wait_ge(s["mem"], 16)
            for m in range(2):
                act.activation((xn, rows)[m][:, :], mem[:, m, :], ACT.Square, scale=1 / 32, accum_out=stat[:, m:m + 1]).then_inc(s["mem_ss"], 1)
            act.wait_ge(s["mem_rstd"], 1)
            for m in range(2):
                act.activation(mem[:, m, :], mem[:, m, :], ACT.Copy, scale=stat[:, 2 + m:3 + m]).then_inc(s["mem_n"], 1)
            act.wait_ge(s["kx_ps"], 1)
            for n in range(2):
                act.activation(kxT[:, 2 * n:2 * n + 2, :], ps[2 + n][:, :].rearrange("p (c n) -> p c n", c=2), ACT.Copy).then_inc(s["kxT"], 1)
            def met(column=0):
                act.activation(spare[:, column:column + 1], ident[:, 0:1], ACT.Copy)

            def norm(f):
                if not is_first(f):
                    act.wait_ge(s["xnT"], f)
                met()
                act.activation(xn[:, :], tile_of(f), ACT.Square, scale=1 / 32, accum_out=stat[:, 4:5]).then_inc(s["ss"], 1)
                act.wait_ge(s["rstd"], f + 1)
                met()
                act.activation(xn[:, :], tile_of(f), ACT.Copy, scale=stat[:, 5:6]).then_inc(s["xn"], 1)

            def queries(f):
                act.wait_ge(s["q_ps"], f + 1)
                act.activation(q_tok[:, :], ps[2][:, :], ACT.Copy).then_inc(s["q_tok"], 1)
                act.wait_ge(s["qT_ps"], f + 1)
                act.activation(qT[:, :, :], c4(ps[3][:, :]), ACT.Copy).then_inc(s["qT"], 1)

            def exps(f):
                act.wait_ge(s["negm"], f + 1)
                for j in range(XH):
                    act.activation(pr[:, j, :], ps[4 + j // 2][:, MEM * (j % 2):MEM * (j % 2) + MEM], ACT.Exp, scale=XD ** -0.5,
                                   bias=sm[:, 1, j:j + 1], accum_out=sm[:, 2, j:j + 1]).then_inc(s["pexp"], 1)

            def probs_out(f):
                act.wait_ge(s["pT_ps"], f + 1)
                act.activation(pT[:, 0, :, :], c4(ps[0][:, :]), ACT.Copy).then_inc(s["pT0"], 1)

            def heads_out(f):
                act.wait_ge(s["oT_ps"], f + 1)
                act.activation(oT[:, :, :], c4(ps[2][:, :]), ACT.Copy).then_inc(s["oT"], 1)

            def body(t, next_in, norm_in):
                act.wait_ge(s["h2"], 2 * t + 2)
                if not is_first(t):
                    act.wait_ge(s["rows_out"], 16 * t)
                met(2)
                act.activation(rows[:, :], tile_of(t), ACT.Square, scale=1 / 32, accum_out=stat[:, 6:7]).then_inc(s["ss2"], 1)
                if norm_in:
                    norm(t + 2)
                if next_in:
                    queries(t + 1)
                    exps(t + 1)
                act.wait_ge(s["neg1"], t + 1)
                act.activation(ge[:, :], mx[:, 0:TOPK], ACT.Exp, bias=stat[:, 8:9], accum_out=stat[:, 9:10]).then_inc(s["ge"], 1)
                if next_in:
                    probs_out(t + 1)
                    heads_out(t + 1)

            norm(0)
            norm(1)
            queries(0)
            exps(0)
            probs_out(0)
            heads_out(0)
            tiles_ahead(act, body)

        @block.tensor
        def _(pe):
            pe.wait_ge(s["consts"], 32)
            pe.wait_ge(s["mem_n"], 2)
            for m in range(2):
                for n in range(2):
                    for k in range(4):
                        i = 4 * n + k
                        tr = pe.transpose(ps[2 * m + n][:, P * k:P * k + P], mem[:, m, P * i:P * i + P], ident[:, :])
            tr.then_inc(s["memT_ps"], 1)
            pe.wait_ge(s["memT"], 4)
            pe.wait_ge(s["w_kv0"], 16)
            for j in range(XH):
                for k in range(KD):
                    m = pe.matmul(ps[2 + j // 2][:, MEM * (j % 2):MEM * (j % 2) + MEM], w_kv[:, k, XD * j:XD * j + XD], memT[:, k, :],
                                  start=k == 0, stop=k == KD - 1)
            m.then_inc(s["kx_ps"], 1)
            pe.wait_ge(s["w_kv1"], 16)
            for half in range(2):
                for k in range(KD):
                    m = pe.matmul(ps[4 + half][:, :], memT[:, k, P * half:P * half + P], w_kv[:, k, XH * XD:],
                                  start=k == 0, stop=k == KD - 1)
            m.then_inc(s["vx_ps"], 1)
            pe.wait_ge(s["kxT"], 2)
            pe.wait_ge(s["vx"], 2)
            pe.wait_ge(s["setup"], 11)
            pe.wait_ge(s["before"], 1)

            def row_transposes(f):
                pe.wait_ge(s["xn"], f + 1)
                if not is_first(f):
                    pe.wait_ge(s["pT0"], f)
                    pe.wait_ge(s["pT1"], f)
                for k in range(KD):
                    m = pe.transpose(ps[k // 4][:, P * (k % 4):P * (k % 4) + P], xn[:, P * k:P * k + P], ident[:, :])
                m.then_inc(s["xnT"], 1)

            def queries(f):
                pe.wait_ge(s["uT"], 2 * f + 2)
                if is_first(f):
                    pe.wait_ge(s["w_q"], 16)
                for k in range(KD):
                    m = pe.matmul(ps[2][:, :], uT[:, k, :], w_q[:, k, :], start=k == 0, stop=k == KD - 1)
                m.then_inc(s["q_ps"], 1)

            def scores(f):
                pe.wait_ge(s["q_tok"], f + 1)
                for k in range(XH):
                    m = pe.transpose(ps[3][:, P * k:P * k + P], q_tok[:, P * k:P * k + P], ident[:, :])
                m.then_inc(s["qT_ps"], 1)
                pe.wait_ge(s["qT"], f + 1)
                if not is_first(f):
                    pe.wait_ge(s["h2"], 2 * f)
                for j in range(XH):
                    m = pe.matmul(ps[4 + j // 2][:, MEM * (j % 2):MEM * (j % 2) + MEM], qT[:, j, :], kxT[:, j, :], start=True, stop=True)
                m.then_inc(s["scores"], 1)

            def prob_transposes(f):
                pe.wait_ge(s["probs"], f + 1)
                for half in range(2):
                    for j in range(XH):
                        m = pe.transpose(ps[half][:, P * j:P * j + P], pr[:, j, P * half:P * half + P], ident[:, :])
                m.then_inc(s["pT_ps"], 1)

            def heads(f):
                pe.wait_ge(s["pT0"], f + 1)
                pe.wait_ge(s["pT1"], f + 1)
                for j in range(XH):
                    for half in range(2):
                        m = pe.matmul(ps[2][:, P * j:P * j + P], vx[:, half, XD * j:XD * j + XD], pT[:, half, j, :],
                                      start=half == 0, stop=half == 1)
                m.then_inc(s["oT_ps"], 1)

            def project_out(f):
                pe.wait_ge(s["oT"], f + 1)
                if is_first(f):
                    pe.wait_ge(s["w_o"], 16)
                for n in range(2):
                    for k in range(XH):
                        m = pe.matmul(ps[4 + n][:, :], oT[:, k, :], w_o[:, k, 512 * n:512 * n + 512], start=k == 0, stop=k == XH - 1)
                m.then_inc(s["o_ps"], 1)

            def body(t, next_in, norm_in):
                if next_in:
                    queries(t + 1)
                for n in range(2):
                    if n == 0:
                        pe.wait_ge(s["rows"], t + 1)
                    if n or not is_first(t):
                        pe.wait_ge(s["rT"], 2 * t + n)
                    for k in range(4):
                        m = pe.transpose(ps[6][:, P * k:P * k + P], rows[:, P * (4 * n + k):P * (4 * n + k) + P], ident[:, :])
                    m.then_inc(s["rowsT"], 1)
                    if n == 0 and next_in:
                        scores(t + 1)
                pe.wait_ge(s["rT"], 2 * t + 2)
                if is_first(t):
                    pe.wait_ge(s["w_r"], 48)
                else:
                    pe.wait_ge(s["carry"], t)
                for k in range(KD):
                    m = pe.matmul(ps[7][:, 0:NE], rT[:, k, :], w_r[:, k, :], start=k == 0, stop=k == KD - 1)
                m.then_inc(s["lg_ps"], 1)
                if next_in:
                    prob_transposes(t + 1)
                pe.wait_ge(s["mask_b"], t + 1)
                pe.matmul(ps[7][:, NE:2 * NE], before_b[:, :], mask_b[:, :], start=True, stop=True).then_inc(s["rank_ps"], 1)
                pe.matmul(ps[7][:, 2 * NE:3 * NE], ones_b[:, :], mask_b[:, :], start=True, stop=True).then_inc(s["count_ps"], 1)
                if next_in:
                    heads(t + 1)
                    if norm_in:
                        row_transposes(t + 2)
                    project_out(t + 1)

            row_transposes(0)
            queries(0)
            scores(0)
            prob_transposes(0)
            heads(0)
            row_transposes(1)
            project_out(0)
            tiles_ahead(pe, body)

        @block.vector
        def _(dve):
            dve.wait_ge(s["consts"], 32)
            dve.tensor_tensor(before_b[:, :], upper[:, :], ident[:, :], ALU.subtract).then_inc(s["before"], 1)
            dve.wait_ge(s["memT_ps"], 1)
            dve.wait_ge(s["gains"], 32)
            for m in range(2):
                for n in range(2):
                    dve.tensor_tensor(memT[:, 4 * n:4 * n + 4, P * m:P * m + P], c4(ps[2 * m + n][:, :]),
                                      over_heads(gains[:, 0, 4 * n:4 * n + 4], 4, P), ALU.mult).then_inc(s["memT"], 1)
            dve.wait_ge(s["bias_all"], 32)
            dve.tensor_copy(bias_parts[:, 0, :], bias_all[:, :]).then_inc(s["bias_parts"], 1)
            for j in range(1, 3):
                dve.wait_ge(s["bias_parts"], 2 * j - 1)
                dve.tensor_tensor(bias_all[:, :], bias_all[:, :], bias_parts[:, j - 1, :],
                                  ALU.subtract).then_inc(s["bias_parts"], 1)
                dve.wait_ge(s["bias_parts"], 2 * j)
                dve.tensor_copy(bias_parts[:, j, :], bias_all[:, :]).then_inc(s["bias_parts"], 1)
            dve.wait_ge(s["vx_ps"], 1)
            for half in range(2):
                dve.tensor_copy(vx[:, half, :], ps[4 + half][:, :]).then_inc(s["vx"], 1)
            dve.wait_ge(s["setup"], 11)
            dve.wait_ge(s["w_r"], 48)
            def met():
                dve.memset(spare[:, 1:2], 0.0)

            def rows_in(f):
                dve.wait_ge(s["xnT"], f + 1)
                for n in range(2):
                    dve.tensor_tensor(uT[:, 4 * n:4 * n + 4, :], c4(ps[n][:, :]), over_heads(gains[:, 1, 4 * n:4 * n + 4], 4, P),
                                      ALU.mult).then_inc(s["uT"], 1)

            def maxima(f):
                dve.wait_ge(s["scores"], f + 1)
                for n in range(2):
                    dve.tensor_reduce(sm[:, 0, 2 * n:2 * n + 2], ps[4 + n][:, :].rearrange("p (c n) -> p c n", c=2), AX_X,
                                      ALU.max).then_inc(s["smax"], 1)
                dve.wait_ge(s["smax"], 2 * f + 2)
                dve.tensor_scalar(sm[:, 1, :], sm[:, 0, :], -XD ** -0.5, None, ALU.mult).then_inc(s["negm"], 1)

            def normalised(f):
                dve.wait_ge(s["pexp"], 4 * f + 4)
                dve.reciprocal(sm[:, 3, :], sm[:, 2, :]).then_inc(s["rden"], 1)
                dve.wait_ge(s["rden"], f + 1)
                dve.tensor_tensor(pr[:, :, :], pr[:, :, :], over_heads(sm[:, 3, :], 4, MEM), ALU.mult).then_inc(s["probs"], 1)

            def probs_out(f):
                dve.wait_ge(s["pT_ps"], f + 1)
                dve.tensor_copy(pT[:, 1, :, :], c4(ps[1][:, :])).then_inc(s["pT1"], 1)

            def residual(f):
                dve.wait_ge(s["o_ps"], f + 1)
                for n in range(2):
                    hn = h[:, bass.ds(f, 1), 512 * n:512 * n + 512].rearrange("p a d -> p (a d)")
                    dve.tensor_tensor(hn, ps[4 + n][:, :], hn, ALU.add).then_inc(s["h2"], 1)

            def body(t, next_in, norm_in):
                dve.wait_ge(s["rstd2"], t + 1)
                dve.scalar_tensor_tensor(rows[:, :], tile_of(t), stat[:, 7:8], g_ffn[:, :], ALU.mult, ALU.mult).then_inc(s["rows"], 1)
                dve.wait_ge(s["rowsT"], 2 * t + 1)
                dve.tensor_copy(rT[:, 0:4, :], c4(ps[6][:, :])).then_inc(s["rT"], 1)
                if next_in:
                    maxima(t + 1)
                dve.wait_ge(s["rowsT"], 2 * t + 2)
                dve.tensor_copy(rT[:, 4:8, :], c4(ps[6][:, :])).then_inc(s["rT"], 1)
                dve.wait_ge(s["lg_ps"], t + 1)
                dve.tensor_tensor(lg[:, :], ps[7][:, 0:NE], b_r[:, :], ALU.add).then_inc(s["lg"], 1)
                dve.wait_ge(s["lg"], t + 1)
                met()
                dve.max(mx[:, :], lg[:, :]).then_inc(s["mx"], 1)
                dve.wait_ge(s["mx"], t + 1)
                dve.tensor_scalar(stat[:, 8:9], mx[:, 0:1], -1.0, None, ALU.mult).then_inc(s["neg1"], 1)
                dve.max_index(ix[:, :], mx[:, :], lg[:, :]).then_inc(s["ix"], 1)
                if next_in:
                    normalised(t + 1)
                dve.wait_ge(s["ix"], t + 1)
                dve.tensor_copy(ixf[:, :], ix[:, 0:TOPK]).then_inc(s["ixf"], 1)
                dve.wait_ge(s["ixf"], t + 1)
                dve.tensor_tensor(hot[:, :, :], repeated(iota_e[:, :], TOPK, NE), over_heads(ixf[:, :], TOPK, NE),
                                  ALU.is_equal).then_inc(s["hot"], 1)
                dve.wait_ge(s["hot"], t + 1)
                dve.tensor_reduce(mask[:, :], hot[:, :, :].rearrange("p j e -> p e j"), AX_X, ALU.add).then_inc(s["mask"], 1)
                dve.wait_ge(s["mask"], t + 1)
                dve.tensor_copy(mask_b[:, :], mask[:, :]).then_inc(s["mask_b"], 1)
                if next_in:
                    probs_out(t + 1)
                dve.wait_ge(s["ge"], t + 1)
                dve.reciprocal(stat[:, 10:11], stat[:, 9:10]).then_inc(s["rge"], 1)
                dve.wait_ge(s["rge"], t + 1)
                dve.tensor_scalar(gates[:, bass.ds(t, 1), :].rearrange("p a j -> p (a j)"), ge[:, :], stat[:, 10:11], None,
                                  ALU.mult).then_inc(s["gates"], 1)
                dve.wait_ge(s["rank_ps"], t + 1)
                dve.wait_ge(s["count_ps"], t + 1)
                dve.tensor_tensor(rank[:, :], ps[7][:, NE:2 * NE], carry[:, :], ALU.add).then_inc(s["rank"], 1)
                dve.wait_ge(s["rank"], t + 1)
                dve.tensor_tensor(carry[:, :], ps[7][:, 2 * NE:3 * NE], carry[:, :], ALU.add).then_inc(s["carry"], 1)
                dve.tensor_tensor(picked[:, :, :], hot[:, :, :], repeated(rank[:, :], TOPK, NE), ALU.mult).then_inc(s["picked"], 1)
                dve.wait_ge(s["picked"], t + 1)
                dve.tensor_reduce(rank4[:, :], picked[:, :, :], AX_X, ALU.add).then_inc(s["rank4"], 1)
                dve.wait_ge(s["rank4"], t + 1)
                dve.scalar_tensor_tensor(slot_f[:, :], ixf[:, :], float(REGION), rank4[:, :], ALU.mult, ALU.add).then_inc(s["slot_f"], 1)
                dve.wait_ge(s["slot_f"], t + 1)
                dve.tensor_copy(slots[:, bass.ds(t, 1), :].rearrange("p a j -> p (a j)"), slot_f[:, :]).then_inc(s["slots"], 1)
                if norm_in:
                    rows_in(t + 2)
                if next_in:
                    residual(t + 1)

            rows_in(0)
            maxima(0)
            normalised(0)
            probs_out(0)
            rows_in(1)
            residual(0)
            tiles_ahead(dve, body)
            step = [0]

            def then(ins):
                step[0] += 1
                ins.then_inc(s["plan_step"], 1)
                dve.wait_ge(s["plan_step"], step[0])

            col = lambda i: pv[:, i:i + 1]
            total, expert, first, count, nth, rem, base = (col(i) for i in range(7))
            dve.wait_ge(s["carry"], NT)
            then(dve.tensor_scalar(c_up, carry[:, :], float(PASS - 1), None, ALU.add))
            then(dve.tensor_copy(pi[:, :], c_up))
            then(dve.tensor_scalar(pi[:, :], pi[:, :], int(math.log2(PASS)), None, ALU.logical_shift_right))
            then(dve.tensor_copy(n_pass, pi[:, :]))
            then(dve.tensor_tensor_scan(n_cum, ones_e[:, :], n_pass, 0.0, ALU.mult, ALU.add))
            then(dve.tensor_scalar(before, n_cum, iota_i[:, 0:1], None, ALU.is_le))
            then(dve.tensor_reduce(expert, before, AX_X, ALU.add))
            then(dve.tensor_tensor(tmp, before, n_pass, ALU.mult))
            then(dve.tensor_reduce(first, tmp, AX_X, ALU.add))
            then(dve.tensor_scalar(expert, expert, float(NE - 1), None, ALU.min))
            then(dve.tensor_scalar(e_hot, iota_e[:, :], expert, None, ALU.is_equal))
            then(dve.tensor_tensor(tmp, e_hot, carry[:, :], ALU.mult))
            then(dve.tensor_reduce(count, tmp, AX_X, ALU.add))
            then(dve.tensor_tensor(nth, iota_i[:, :], first, ALU.subtract))
            then(dve.tensor_scalar(nth, nth, float(REGION // PASS - 1), 0.0, ALU.min, ALU.max))
            then(dve.scalar_tensor_tensor(rem, nth, -float(PASS), count, ALU.mult, ALU.add))
            then(dve.tensor_scalar(base, expert, float(REGION), None, ALU.mult))
            then(dve.scalar_tensor_tensor(base, nth, float(PASS), base, ALU.mult, ALU.add))
            dve.tensor_copy(plan[:, 0:1], expert).then_inc(s["plan"], 1)
            dve.tensor_copy(plan[:, 1:2], base).then_inc(s["plan"], 1)
            dve.tensor_scalar(plan[:, 2:3], rem, float(P), None, ALU.is_gt).then_inc(s["plan"], 1)
            dve.tensor_copy(plan[:, 3:4], n_cum[:, NE - 1:NE]).then_inc(s["plan"], 1)


def expert_stage(nc, a, plan_row, scratch):
    with ExitStack() as ctx:
        sb = lambda n, s, d=F32: ctx.enter_context(nc.sbuf_tensor(n, s, d))
        s = Signals(nc, ctx, "ex")
        raw = sb("raw_pieces", [P, RING, KD // 2 * FW])
        w1 = sb("w1_parts", [P, 2, 2, KD, FW], F32R)
        w2 = sb("w2_parts", [P, 2, 2, GK, D], F32R)
        ident = sb("ident3", [P, P])
        bias3 = sb("bias3", [B2_AT + 3, FF2], BF16)
        ones3 = sb("ones3", [B2_AT + 3, P], BF16)
        idx = sb("row_index", [P, 2, 2], I32)
        out_idx = sb("out_index", [P, 2, 2], I32)
        spare = sb("spare3", [P, 2])
        got = sb("gathered", [P, 2, D])
        uT = sb("uT3", [P, 2, 2, KD, P], F32R)
        glu = sb("glu", [P, 2, FW // 2])
        sig = sb("sig", [P, 2, FW // 2])
        lin = sb("lin", [P, 2, 2, FW // 2])
        actT = sb("actT", [P, 2, 2, GK, P], F32R)
        y = sb("y_rows", [P, 2, D])

        ps_h = [ctx.enter_context(nc.psum_tensor(f"ex_h{b}", [P, FW], F32)) for b in range(2)]
        ps_g = ctx.enter_context(nc.psum_tensor("ex_g", [P, 2, GK, P], F32))
        ps_u = ctx.enter_context(nc.psum_tensor("ex_u", [P, 4, P], F32))
        ps_y = [[ctx.enter_context(nc.psum_tensor(f"ex_y{b}{n}", [P, 512], F32)) for n in range(2)] for b in range(2)]
        block = ctx.enter_context(nc.Block())

        w1_v = a["w1"][0].rearrange("e (k p) f -> e p k f", p=P)
        w2_v = a["w2"][0].rearrange("e (c k p) d -> e p c k d", k=GK, p=P)

        first_pieces = [("w1", c, half) for c in range(2) for half in range(2)]
        pieces = []
        for c in range(FCH - 2):
            pieces += [("w1", c + 2, 0), ("w1", c + 2, 1), ("w2", c, 0)]
        pieces += [("w2", c, 0) for c in (FCH - 2, FCH - 1)]
        pieces += [("w1", c + FCH, half) for c in range(2) for half in range(2)]
        N0, NQ = len(first_pieces), len(pieces)

        def splitter(piece):
            return "pool" if piece[0] == "w2" and piece[1] < FCH - 1 else "dve"

        def count(i, piece, of=lambda piece: True, passes_ago=0):
            per_pass, before = sum(map(of, pieces)), sum(map(of, first_pieces))
            if piece in first_pieces:
                if is_first(i):
                    return sum(map(of, first_pieces[:first_pieces.index(piece) + 1]))
                piece, before = (piece[0], piece[1] + FCH, piece[2]), before - per_pass
            before -= passes_ago * per_pass
            return i * per_pass + (before + sum(map(of, pieces[:pieces.index(piece) + 1])))

        def split(i, piece, passes_ago=0):
            by = splitter(piece)
            return s[f"split_{by}"], count(i, piece, lambda p: splitter(p) == by, passes_ago)

        def ring_place(piece):
            return first_pieces.index(piece) if piece in first_pieces else N0 + pieces.index(piece)

        def parts_of(piece):
            kind, c, half = piece
            if kind == "w1":
                return [w1[:, c % 2, j, 4 * half:4 * half + 4, :].rearrange("p k f -> p (k f)") for j in range(2)]
            return [w2[:, c % 2, j, :, :].rearrange("p k f -> p (k f)") for j in range(2)]

        def raw_of(piece):
            return raw[:, ring_place(piece) % RING, :]

        def rest_of(eng, i, *piece):
            eng.wait_ge(s["rounded"], count(i, piece))
            part = parts_of(piece)
            eng.tensor_tensor(part[1], raw_of(piece), part[0].bitcast(F32), ALU.subtract).then_inc(s[f"split_{splitter(piece)}"], 1)

        def slots_at(first_slot):
            return scratch["slot_table"][bass.ds(first_slot, PASS), :].rearrange("(b p) a -> p b a", p=P)

        def passes(eng):
            return eng.value_load(plan_row[0:1, 3:4], min_val=1, max_val=MAX_PASSES)

        def plan_of(eng, i, what, most):
            return eng.value_load(plan_row[0:1, bass.ds(i * 4 + what, 1)], min_val=0, max_val=most)

        def bank_of(c, b, nb):
            return b if nb == 2 else c % 2

        def each_pass(eng, n, body):
            body(0)
            with eng.Fori(1, n) as i:
                body(i)

        def by_blocks(eng, body):
            def choose(i):
                two = plan_of(eng, i, 2, 1)
                with eng.If(two > 0):
                    body(i, 2)
                with eng.Else():
                    body(i, 1)
            return choose

        @block.sync
        def _(sp):
            def load(e, piece):
                kind, c, half = piece
                if kind == "w1":
                    cols = slice(FW * (c % FCH), FW * (c % FCH) + FW)
                    src = w1_v[bass.ds(e, 1), :, 4 * half:4 * half + 4, cols].rearrange("a p k f -> (a p) k f")
                else:
                    src = w2_v[bass.ds(e, 1), :, c, :, :].rearrange("a p k d -> (a p) k d")
                sp.dma_start(raw_of(piece).rearrange("p (k f) -> p k f", f=src.shape[-1]), src).then_inc(s[f"raw_{ring_place(piece) % RING}"], 16)

            def body(i):
                e = plan_of(sp, i, 0, NE - 1)
                e_next = plan_of(sp, i + 1, 0, NE - 1)
                for q, piece in enumerate(pieces):
                    if q >= RING:
                        sp.wait_ge(*split(i, pieces[q - RING]))
                    elif not is_first(i):
                        sp.wait_ge(*split(i, pieces[q - RING + NQ], passes_ago=1))
                    elif N0 + q >= RING:
                        sp.wait_ge(*split(i, first_pieces[N0 + q - RING]))
                    load(e if piece[1] < FCH else e_next, piece)

            sp.dma_start(ident[:, :], a["c_ident"]).then_inc(s["consts"], 16)
            n = passes(sp)
            e = plan_of(sp, 0, 0, NE - 1)
            for g, piece in enumerate(first_pieces):
                if g == 2:
                    sp.wait_ge(s["got"], 32)
                load(e, piece)
            each_pass(sp, n, body)

        @block.gpsimd
        def _(pool):
            pool.memset(ones3[:, :], 1.0).then_inc(s["cleared"], 1)
            pool.memset(spare[:, :], 0.0).then_inc(s["cleared"], 1)
            pool.memset(got[:, :, :], 0.0).then_inc(s["cleared"], 1)
            pool.wait_ge(s["cleared"], 3)

            def met():
                pool.tensor_tensor(spare[:, 0:1], spare[:, 1:2], spare[:, 1:2], ALU.add).then_inc(s["met"], 1)

            def gather(i, mets):
                first_slot = plan_of(pool, i, 1, NE * REGION - PASS)
                if not is_first(i):
                    pool.wait_ge(s["uT_ps"], 4 * i)
                with nc.allow_non_contiguous_dma("256 row numbers"):
                    pool.dma_start(idx[:, :, :], slots_at(first_slot)).then_inc(s["idx"], 16)
                if not is_first(i):
                    pool.wait_ge(s["met"], mets)
                pool.wait_ge(s["idx"], 16 * i + 16)
                met()
                for b in range(2):
                    pool.indirect_dma_start(got[:, b, :], None, scratch["rows"],
                                            bass.IndirectOffsetOnAxis(ap=idx[:, b, 0:1], axis=0),
                                            bounds_check=SEQ - 1, oob_is_err=False).then_inc(s["got"], 16)

            def body(i):
                gather(i + 1, 2 * i + 1)
                for c in range(FCH - 1):
                    rest_of(pool, i, "w2", c, 0)
                first_slot = plan_of(pool, i, 1, NE * REGION - PASS)
                if not is_first(i):
                    pool.wait_ge(s["stored"], 32 * i)
                with nc.allow_non_contiguous_dma("256 row numbers"):
                    pool.dma_start(out_idx[:, :, :], slots_at(first_slot)).then_inc(s["out_idx"], 16)
                pool.wait_ge(s["met"], 2 * i + 2)
                pool.wait_ge(s["out_idx"], 16 * i + 16)
                pool.wait_ge(s["y_left"], 2 * i + 2)
                met()
                for b in range(2):
                    pool.indirect_dma_start(scratch["y"], bass.IndirectOffsetOnAxis(ap=out_idx[:, b, 1:2], axis=0), y[:, b, :], None,
                                            bounds_check=SEQ * TOPK - 1, oob_is_err=False).then_inc(s["stored"], 16)

            gather(0, None)
            pool.memset(y[:, :, :], 0.0).then_inc(s["cleared"], 1)
            n = passes(pool)
            each_pass(pool, n, body)
            pool.wait_ge(s["stored"], 32 * n)

        @block.tensor
        def _(pe):
            def product(ps, lhsT, rhs, start):
                pe.matmul(ps, lhsT[0], rhs[0], start=start, stop=False)
                pe.matmul(ps, lhsT[0], rhs[1], start=False, stop=False)
                pe.matmul(ps, lhsT[1], rhs[0], start=False, stop=False)

            def row_transposes(i, r):
                if r == 0:
                    pe.wait_ge(s["got"], 32 * i + 32)
                if r or not is_first(i):
                    pe.wait_ge(s["uT"], 4 * i + r)
                for k in range(4):
                    m = pe.transpose(ps_u[:, k, :], got[:, r // 2, P * (4 * (r % 2) + k):P * (4 * (r % 2) + k) + P], ident[:, :])
                m.then_inc(s["uT_ps"], 1)

            def hidden(i, c, nb):
                for b in range(nb):
                    if c == 0:
                        pe.wait_ge(s["uT"], 4 * i + 2 * b + 2)
                    elif nb == 2:
                        pe.wait_ge(s["act"], 8 * i + (2 * c + b - 1))
                    bank = ps_h[bank_of(c, b, nb)]
                    for k in range(KD):
                        if b == 0 and k % 4 == 0:
                            pe.wait_ge(*split(i, ("w1", c, k // 4)))
                        product(bank[:, :], [uT[:, j, b, k, :] for j in range(2)], [w1[:, c % 2, j, k, :] for j in range(2)], k == 0)
                    if b == 0 and c == 0:
                        pe.wait_ge(s["bias3"], 32 * i + 32)
                    m = pe.matmul(bank[:, :], ones3[0:3, :], bias3[0:3, FW * c:FW * c + FW], start=False, stop=True)
                    m.then_inc(s["h"], 1 if nb == 2 else 2)

            def gated_transposes(i, c, nb):
                pe.wait_ge(s["act"], 8 * i + (2 * c + 2))
                if c:
                    pe.wait_ge(s["actT"], 4 * i + c)
                for b in range(nb):
                    for k in range(GK):
                        m = pe.transpose(ps_g[:, b, k, :], lin[:, c % 2, b, P * k:P * k + P], ident[:, :])
                m.then_inc(s["gT"], 1)

            def out(i, c, nb):
                pe.wait_ge(s["actT"], 4 * i + (c + 1))
                pe.wait_ge(*split(i, ("w2", c, 0)))
                if c == 0 and not is_first(i):
                    pe.wait_ge(s["y_left"], 2 * i)
                for n in range(2):
                    for b in range(nb):
                        for k in range(GK):
                            cols = slice(512 * n, 512 * n + 512)
                            product(ps_y[b][n][:, :], [actT[:, j, b, k, :] for j in range(2)], [w2[:, c % 2, j, k, cols] for j in range(2)],
                                    c == 0 and k == 0)
                        if c == FCH - 1:
                            m = pe.matmul(ps_y[b][n][:, :], ones3[B2_AT:, :], bias3[B2_AT:, 512 * n:512 * n + 512], start=False, stop=True)
                            if (n, b) == (1, nb - 1):
                                m.then_inc(s["out"], 1)

            def body(i, nb):
                hidden(i, 0, nb)
                for c in range(FCH - 1):
                    hidden(i, c + 1, nb)
                    if c:
                        out(i, c - 1, nb)
                    gated_transposes(i, c, nb)
                row_transposes(i + 1, 0)
                out(i, FCH - 2, nb)
                row_transposes(i + 1, 1)
                gated_transposes(i, FCH - 1, nb)
                row_transposes(i + 1, 2)
                out(i, FCH - 1, nb)
                row_transposes(i + 1, 3)

            pe.wait_ge(s["consts"], 16)
            pe.wait_ge(s["cleared"], 4)
            for r in range(4):
                row_transposes(0, r)
            n = passes(pe)
            each_pass(pe, n, by_blocks(pe, body))
            pe.wait_ge(s["bias3"], 32 * n + 32)

        @block.scalar
        def _(act):
            def bias_in(i):
                parts = scratch["bias_parts"][bass.ds(plan_of(act, i, 0, NE - 1), 1), :, :].rearrange("a j n -> (a j) n")
                act.dma_start(bias3[0:3, :], parts[:, 0:FF2]).then_inc(s["bias3"], 16)
                act.dma_start(bias3[B2_AT:, 0:D], parts[:, FF2:]).then_inc(s["bias3"], 16)

            def rounded(i, *piece):
                kind, c, half = piece
                g = ring_place(piece)
                act.wait_ge(s[f"raw_{g % RING}"], 16 * (NQ // RING) * i + 16 * (g // RING + 1))
                if kind == "w1" and c >= 2:
                    act.wait_ge(s["h"], 8 * i + (2 * c - 2))
                elif kind == "w2" and (c >= 2 or not is_first(i)):
                    act.wait_ge(s["gT"], 4 * i + c)
                act.activation(parts_of(piece)[0], raw_of(piece), ACT.Copy).then_inc(s["rounded"], 1)

            def rows_rounded(i, r):
                act.wait_ge(s["uT_ps"], 4 * i + (r + 1))
                k = 4 * (r % 2)
                act.activation(uT[:, 0, r // 2, k:k + 4, :].rearrange("p k n -> p (k n)"), ps_u[:, :, :].rearrange("p k n -> p (k n)"),
                               ACT.Copy).then_inc(s["uT_rounded"], 1)

            def sigmoids(i, c, nb):
                for b in range(nb):
                    act.wait_ge(s["glu"], 8 * i + (2 * c + (b + 1 if nb == 2 else 2)))
                    act.activation(sig[:, b, :], glu[:, b, :], ACT.Sigmoid, scale=ALPHA).then_inc(s["sig"], 1 if nb == 2 else 2)

            def body(i, nb):
                sigmoids(i, 0, nb)
                for c in range(FCH):
                    if c + 2 < FCH:
                        rounded(i, "w1", c + 2, 0)
                        rounded(i, "w1", c + 2, 1)
                    if c + 1 < FCH:
                        rounded(i, "w2", c, 0)
                        sigmoids(i, c + 1, nb)
                    else:
                        rows_rounded(i + 1, 0)
                        rounded(i, "w2", c, 0)
                        rounded(i, "w1", FCH, 0)
                        rows_rounded(i + 1, 1)
                    act.wait_ge(s["gT"], 4 * i + (c + 1))
                    act.activation(actT[:, 0, 0:nb, :, :].rearrange("p b k n -> p (b k n)"),
                                   ps_g[:, 0:nb, :, :].rearrange("p b k n -> p (b k n)"), ACT.Copy).then_inc(s["actT_rounded"], 1)
                rounded(i, "w1", FCH, 1)
                rows_rounded(i + 1, 2)
                rounded(i, "w1", FCH + 1, 0)
                rows_rounded(i + 1, 3)
                act.wait_ge(s["out"], i + 1)
                if not is_first(i):
                    act.wait_ge(s["stored"], 32 * i)
                for b in range(nb):
                    m = act.activation(y[:, b, 0:512], ps_y[b][0][:, :], ACT.Copy)
                m.then_inc(s["y_left"], 1)
                bias_in(i + 1)
                rounded(i, "w1", FCH + 1, 1)

            act.wait_ge(s["cleared"], 4)
            bias_in(0)
            for g, piece in enumerate(first_pieces):
                if g == 2:
                    for r in range(4):
                        rows_rounded(0, r)
                rounded(0, *piece)
            n = passes(act)
            each_pass(act, n, by_blocks(act, body))

        @block.vector
        def _(dve):
            def rows_rest(i, r):
                dve.wait_ge(s["uT_rounded"], 4 * i + (r + 1))
                k = 4 * (r % 2)
                dve.tensor_tensor(uT[:, 1, r // 2, k:k + 4, :], ps_u[:, :, :], uT[:, 0, r // 2, k:k + 4, :].bitcast(F32),
                                  ALU.subtract).then_inc(s["uT"], 1)

            def gated(i, c, b, nb):
                inc = 1 if nb == 2 else 2
                at = 8 * i + (2 * c + (b + 1 if nb == 2 else 2))
                dve.wait_ge(s["h"], at)
                bank, ln = ps_h[bank_of(c, b, nb)], lin[:, c % 2, b, :]
                dve.tensor_scalar(glu[:, b, :], bank[:, 0::2], LIMIT, None, ALU.min).then_inc(s["glu"], inc)
                dve.tensor_scalar(ln, bank[:, 1::2], LIMIT, -LIMIT, ALU.min, ALU.max).then_inc(s["lin"], inc)
                dve.wait_ge(s["lin"], at)
                dve.scalar_tensor_tensor(ln, ln, 1.0, glu[:, b, :], ALU.add, ALU.mult).then_inc(s["lin_glu"], inc)
                dve.wait_ge(s["lin_glu"], at)
                dve.wait_ge(s["sig"], at)
                dve.tensor_tensor(ln, ln, sig[:, b, :], ALU.mult).then_inc(s["act"], inc)

            def body(i, nb):
                for b in range(nb):
                    gated(i, 0, b, nb)
                for c in range(FCH):
                    if c + 2 < FCH:
                        rest_of(dve, i, "w1", c + 2, 0)
                        rest_of(dve, i, "w1", c + 2, 1)
                    if c + 1 < FCH:
                        for b in range(nb):
                            gated(i, c + 1, b, nb)
                    else:
                        rows_rest(i + 1, 0)
                        rest_of(dve, i, "w2", c, 0)
                        rows_rest(i + 1, 1)
                    dve.wait_ge(s["actT_rounded"], 4 * i + (c + 1))
                    dve.tensor_tensor(actT[:, 1, 0:nb, :, :].rearrange("p b k n -> p (b k n)"), ps_g[:, 0:nb, :, :].rearrange("p b k n -> p (b k n)"),
                                      actT[:, 0, 0:nb, :, :].rearrange("p b k n -> p (b k n)").bitcast(F32), ALU.subtract).then_inc(s["actT"], 1)
                rest_of(dve, i, "w1", FCH, 0)
                rest_of(dve, i, "w1", FCH, 1)
                rows_rest(i + 1, 2)
                rest_of(dve, i, "w1", FCH + 1, 0)
                rows_rest(i + 1, 3)
                dve.wait_ge(s["out"], i + 1)
                if not is_first(i):
                    dve.wait_ge(s["stored"], 32 * i)
                for b in range(nb):
                    m = dve.tensor_copy(y[:, b, 512:D], ps_y[b][1][:, :])
                m.then_inc(s["y_left"], 1)
                rest_of(dve, i, "w1", FCH + 1, 1)

            dve.wait_ge(s["cleared"], 4)
            for g, piece in enumerate(first_pieces):
                if g == 2:
                    for r in range(4):
                        rows_rest(0, r)
                rest_of(dve, 0, *piece)
            n = passes(dve)
            each_pass(dve, n, by_blocks(dve, body))


def combine_stage(nc, a, gates, scratch, out):
    with ExitStack() as ctx:
        sb = lambda n, s, d=F32: ctx.enter_context(nc.sbuf_tensor(n, s, d))
        s = Signals(nc, ctx, "cb")
        AHEAD = 4
        got = [sb(f"expert_rows{i}", [P, TOPK, D]) for i in range(AHEAD)]
        hb = [sb(f"h_tile{i}", [P, D]) for i in range(AHEAD)]
        junk = sb("junk", [P, D])
        res = [sb(f"result{i}", [P, D]) for i in range(2)]
        g_fin = sb("g_final_sb", [P, D])
        stat = sb("stat4", [P, 2 * NT])
        norm_c = sb("norm_c4", [P, 2, 2])
        block = ctx.enter_context(nc.Block())

        @block.gpsimd
        def _(pool):
            pool.memset(norm_c[:, 0, :], EPS).then_inc(s["norm_c"], 1)
            pool.memset(norm_c[:, 1, :], -0.5).then_inc(s["norm_c"], 1)
            pool.wait_ge(s["norm_c"], 2)

            def pair(t):
                rows = got[t % AHEAD]
                pool.wait_ge(s["weighed"], 2 * t + 2)
                pool.tensor_tensor(rows[:, 2, :], rows[:, 2, :], rows[:, 3, :], ALU.add).then_inc(s["paired"], 1)

            pair(0)
            for t in range(NT):
                if t + 1 < NT:
                    pair(t + 1)
                pool.wait_ge(s["ss"], t + 1)
                rstd_of(pool, norm_c, stat[:, 2 * t + 1:2 * t + 2], stat[:, 2 * t:2 * t + 1], 1, s["rstd_ms"], s["rstd"], t + 1)

        @block.vector
        def _(dve):
            def finish(t):
                dve.wait_ge(s["rstd"], t + 1)
                if t == 0:
                    dve.wait_ge(s["g_fin"], 16)
                if t >= 2:
                    dve.wait_ge(s[f"stored{t % 2}"], 16 * (t // 2))
                dve.scalar_tensor_tensor(res[t % 2][:, :], hb[t % AHEAD][:, :], stat[:, 2 * t + 1:2 * t + 2], g_fin[:, :],
                                         ALU.mult, ALU.mult).then_inc(s["result"], 1)

            for t in range(NT):
                rows, ht = got[t % AHEAD], hb[t % AHEAD]
                dve.wait_ge(s[f"h{t % AHEAD}"], 16 * (t // AHEAD + 1))
                dve.wait_ge(s[f"got{t % AHEAD}"], 16 * (t // AHEAD + 1))
                for j in range(2):
                    if j:
                        dve.wait_ge(s["summed"], 3 * t + j)
                    dve.scalar_tensor_tensor(ht[:, :], rows[:, j, :], gates[:, t, j:j + 1], ht[:, :],
                                             ALU.mult, ALU.add).then_inc(s["summed"], 1)
                dve.wait_ge(s["summed"], 3 * t + 2)
                dve.wait_ge(s["paired"], t + 1)
                dve.tensor_tensor(ht[:, :], rows[:, 2, :], ht[:, :], ALU.add).then_inc(s["summed"], 1)
                if t:
                    finish(t - 1)
            finish(NT - 1)

        @block.scalar
        def _(act):
            def weigh(t):
                act.wait_ge(s[f"got{t % AHEAD}"], 16 * (t // AHEAD + 1))
                for j in range(2, 4):
                    rows = got[t % AHEAD][:, j, :]
                    act.activation(rows, rows, ACT.Copy, scale=gates[:, t, j:j + 1]).then_inc(s["weighed"], 1)

            weigh(0)
            for t in range(NT):
                if t + 1 < NT:
                    weigh(t + 1)
                act.wait_ge(s["summed"], 3 * t + 3)
                if t:
                    act.wait_ge(s["ss"], t)
                act.activation(junk[:, :], hb[t % AHEAD][:, :], ACT.Square, scale=1 / 32, accum_out=stat[:, 2 * t:2 * t + 1]).then_inc(s["ss"], 1)

        @block.sync
        def _(sp):
            def load(t):
                sp.dma_start(got[t % AHEAD][:, :, :], scratch["y"][TOPK * P * t:TOPK * P * (t + 1), :].rearrange(
                    "(p j) d -> p j d", j=TOPK)).then_inc(s[f"got{t % AHEAD}"], 16)
                sp.dma_start(hb[t % AHEAD][:, :], scratch["h"][P * t:P * t + P, :]).then_inc(s[f"h{t % AHEAD}"], 16)

            load(0)
            sp.dma_start(g_fin[:, :], a["g_final"].partition_broadcast(P)).then_inc(s["g_fin"], 16)
            for t in range(1, AHEAD):
                load(t)
            for t in range(NT):
                sp.wait_ge(s["result"], t + 1)
                if t + AHEAD < NT:
                    load(t + AHEAD)
                sp.dma_start(out[0, P * t:P * t + P, :], res[t % 2][:, :]).then_inc(s[f"stored{t % 2}"], 16)
            for i in range(2):
                sp.wait_ge(s[f"stored{i}"], 16 * NT // 2)


def build_program(nc, a, out):
    with ExitStack() as ctx:
        sb = lambda n, s, d=F32: ctx.enter_context(nc.sbuf_tensor(n, s, d))
        gates = sb("gates", [P, NT, TOPK])
        plan_row = sb("plan_row", [1, 4 * (MAX_PASSES + 1)], I32)
        dram = lambda n, s, d=F32: nc.dram_tensor(n, s, d).ap()
        scratch = {
            "bias_rows": dram("bias_rows_dram", [8, P, 3 * P]),
            "h": dram("h_dram", [SEQ, D]),
            "rows": dram("moe_rows_dram", [SEQ, D]),
            "slot_table": dram("slot_table_dram", [NE * REGION, 2], I32),
            "plan": dram("plan_dram", [MAX_PASSES + 1, 4], I32),
            "bias_parts": dram("bias_parts_dram", [NE, 3, FF2 + D], BF16),
            "y": dram("expert_y_dram", [SEQ * TOPK, D]),
        }
        with nc.sbuf_tensor("h_rows", [P, NT, D], F32) as h:
            mixer_stage(nc, a, h, scratch)
            cross_stage(nc, a, h, gates, plan_row, scratch)
        expert_stage(nc, a, plan_row, scratch)
        combine_stage(nc, a, gates, scratch, out)


def shape_constants():
    dist = np.arange(P - 1, -1, -1)
    exact = BUCKETS // 2
    ratio = np.maximum(dist, exact).astype(np.float32) / exact
    large = exact + (np.log(ratio) / math.log(MAX_DIST / exact) * (BUCKETS - exact)).astype(np.int32)
    bucket = np.where(dist < exact, dist, np.minimum(large, BUCKETS - 1))
    return {
        "c_ident": np.eye(P, dtype=np.float32),
        "c_upper": np.triu(np.ones((P, P), np.float32)),
        "c_bucket": (np.arange(BUCKETS)[:, None] == bucket[None, :]).astype(np.float32),
    }


_INS = ["x", "mem", "g_mix", "w_in", "b_qkv", "conv_w", "conv_b", "dt_bias", "a_log", "d_skip", "g_ssm_out",
        "attn_sinks", "rel_bias", "w_out", "b_out", "g_cross", "g_mem", "w_q_cross", "w_kv_cross", "w_o_cross",
        "g_ffn", "w_router", "b_router", "w1", "b1", "w2", "b2", "g_final"]


def kernel(**inputs):
    import concourse.bacc as bacc
    from concourse.bass_utils import run_bass_kernel_spmd

    nc = bacc.Bacc("TRN2", target_bir_lowering=False, num_devices=1)
    arrays, aps = {}, {}
    given = {n: np.ascontiguousarray(inputs[n]) for n in _INS} | shape_constants()
    for name, v in given.items():
        arrays[f"in_{name}"] = v
        aps[name] = nc.dram_tensor(f"in_{name}", v.shape, mybir.dt.from_np(v.dtype), kind="ExternalInput").ap()
    out = nc.dram_tensor("out_rows", (1, SEQ, D), F32, kind="ExternalOutput").ap()
    build_program(nc, aps, out)
    r = run_bass_kernel_spmd(nc, [arrays], core_ids=[0])
    return r.results[0]["out_rows"]
```
